# Optimizing a Trainium2 kernel written in Bass

```python
import jax
import jax.numpy as jnp
from jax import lax
import numpy as np

D_MODEL = 1024
BATCH = 1
SEQ = 512
DEPTH = 1

CTX_LEN = 256
GRID_W = 64
EPS = 1e-6

HG_HEADS = 4
HG_DK = 128
HG_DV = 128
HG_KEY_WIDTH = HG_HEADS * HG_DK
HG_WIDTH = HG_HEADS * HG_DV
HG_CHUNK = 16

CM_CHUNK = 128
CM_GROUPS = 4
CM_WIDTH = 512
CM_GROUP_DIM = CM_WIDTH // CM_GROUPS
ROWS_PER_CHUNK = CM_CHUNK // GRID_W

SPLIT_IDX = (HG_KEY_WIDTH, 2 * HG_KEY_WIDTH, 3 * HG_KEY_WIDTH, 3 * HG_KEY_WIDTH + HG_WIDTH,
             3 * HG_KEY_WIDTH + 2 * HG_WIDTH, 3 * HG_KEY_WIDTH + 2 * HG_WIDTH + 2 * CM_WIDTH)
D_IN = 3 * HG_KEY_WIDTH + 2 * HG_WIDTH + 2 * CM_WIDTH + 2 * D_MODEL

N_EXPERTS = 64
TOP_K = 8
N_EXPERT_GROUPS = 8
TOPK_GROUPS = 4
D_EXPERT = 256
D_SHARED = 256
ROUTED_SCALE = 2.5
MOE_BLOCK = 256


def rms_norm(x, g):
    x32 = x.astype(jnp.float32)
    y = x32 * lax.rsqrt(jnp.mean(x32 * x32, axis=-1, keepdims=True) + EPS)
    return (y * g.astype(jnp.float32)).astype(x.dtype)

def layer_norm(x, g, b):
    x32 = x.astype(jnp.float32)
    xc = x32 - jnp.mean(x32, axis=-1, keepdims=True)
    y = xc * lax.rsqrt(jnp.mean(xc * xc, axis=-1, keepdims=True) + EPS)
    return (y * g.astype(jnp.float32) + b.astype(jnp.float32)).astype(x.dtype)

def hgrn2_gates(z, lb):
    B, T, _ = z.shape
    z = z.astype(jnp.float32).reshape(B, T, HG_HEADS, HG_DK)
    lb = lb.reshape(HG_HEADS, HG_DK)
    log_f = jnp.log(lb + (1.0 - lb) * jax.nn.sigmoid(z))
    k = (1.0 - lb) * jax.nn.sigmoid(-z)
    return k, log_f

def gla_chunk_scan(q, k, v, log_f, s0, readout):
    B, T, H, DK = k.shape
    DV = v.shape[-1]
    n = T // HG_CHUNK

    def to_chunks(a):
        return a.astype(jnp.float32).reshape(B, n, HG_CHUNK, H, a.shape[-1]).transpose(1, 0, 3, 2, 4)

    kc, vc = to_chunks(k), to_chunks(v)
    bc = jnp.cumsum(to_chunks(log_f), axis=3)
    tri = jnp.tril(jnp.ones((HG_CHUNK, HG_CHUNK), dtype=bool))
    mid = HG_CHUNK // 2 - 1

    def step(S, xs):
        k_, v_, b_ = xs[0], xs[1], xs[2]
        b_last = b_[:, :, -1:, :]
        S_new = jnp.exp(b_last[:, :, 0, :, None]) * S + jnp.einsum('bhsd,bhsv->bhdv', k_ * jnp.exp(b_last - b_), v_)
        if not readout:
            return S_new, None
        q_ = xs[3]
        b_mid = b_[:, :, mid:mid + 1, :]
        A = jnp.einsum('bhtd,bhsd->bhts', q_ * jnp.exp(b_ - b_mid), k_ * jnp.exp(b_mid - b_))
        A = jnp.where(tri, A, 0.0)
        o = jnp.einsum('bhts,bhsv->bhtv', A, v_) + jnp.einsum('bhtd,bhdv->bhtv', q_ * jnp.exp(b_), S)
        return S_new, o

    xs = (kc, vc, bc, to_chunks(q)) if readout else (kc, vc, bc)
    S_fin, o = lax.scan(step, s0, xs)
    if readout:
        o = o.transpose(1, 0, 3, 2, 4).reshape(B, T, H, DV)
    return o, S_fin

def chunk_spatial_gating(p, n_chunks, ln_g, ln_b, w_s, b_s):
    a = jax.nn.gelu(p)
    u, v = jnp.split(a, 2, axis=-1)
    v = layer_norm(v, ln_g, ln_b)
    B, T, _ = v.shape
    v = v.reshape(B, n_chunks, CM_CHUNK, CM_GROUPS, CM_GROUP_DIM)
    z = jnp.einsum('gpq,bnqgc->bnpgc', w_s, v) + b_s[None, None, :, :, None]
    return u * z.reshape(B, T, CM_WIDTH)

def token_mixer(h_lat, h_ctx, w_in, lb, g_out, ln_g, ln_b, w_s, b_s, w_a, w_b, w_o,
                n_lat_chunks, n_ctx_chunks, need_ctx):
    B, T, _ = h_lat.shape
    L = h_ctx.shape[1]
    p_lat = h_lat @ w_in
    p_ctx = h_ctx @ w_in
    ql, fl_fwd, fl_bwd, il, gl, cml, gtl = jnp.split(p_lat, SPLIT_IDX, axis=-1)
    qc, fc_fwd, fc_bwd, ic, gc, cmc, gtc = jnp.split(p_ctx, SPLIT_IDX, axis=-1)

    q_lat = jax.nn.silu(ql).reshape(B, T, HG_HEADS, HG_DK)
    v_lat = il.reshape(B, T, HG_HEADS, HG_DV)
    q_ctx = jax.nn.silu(qc).reshape(B, L, HG_HEADS, HG_DK) if need_ctx else None
    v_ctx = ic.reshape(B, L, HG_HEADS, HG_DV)
    s0 = jnp.zeros((B, HG_HEADS, HG_DK, HG_DV), jnp.float32)

    lat_outs, ctx_outs = [], []
    for d, (f_lat, f_ctx) in enumerate(((fl_fwd, fc_fwd), (fl_bwd, fc_bwd))):
        rev = (lambda a: a[:, ::-1]) if d == 1 else (lambda a: a)
        k_l, lf_l = hgrn2_gates(f_lat, lb[d])
        k_c, lf_c = hgrn2_gates(f_ctx, lb[d])
        q_c = rev(q_ctx) if need_ctx else None
        oc, s_ctx = gla_chunk_scan(q_c, rev(k_c), rev(v_ctx), rev(lf_c), s0, need_ctx)
        ol, _ = gla_chunk_scan(rev(q_lat), rev(k_l), rev(v_lat), rev(lf_l), s_ctx, True)
        lat_outs.append(rev(ol))
        if need_ctx:
            ctx_outs.append(rev(oc))

    def merge(o, g, cm, gt, n_chunks, dtype):
        n_tok = o.shape[1]
        g = g.reshape(B, n_tok, HG_HEADS, HG_DV).astype(jnp.float32)
        a = (rms_norm(o, g_out) * jax.nn.silu(g)).reshape(B, n_tok, HG_WIDTH).astype(dtype)
        bm = chunk_spatial_gating(cm, n_chunks, ln_g, ln_b, w_s, b_s)
        ga, gb = jnp.split(gt, 2, axis=-1)
        y = jax.nn.sigmoid(ga) * (a @ w_a) + jax.nn.sigmoid(gb) * (bm @ w_b)
        return y @ w_o

    y_lat = merge(lat_outs[0] + lat_outs[1], gl, cml, gtl, n_lat_chunks, h_lat.dtype)
    y_ctx = merge(ctx_outs[0] + ctx_outs[1], gc, cmc, gtc, n_ctx_chunks, h_ctx.dtype) if need_ctx else None
    return y_lat, y_ctx

def swiglu(h, w_gu, w_down):
    gate, up = jnp.split(h @ w_gu, 2, axis=-1)
    return (jax.nn.silu(gate) * up) @ w_down

def moe_ffn(h, w_router, b_router, w_gu, w_down, w_sh_gu, w_sh_down):
    N, D = h.shape
    scores = jax.nn.sigmoid((h @ w_router).astype(jnp.float32))
    sel = scores + b_router.astype(jnp.float32)
    grp = sel.reshape(N, N_EXPERT_GROUPS, N_EXPERTS // N_EXPERT_GROUPS)
    grp_score = jnp.sum(lax.top_k(grp, 2)[0], axis=-1)
    _, top_g = lax.top_k(grp_score, TOPK_GROUPS)
    gmask = jnp.any(top_g[:, :, None] == jnp.arange(N_EXPERT_GROUPS)[None, None, :], axis=1)
    sel = jnp.where(jnp.repeat(gmask, N_EXPERTS // N_EXPERT_GROUPS, axis=1), sel, -jnp.inf)
    _, top_e = lax.top_k(sel, TOP_K)
    w = jnp.take_along_axis(scores, top_e, axis=1)
    w = w / jnp.sum(w, axis=-1, keepdims=True) * ROUTED_SCALE

    M = N * TOP_K
    flat_e = top_e.reshape(M).astype(jnp.int32)
    flat_tok = jnp.repeat(jnp.arange(N, dtype=jnp.int32), TOP_K)
    flat_w = w.reshape(M)
    counts = jnp.bincount(flat_e, length=N_EXPERTS).astype(jnp.int32)
    padded = (counts + MOE_BLOCK - 1) // MOE_BLOCK * MOE_BLOCK
    pad_end = jnp.cumsum(padded)
    pad_start = pad_end - padded
    start = jnp.cumsum(counts) - counts
    order = jnp.argsort(flat_e)
    se, stok, sw = flat_e[order], flat_tok[order], flat_w[order]
    dest = pad_start[se] + jnp.arange(M, dtype=jnp.int32) - start[se]
    NB = -(-M // MOE_BLOCK) + N_EXPERTS
    row_tok = jnp.full((NB * MOE_BLOCK,), N, jnp.int32).at[dest].set(stok)
    row_w = jnp.zeros((NB * MOE_BLOCK,), jnp.float32).at[dest].set(sw)
    block_e = jnp.clip(jnp.searchsorted(pad_end, jnp.arange(NB, dtype=jnp.int32) * MOE_BLOCK, side='right'),
                       0, N_EXPERTS - 1)
    h_pad = jnp.concatenate([h, jnp.zeros((1, D), h.dtype)], axis=0)

    def expert_block(acc, blk):
        tok, wts, e = blk
        out = swiglu(h_pad[tok], w_gu[e], w_down[e])
        return acc.at[tok].add(out * wts[:, None].astype(out.dtype)), None

    acc, _ = lax.scan(expert_block, jnp.zeros((N + 1, D), h.dtype),
                      (row_tok.reshape(NB, MOE_BLOCK), row_w.reshape(NB, MOE_BLOCK), block_e))
    return acc[:N] + swiglu(h, w_sh_gu, w_sh_down)

def first_inputs(seed: int = 0) -> dict:
    key = jax.random.key(seed)
    ks = jax.random.split(key, 26)

    def nrm(k, shape, scale):
        return jax.random.normal(k, shape, jnp.float32) * scale

    def gain(k, shape):
        return 1.0 + nrm(k, shape, 0.05)

    D = D_MODEL
    return {
        'x': nrm(ks[0], (BATCH, SEQ, D), 1.0),
        'c': nrm(ks[1], (BATCH, D), 1.0),
        'ctx': nrm(ks[2], (BATCH, CTX_LEN, D), 1.0),
        'c_ctx': nrm(ks[3], (D,), 1.0),
        'w_ada': nrm(ks[4], (DEPTH, D, 6 * D), 0.5 * D ** -0.5),
        'b_ada': nrm(ks[5], (DEPTH, 6 * D), 0.02),
        'g_pre_mix': gain(ks[6], (DEPTH, D)),
        'g_post_mix': gain(ks[7], (DEPTH, D)),
        'g_pre_ffn': gain(ks[8], (DEPTH, D)),
        'g_post_ffn': gain(ks[9], (DEPTH, D)),
        'w_in': nrm(ks[10], (DEPTH, D, D_IN), D ** -0.5),
        'lb_logits': nrm(ks[11], (2, DEPTH + 1, HG_KEY_WIDTH), 0.1),
        'g_hgrn_out': gain(ks[12], (DEPTH, HG_DV)),
        'cm_ln_g': gain(ks[13], (DEPTH, CM_WIDTH)),
        'cm_ln_b': nrm(ks[14], (DEPTH, CM_WIDTH), 0.02),
        'w_spatial': nrm(ks[15], (DEPTH, CM_GROUPS, CM_CHUNK, CM_CHUNK), CM_CHUNK ** -0.5),
        'b_spatial': 1.0 + nrm(ks[16], (DEPTH, CM_CHUNK, CM_GROUPS), 0.1),
        'w_branch_a': nrm(ks[17], (DEPTH, HG_WIDTH, D), HG_WIDTH ** -0.5),
        'w_branch_b': nrm(ks[18], (DEPTH, CM_WIDTH, D), CM_WIDTH ** -0.5),
        'w_out': nrm(ks[19], (DEPTH, D, D), D ** -0.5),
        'w_router': nrm(ks[20], (DEPTH, D, N_EXPERTS), D ** -0.5),
        'b_router': nrm(ks[21], (DEPTH, N_EXPERTS), 0.01),
        'w_expert_gu': nrm(ks[22], (DEPTH, N_EXPERTS, D, 2 * D_EXPERT), D ** -0.5),
        'w_expert_down': nrm(ks[23], (DEPTH, N_EXPERTS, D_EXPERT, D), D_EXPERT ** -0.5),
        'w_shared_gu': nrm(ks[24], (DEPTH, D, 2 * D_SHARED), D ** -0.5),
        'w_shared_down': nrm(ks[25], (DEPTH, D_SHARED, D), D_SHARED ** -0.5),
    }

def first_block(x, c, ctx, c_ctx, w_ada, b_ada, g_pre_mix, g_post_mix, g_pre_ffn, g_post_ffn, w_in,
              lb_logits, g_hgrn_out, cm_ln_g, cm_ln_b, w_spatial, b_spatial, w_branch_a, w_branch_b,
              w_out, w_router, b_router, w_expert_gu, w_expert_down, w_shared_gu, w_shared_down):
    B, T, D = x.shape
    L = ctx.shape[1]
    rows = T // GRID_W
    n_lat_chunks = rows // ROWS_PER_CHUNK
    n_ctx_chunks = L // CM_CHUNK
    lower_bounds = jnp.cumsum(jax.nn.softmax(lb_logits.astype(jnp.float32), axis=1), axis=1)
    silu_c = jax.nn.silu(c)
    silu_cc = jax.nn.silu(c_ctx)
    x_lat, x_ctx = x, ctx
    for l in range(DEPTH):
        need_ctx = l < DEPTH - 1
        mod_lat = (silu_c @ w_ada[l] + b_ada[l])[:, None, :]
        mod_ctx = silu_cc @ w_ada[l] + b_ada[l]
        sh1, sc1, gt1, sh2, sc2, gt2 = jnp.split(mod_lat, 6, axis=-1)
        csh1, csc1, cgt1, csh2, csc2, cgt2 = jnp.split(mod_ctx, 6, axis=-1)

        h_lat = rms_norm(x_lat, g_pre_mix[l]) * (1.0 + sc1) + sh1
        h_ctx = rms_norm(x_ctx, g_pre_mix[l]) * (1.0 + csc1) + csh1
        y_lat, y_ctx = token_mixer(h_lat, h_ctx, w_in[l], lower_bounds[:, l], g_hgrn_out[l], cm_ln_g[l],
                                   cm_ln_b[l], w_spatial[l], b_spatial[l], w_branch_a[l], w_branch_b[l],
                                   w_out[l], n_lat_chunks, n_ctx_chunks, need_ctx)
        x_lat = x_lat + gt1 * rms_norm(y_lat, g_post_mix[l])
        if need_ctx:
            x_ctx = x_ctx + cgt1 * rms_norm(y_ctx, g_post_mix[l])

        h2_lat = (rms_norm(x_lat, g_pre_ffn[l]) * (1.0 + sc2) + sh2).reshape(B * T, D)
        if need_ctx:
            h2_ctx = (rms_norm(x_ctx, g_pre_ffn[l]) * (1.0 + csc2) + csh2).reshape(B * L, D)
            f_all = moe_ffn(jnp.concatenate([h2_lat, h2_ctx], axis=0), w_router[l], b_router[l],
                            w_expert_gu[l], w_expert_down[l], w_shared_gu[l], w_shared_down[l])
            f_lat, f_ctx = f_all[:B * T], f_all[B * T:]
            x_ctx = x_ctx + cgt2 * rms_norm(f_ctx.reshape(B, L, D), g_post_ffn[l])
        else:
            f_lat = moe_ffn(h2_lat, w_router[l], b_router[l], w_expert_gu[l], w_expert_down[l],
                            w_shared_gu[l], w_shared_down[l])
        x_lat = x_lat + gt2 * rms_norm(f_lat.reshape(B, T, D), g_post_ffn[l])
    return x_lat


ATT_HEADS = 8
ATT_KV_HEADS = 2
ATT_GROUP = ATT_HEADS // ATT_KV_HEADS
ATT_HEAD_DIM = 64
WINDOW = 128
ATT_BLOCK = 128
ROPE_DIM = ATT_HEAD_DIM // 4
ROPE_THETA = 500000.0

RET_HEADS = 4
RET_KEY_DIM = 128
RET_VAL_DIM = 256
RET_CHUNK = 128
RET_ROT_BASE = 10000.0

D_FF = 4 * D_MODEL

NORM_EPS = 1e-6
GN_EPS = 1e-6
NEG_INF = -1e30

ATT_Q_W = ATT_HEADS * ATT_HEAD_DIM
ATT_KV_W = ATT_KV_HEADS * ATT_HEAD_DIM
RET_QK_W = RET_HEADS * RET_KEY_DIM
RET_V_W = RET_HEADS * RET_VAL_DIM
IN_SPLITS = (ATT_Q_W, ATT_KV_W, ATT_KV_W, RET_QK_W, RET_QK_W, RET_V_W, RET_V_W, D_MODEL, D_MODEL)
IN_WIDTH = sum(IN_SPLITS)
IN_OFFSETS = tuple(int(v) for v in np.cumsum(IN_SPLITS)[:-1])


def rmsnorm(x, gain):
    xf = x.astype(jnp.float32)
    y = xf * lax.rsqrt(jnp.mean(xf * xf, axis=-1, keepdims=True) + NORM_EPS)
    return (y * gain.astype(jnp.float32)).astype(x.dtype)

def rope_tables(seq_len, dim, theta):
    pos = jnp.arange(seq_len, dtype=jnp.float32)
    inv_freq = theta ** (-jnp.arange(0, dim, 2, dtype=jnp.float32) / dim)
    ang = pos[:, None] * inv_freq[None, :]
    return jnp.cos(ang)[:, None, :], jnp.sin(ang)[:, None, :]

def apply_rope(x, cos, sin):
    xf = x.astype(jnp.float32)
    x1, x2 = jnp.split(xf, 2, axis=-1)
    out = jnp.concatenate([x1 * cos - x2 * sin, x2 * cos + x1 * sin], axis=-1)
    return out.astype(x.dtype)

def partial_rope(x, cos, sin):
    return jnp.concatenate([apply_rope(x[..., :ROPE_DIM], cos, sin), x[..., ROPE_DIM:]], axis=-1)

def sliding_window_sink_attention(q, k, v, sinks):
    b, s, _, dh = q.shape
    c = ATT_BLOCK
    nb = s // c
    qb = q.reshape(b, nb, c, ATT_KV_HEADS, ATT_GROUP, dh)
    kb = k.reshape(b, nb, c, ATT_KV_HEADS, dh)
    vb = v.reshape(b, nb, c, ATT_KV_HEADS, dh)

    def with_prev(t):
        prev = jnp.concatenate([jnp.zeros_like(t[:, :1]), t[:, :-1]], axis=1)
        return jnp.concatenate([prev, t], axis=2)

    kw, vw = with_prev(kb), with_prev(vb)
    scores = jnp.einsum('bnqhgd,bnkhd->bnhgqk', qb, kw,
                        preferred_element_type=jnp.float32) * (dh ** -0.5)
    qi = jnp.arange(c)[:, None] + c
    kj = jnp.arange(2 * c)[None, :]
    delta = qi - kj
    in_window = (delta >= 0) & (delta < WINDOW)
    has_prev = (jnp.arange(nb) > 0)[:, None, None] | (kj >= c)[None]
    mask = in_window[None] & has_prev
    scores = jnp.where(mask[None, :, None, None], scores, NEG_INF)
    sink = sinks.astype(jnp.float32).reshape(ATT_KV_HEADS, ATT_GROUP)[None, None, :, :, None, None]
    sink = jnp.broadcast_to(sink, scores.shape[:-1] + (1,))
    probs = jax.nn.softmax(jnp.concatenate([scores, sink], axis=-1), axis=-1)[..., :-1]
    out = jnp.einsum('bnhgqk,bnkhd->bnqhgd', probs.astype(v.dtype), vw)
    return out.reshape(b, s, ATT_HEADS * dh)

def chunkwise_retention(q, k, v):
    b, s, h, dk = q.shape
    dv = v.shape[-1]
    c = RET_CHUNK
    nc = s // c
    log_gamma = jnp.log1p(-jnp.exp2(-5.0 - jnp.arange(h, dtype=jnp.float32)))
    idx = jnp.arange(c, dtype=jnp.float32)
    diff = idx[:, None] - idx[None, :]
    intra = jnp.where(diff >= 0, jnp.exp(jnp.maximum(diff, 0.0) * log_gamma[:, None, None]), 0.0)
    q_decay = jnp.exp((idx + 1.0)[None, :] * log_gamma[:, None])[..., None]
    k_decay = jnp.exp((c - 1.0 - idx)[None, :] * log_gamma[:, None])[..., None]
    chunk_decay = jnp.exp(c * log_gamma)[:, None, None]

    def to_chunks(t):
        return t.astype(jnp.float32).reshape(b, nc, c, h, t.shape[-1]).transpose(1, 0, 3, 2, 4)

    qc, kc, vc = to_chunks(q), to_chunks(k), to_chunks(v)

    def step(state, inp):
        qi, ki, vi = inp
        att = jnp.einsum('bhqd,bhkd->bhqk', qi, ki) * intra
        inner = jnp.einsum('bhqk,bhkv->bhqv', att, vi)
        cross = jnp.einsum('bhqd,bhdv->bhqv', qi * q_decay, state)
        new_state = state * chunk_decay + jnp.einsum('bhkd,bhkv->bhdv', ki * k_decay, vi)
        return new_state, inner + cross

    state0 = jnp.zeros((b, h, dk, dv), jnp.float32)
    _, out = lax.scan(step, state0, (qc, kc, vc))
    return out.transpose(1, 0, 3, 2, 4).reshape(b, s, h, dv)

def head_groupnorm(y, gain):
    b, s, h, dv = y.shape
    mu = jnp.mean(y, axis=-1, keepdims=True)
    var = jnp.mean(jnp.square(y - mu), axis=-1, keepdims=True)
    yn = (y - mu) * lax.rsqrt(var + GN_EPS)
    return yn.reshape(b, s, h * dv) * gain.astype(jnp.float32)

def mixer_block(xn, w_in, b_gates, attn_sinks, ret_gn_gain, w_att_up, w_ret_up, w_out, att_rope, ret_rope):
    b, s, _ = xn.shape
    proj = jnp.einsum('bsd,dn->bsn', xn, w_in)
    q_a, k_a, v_a, q_r, k_r, v_r, g_r, gate_a, gate_r = jnp.split(proj, IN_OFFSETS, axis=-1)

    q_a = partial_rope(q_a.reshape(b, s, ATT_HEADS, ATT_HEAD_DIM), *att_rope)
    k_a = partial_rope(k_a.reshape(b, s, ATT_KV_HEADS, ATT_HEAD_DIM), *att_rope)
    v_a = v_a.reshape(b, s, ATT_KV_HEADS, ATT_HEAD_DIM)
    y_a = sliding_window_sink_attention(q_a, k_a, v_a, attn_sinks) @ w_att_up

    q_r = apply_rope(q_r.reshape(b, s, RET_HEADS, RET_KEY_DIM), *ret_rope)
    k_r = apply_rope(k_r.reshape(b, s, RET_HEADS, RET_KEY_DIM), *ret_rope) * (RET_KEY_DIM ** -0.5)
    ret = chunkwise_retention(q_r, k_r, v_r.reshape(b, s, RET_HEADS, RET_VAL_DIM))
    ret = head_groupnorm(ret, ret_gn_gain)
    y_r = (jax.nn.silu(g_r.astype(jnp.float32)) * ret).astype(xn.dtype) @ w_ret_up

    bg = b_gates.astype(jnp.float32)
    ga = jax.nn.sigmoid(gate_a.astype(jnp.float32) + bg[:D_MODEL])
    gr = jax.nn.sigmoid(gate_r.astype(jnp.float32) + bg[D_MODEL:])
    merged = (ga * y_a.astype(jnp.float32) + gr * y_r.astype(jnp.float32)).astype(xn.dtype)
    return merged @ w_out

def squared_relu_mlp(xn, w_ff1, w_ff2):
    hdn = jnp.square(jax.nn.relu(xn @ w_ff1))
    return hdn @ w_ff2

def second_inputs(seed: int = 0) -> dict:
    key = jax.random.key(seed)
    ks = jax.random.split(key, 14)
    f32 = jnp.float32

    def normal(k, shape, scale):
        return jax.random.normal(k, shape, f32) * scale

    def gain(k, shape):
        return 1.0 + 0.02 * jax.random.normal(k, shape, f32)

    return {
        'x': normal(ks[0], (BATCH, SEQ, D_MODEL), 1.0),
        'norm_mix_gain': gain(ks[1], (DEPTH, D_MODEL)),
        'w_in': normal(ks[2], (DEPTH, D_MODEL, IN_WIDTH), D_MODEL ** -0.5),
        'b_gates': normal(ks[3], (DEPTH, 2 * D_MODEL), 0.1),
        'attn_sinks': normal(ks[4], (DEPTH, ATT_HEADS), 0.5),
        'ret_gn_gain': gain(ks[5], (DEPTH, RET_V_W)),
        'w_att_up': normal(ks[6], (DEPTH, ATT_Q_W, D_MODEL), ATT_Q_W ** -0.5),
        'w_ret_up': normal(ks[7], (DEPTH, RET_V_W, D_MODEL), RET_V_W ** -0.5),
        'w_out': normal(ks[8], (DEPTH, D_MODEL, D_MODEL), D_MODEL ** -0.5),
        'norm_mlp_gain': gain(ks[9], (DEPTH, D_MODEL)),
        'w_ff1': normal(ks[10], (DEPTH, D_MODEL, D_FF), D_MODEL ** -0.5),
        'w_ff2': normal(ks[11], (DEPTH, D_FF, D_MODEL), D_FF ** -0.5),
        'norm_final_gain': gain(ks[12], (D_MODEL,)),
    }

def second_block(x, norm_mix_gain, w_in, b_gates, attn_sinks, ret_gn_gain, w_att_up, w_ret_up, w_out,
              norm_mlp_gain, w_ff1, w_ff2, norm_final_gain):
    s = x.shape[1]
    att_rope = rope_tables(s, ROPE_DIM, ROPE_THETA)
    ret_rope = rope_tables(s, RET_KEY_DIM, RET_ROT_BASE)
    h = x
    for l in range(DEPTH):
        h = h + mixer_block(rmsnorm(h, norm_mix_gain[l]), w_in[l], b_gates[l], attn_sinks[l],
                            ret_gn_gain[l], w_att_up[l], w_ret_up[l], w_out[l], att_rope, ret_rope)
        h = h + squared_relu_mlp(rmsnorm(h, norm_mlp_gain[l]), w_ff1[l], w_ff2[l])
    return rmsnorm(h, norm_final_gain)


def setup_inputs(seed=0):
    out = dict(first_inputs(seed))
    for name, value in second_inputs(seed + 1).items():
        if name != "x":
            out[name + "_2"] = value
    return out


def reference(
    x, c, ctx, c_ctx, w_ada, b_ada, g_pre_mix, g_post_mix, g_pre_ffn, g_post_ffn, w_in,
    lb_logits, g_hgrn_out, cm_ln_g, cm_ln_b, w_spatial, b_spatial, w_branch_a, w_branch_b,
    w_out, w_router, b_router, w_expert_gu, w_expert_down, w_shared_gu, w_shared_down,
    norm_mix_gain_2, w_in_2, b_gates_2, attn_sinks_2, ret_gn_gain_2, w_att_up_2, w_ret_up_2,
    w_out_2, norm_mlp_gain_2, w_ff1_2, w_ff2_2, norm_final_gain_2,
):
    x = first_block(
        x, c, ctx, c_ctx, w_ada, b_ada, g_pre_mix, g_post_mix, g_pre_ffn, g_post_ffn, w_in,
        lb_logits, g_hgrn_out, cm_ln_g, cm_ln_b, w_spatial, b_spatial, w_branch_a, w_branch_b,
        w_out, w_router, b_router, w_expert_gu, w_expert_down, w_shared_gu, w_shared_down,
    )
    return second_block(
        x, norm_mix_gain_2, w_in_2, b_gates_2, attn_sinks_2, ret_gn_gain_2, w_att_up_2,
        w_ret_up_2, w_out_2, norm_mlp_gain_2, w_ff1_2, w_ff2_2, norm_final_gain_2,
    )


_drawn_inputs = setup_inputs


def setup_inputs(seed=0):
    import zlib

    import numpy as np

    out = dict(_drawn_inputs(seed))
    spreads = {}
    factors = {'ctx': 3.508,
     'c_ctx': 5.48,
     'g_post_ffn': 3.073,
     'lb_logits': 5.745,
     'cm_ln_b': 3.612,
     'norm_mix_gain_2': 4.205,
     'b_gates_2': 4.349,
     'attn_sinks_2': 64.0,
     'ret_gn_gain_2': 22.175,
     'norm_mlp_gain_2': 11.952,
     'norm_final_gain_2': 8.066}
    for name, (base, spread) in spreads.items():
        noise = np.random.default_rng([zlib.crc32(name.encode()), seed]).standard_normal(out[name].shape)
        drawn = base * np.exp(spread * noise) if base else spread * noise
        out[name] = jnp.asarray(drawn.astype(out[name].dtype))
    for name, factor in factors.items():
        out[name] = (out[name] * factor).astype(out[name].dtype)
    return out
```

```python
from contextlib import ExitStack

import numpy as np

import concourse.bass as bass
from concourse import mybir

ALU = mybir.AluOpType
ACT = mybir.ActivationFunctionType
F32 = mybir.dt.float32
I32 = mybir.dt.int32
U32 = mybir.dt.uint32
AX = mybir.AxisListType.X

P = 128
TOK, CTX, D = 512, 256, 1024
KD = D // P
NT, NC_ = TOK // P, CTX // P
HG = 4
SUB = 16
NS = P // SUB
NE, TOPK, NGRP = 64, 8, 8
EPS = 1e-6
UNIT = 2048
RING = 6
NBANK = 4
NEG = -1.0e30
CHUNK_DECAY = [float(np.exp(np.float32(P) * np.log1p(-np.exp2(np.float32(-5.0 - h)))).astype(np.float32)) for h in range(4)]
WORK = 26800

U_ADAC, U_Q, U_F0, U_V, U_G, U_U, U_CV, U_F1, U_ROW = 8, 2, 2, 2, 2, 2, 2, 2, 16
U_MIX = U_ADAC + U_Q + U_F0 + U_V + U_G + U_U + U_CV + U_F1 + U_ROW + 2 * 6 + 4
U_EXP = 3 * NE
U_SHARED = 3

PC = {}
for _name, _w in (("c", KD), ("cc", KD), ("gpre", KD), ("bsh1", KD), ("bsc1", KD), ("lb", 16),
                  ("bg", 16), ("nmix", KD), ("nmlp", KD)):
    PC[_name] = (sum(w for _, w in PC.values()), _w)
PCW = sum(w for _, w in PC.values())

C1 = {}
for _name, _w in (("ident", P), ("before", P), ("maskf", 4 * P), ("maskb", 4 * P), ("slots", P), ("part", 1),
                  ("tok", 4), ("pad", 3)):
    C1[_name] = (sum(w for _, w in C1.values()), _w)
C1W = sum(w for _, w in C1.values())

C2 = {}
for _name, _w in (("acos", 4 * 8), ("asin", 4 * 8), ("qcos", 4 * 64), ("qsin", 4 * 64), ("kcos", 4 * 64),
                  ("ksin", 4 * 64), ("win", 256), ("intra", 4 * P), ("qdec", 4 * P), ("kdec", 4), ("pad", 4)):
    C2[_name] = (sum(w for _, w in C2.values()), _w)
C2W = sum(w for _, w in C2.values())

ROWS = {}
for _name, _w in (("b_ada", 4096), ("g_post_mix", D), ("g_pre_ffn", D), ("g_post_ffn", D), ("g_hgrn", P),
                  ("ln_g", 512), ("ln_b", 512), ("b_s", 512), ("b_router", NE), ("sinks", 8),
                  ("ret_gain", D), ("norm_final", D)):
    ROWS[_name] = (sum(w for _, w in ROWS.values()), _w)
ROWSW = sum(w for _, w in ROWS.values())


class Items:

    def __init__(self):
        self.order, self.number, self.freed = [], {}, {"act": 0, "dve": 0}

    def add(self, key, by):
        self.number[key] = len(self.order)
        self.freed[by] += 1
        self.order.append((key, by, self.freed[by]))


def mixer_items():
    it = Items()
    for n in range(U_ADAC):
        it.add(("ada", n), "dve")
    for k in range(KD):
        it.add(("xT", k), "dve" if k % 2 else "act")
    for k in range(KD):
        it.add(("cT", k), "dve" if k % 2 else "act")
    for m in range(4):
        it.add(("q", m), "act")
    for h in range(4):
        it.add(("f", 0, h), "act")
        it.add(("fc", 0, h), "act")
    for c in range(2):
        for tp in range(3):
            it.add(("v", c, tp), "dve")
    for c in range(2):
        for tp in range(2):
            it.add(("g", c, tp), "act")
    for m in range(4):
        it.add(("u", m), "act")
    for c in range(2):
        for tp in range(2):
            it.add(("cv", c, tp), "act")
    for h in range(4):
        it.add(("f", 1, h), "act")
        it.add(("fc", 1, h), "act")
    for r in range(4):
        for j in range(2):
            it.add(("row", r, j), "dve")
    for g in range(4):
        it.add(("sp", g), "dve")
    for h in range(4):
        it.add(("aT", h), "act")
    for j in range(2):
        for kind, by in (("ga", "act"), ("A", "dve"), ("gb", "act"), ("B", "dve")):
            for m in range(4):
                it.add((kind, 4 * j + m), by)
    for c in range(4):
        for tp in range(2):
            it.add(("y", c, tp), "act")
    return it


FILL0 = [("g", c, tp) for c in range(2) for tp in range(2)] + [("u", m) for m in range(4)] + \
        [("cv", c, tp) for c in range(2) for tp in range(2)]
FILL1 = [("row", r, j) for r in range(4) for j in range(2)] + [("sp", g) for g in range(4)]
ORDER = ((0, 1, 2, 3, 4, 5), (1, 0, 5, 4, 3, 2))


def program(nc, x, ctx_in, stream, rows, cols, const1, w_spatial, experts, w_router, const2, out):
    with ExitStack() as es:
        def sb(name, width, dt=F32):
            return es.enter_context(nc.sbuf_tensor(name, [P, width], dt))

        banks = [es.enter_context(nc.psum_tensor(f"bank{i}", [P, 512], F32)) for i in range(8)]
        m = {
            "ring": sb("ring", RING * UNIT), "X": sb("X", NT * D), "HT": sb("HT", KD * TOK),
            "cols": sb("cols", PCW), "const1": sb("const1", C1W), "adarow": sb("adarow", 4 * D),
            "work": sb("work", WORK),
        }
        dram = {
            "xn": nc.dram_tensor("h2_rows", [TOK, D], F32),
            "slots": nc.dram_tensor("slot_outputs", [TOK * TOPK, D], F32),
        }
        s_unit = [es.enter_context(nc.semaphore(f"unit_arrived{i}")) for i in range(RING)]
        taken = []

        def sem(name):
            taken.append(nc.alloc_semaphore(name=name))
            return taken[-1]

        def next_phase():
            nc.all_engine_barrier()
            nc.clear_and_free_semaphores(list(taken))
            taken.clear()
            nc.all_engine_barrier()

        mixer(nc, sem, banks, m, s_unit, x, ctx_in, stream, rows, cols, const1, w_spatial)
        next_phase()
        moe(nc, sem, banks, m, dram, s_unit, stream, experts, rows, w_router)
        next_phase()
        block2(nc, sem, banks, m, s_unit, stream, rows, const2, out)


def unit_in(sp, m, stream, s_unit, s_used, last_item, n):
    if n >= RING:
        sp.wait_ge(s_used, last_item(n - RING) + 1)
    s = n % RING
    sp.dma_start(m["ring"][:, s * UNIT:(s + 1) * UNIT], stream[n]).then_inc(s_unit[s], 16)


def unit_ready(eng, s_unit, n):
    eng.wait_ge(s_unit[n % RING], 16 * (n // RING + 1))


def mixer(nc, sem, banks, mem, s_unit, x, ctx_in, stream, rows, cols, const1, w_spatial):
    W = mem["work"]

    def part(first, width):
        assert first + width <= WORK
        return W[:, first:first + width]

    def grid(a, outer):
        return a.rearrange("p (a b) -> p a b", a=outer)

    X = grid(mem["X"][:, :], NT)
    HT = grid(mem["HT"][:, :], KD)
    XN, XC, XCN, JUNK = grid(part(0, 4096), NT), grid(part(4096, 2048), NC_), grid(part(6144, 2048), NC_), part(8192, 1024)
    qT, KK, LF = grid(part(0, 2048), 4), grid(part(2048, 3072), 4), grid(part(5120, 3072), 4)
    V, G = grid(part(8192, 3072), 6), grid(part(11264, 2048), 4)
    UT, CV, O = grid(part(13312, 2048), 4), grid(part(15360, 2048), 4), grid(part(17408, 2048), 4)
    HC = grid(part(19456, 2048), KD)
    CSB = grid(part(20480, 1024), KD)
    BB, EK, QE, QD, KTs, AT, S = (grid(part(21504 + 512 * i, 512), 4) for i in range(7))
    KM = [grid(part(25088 + 512 * i, 512), 4) for i in range(2)]
    ONES, small = part(26112, P), [26112 + P]

    def tiny(width):
        small[0] += width
        return part(small[0] - width, width)

    CSC = grid(tiny(2 * KD), KD)
    SH, SC = grid(tiny(2 * KD), 2), grid(tiny(2 * KD), 2)
    LBE, LB1, LBM = tiny(16), tiny(16), tiny(8)
    ADA = tiny(32)
    DEC, SS, SS2 = tiny(4), tiny(16), tiny(16)
    ST, MV, RS = tiny(24), tiny(8), tiny(4)
    aT, SG, yT = grid(part(0, 2048), 4), grid(part(2048, 2048), 4), grid(part(4096, 4096), KD)
    GAIN, Y = part(8192, 3072), grid(part(11264, 4096), NT)
    XS = mem["X"]
    LNG, LNB, BS, GH = XS[:, 0:512], XS[:, 512:1024], grid(XS[:, 1024:1536], 4), XS[:, 1536:1664]
    WS = grid(XS[:, 2048:2560], 4)
    ROW = grid(mem["adarow"][:, :], 4)

    def col(name):
        a, w = PC[name]
        return mem["cols"][:, a:a + w]

    def con(name):
        a, w = C1[name]
        return mem["const1"][:, a:a + w]

    ident = con("ident")
    it = mixer_items()
    s_full, s_act, s_dve = sem("bank_full"), sem("bank_read_by_act"), sem("bank_read_by_dve")
    freed_by = {"act": s_act, "dve": s_dve}

    def bank_of(key):
        return banks[it.number[key] % NBANK]

    def bank_free(pe, key):
        n = it.number[key]
        if n >= NBANK:
            _, by, count = it.order[n - NBANK]
            pe.wait_ge(freed_by[by], count)

    def item_full(eng, key):
        eng.wait_ge(s_full, it.number[key] + 1)

    def item_read(key):
        _, by, count = it.order[it.number[key]]
        return freed_by[by], count

    names = ("x_in", "ctx_in", "cols_in", "const_in", "lnrow_in", "adarow_in", "gain_in", "x_again", "ws_in",
             "silu_c", "sums_ready", "mean_ready", "root_ready", "xn_ready", "ada_ready", "csb_ready",
             "lb_diff", "lb_exp", "f_ready", "logf_ready",
             "b_ready", "qmid_ready", "kmid_ready", "q_ready", "kend_ready", "at_ready", "state_ready", "o_added",
             "e_end", "e_q", "e_k", "kt_copied", "o_copied", "k_ready", "kt_done", "a_done", "su_done", "o_done",
             "ln_var", "ln_root", "ln_ready", "o_sq", "o_root", "a_ready", "bm_ready", "summed",
             "y_sums", "y_ss", "y_root", "mixed", "dve_order")
    s = {n: sem(n) for n in names}
    unit0 = {}
    n = 0
    for name, width in (("ada", U_ADAC), ("q", 2), ("f0", 2), ("v", 2), ("g", 2), ("u", 2), ("cv", 2), ("f1", 2),
                        ("row", U_ROW), ("ga0", 2), ("A0", 1), ("gb0", 2), ("B0", 1),
                        ("ga1", 2), ("A1", 1), ("gb1", 2), ("B1", 1), ("y", 4)):
        unit0[name] = n
        n += width
    assert n == U_MIX
    uses = {}

    def use(name, keys):
        for i, key in enumerate(keys):
            uses[unit0[name] + i] = it.number[key]

    use("ada", [("ada", n) for n in range(U_ADAC)])
    use("q", [("q", 1), ("q", 3)])
    use("f0", [("fc", 0, 1), ("fc", 0, 3)])
    use("v", [("v", 0, 2), ("v", 1, 2)])
    use("g", [("g", 0, 1), ("g", 1, 1)])
    use("u", [("u", 1), ("u", 3)])
    use("cv", [("cv", 0, 1), ("cv", 1, 1)])
    use("f1", [("fc", 1, 1), ("fc", 1, 3)])
    use("row", [("row", n // 4, n % 4 // 2) for n in range(U_ROW)])
    for j in range(2):
        use(f"ga{j}", [("ga", 4 * j + 1), ("ga", 4 * j + 3)])
        use(f"A{j}", [("A", 4 * j + 3)])
        use(f"gb{j}", [("gb", 4 * j + 1), ("gb", 4 * j + 3)])
        use(f"B{j}", [("B", 4 * j + 3)])
    use("y", [("y", c, 1) for c in range(4)])

    def last_item(n):
        return uses[n]

    STEPS = [(d, i, t) for d in range(2) for i, t in enumerate(ORDER[d])]

    with nc.Block() as block:

        @block.sync
        def _(sp):
            for t in range(NT):
                sp.dma_start(X[:, t, :], x[t * P:(t + 1) * P, :]).then_inc(s["x_in"], 16)
            sp.dma_start(mem["cols"][:, :], cols).then_inc(s["cols_in"], 16)
            for t in range(NC_):
                sp.dma_start(XC[:, t, :], ctx_in[t * P:(t + 1) * P, :]).then_inc(s["ctx_in"], 16)
            for n in range(U_ADAC):
                unit_in(sp, mem, stream, s_unit, s_full, last_item, n)
            sp.dma_start(mem["const1"][:, :], const1).then_inc(s["const_in"], 16)
            sp.dma_start(mem["adarow"][:, :], rows[0:1, 0:4 * D].to_broadcast([P, 4 * D])).then_inc(s["adarow_in"], 16)
            for n in range(U_ADAC, unit0["g"]):
                unit_in(sp, mem, stream, s_unit, s_full, last_item, n)
            sp.wait_ge(s["xn_ready"], NT)
            a = ROWS["ln_g"][0]
            sp.dma_start(XS[:, 0:1536], rows[0:1, a:a + 1536].to_broadcast([P, 1536])).then_inc(s["lnrow_in"], 16)
            a = ROWS["g_hgrn"][0]
            sp.dma_start(GH, rows[0:1, a:a + P].to_broadcast([P, P])).then_inc(s["lnrow_in"], 16)
            sp.dma_start(XS[:, 2048:2560], w_spatial).then_inc(s["ws_in"], 16)
            for n in range(unit0["g"], unit0["ga0"] + 2):
                unit_in(sp, mem, stream, s_unit, s_full, last_item, n)
            sp.wait_ge(s["o_done"], 8)
            a = ROWS["g_post_mix"][0]
            sp.dma_start(GAIN, rows[0:1, a:a + 3072].to_broadcast([P, 3072])).then_inc(s["gain_in"], 16)
            sp.wait_ge(s["a_ready"], 4)
            sp.wait_ge(s["bm_ready"], 4)
            for t in range(NT):
                sp.dma_start(X[:, t, :], x[t * P:(t + 1) * P, :]).then_inc(s["x_again"], 16)
            for n in range(unit0["ga0"] + 2, U_MIX):
                unit_in(sp, mem, stream, s_unit, s_full, last_item, n)

        @block.gpsimd
        def _(pool):
            step = 0
            for d, i, t in STEPS:
                if t < NC_:
                    continue
                for j in range(NS):
                    lo, hi = (0, SUB * (j + 1)) if d == 0 else (SUB * j, P)
                    pool.wait_ge(s["e_k"], NS * step + j + 1)
                    km = KM[j % 2][:, :, lo:hi]
                    nc.gpsimd.tensor_tensor(km, km, KK[:, :, t * P + lo:t * P + hi], ALU.mult).then_inc(s["k_ready"], 1)
                step += 1

        @block.scalar
        def _(act):
            act.wait_ge(s["cols_in"], 16)
            nc.scalar.activation(CSC[:, :, 0], col("c"), ACT.Silu)
            nc.scalar.activation(CSC[:, :, 1], col("cc"), ACT.Silu).then_inc(s["silu_c"], 1)
            act.wait_ge(s["lb_diff"], 1)
            nc.scalar.activation(LBE[:, :], LBE[:, :], ACT.Exp).then_inc(s["lb_exp"], 1)
            act.wait_ge(s["x_in"], 16 * NT)
            act.wait_ge(s["ctx_in"], 16 * NC_)
            for t in range(NT + NC_):
                src = X[:, t, :] if t < NT else XC[:, t - NT, :]
                nc.scalar.activation(JUNK, src, ACT.Square, accum_out=SS[:, t:t + 1]).then_inc(s["sums_ready"], 1)
                act.wait_ge(s["sums_ready"], t + 1)
            act.wait_ge(s["mean_ready"], 1)
            nc.scalar.activation(SS2[:, 0:6], SS[:, 0:6], ACT.Sqrt).then_inc(s["root_ready"], 1)
            act.wait_ge(s["ada_ready"], 2)
            for v, kind, dst, width in ((0, "xT", HT, TOK), (1, "cT", HC, CTX)):
                for k in range(0, KD, 2):
                    item_full(act, (kind, k))
                    nc.scalar.activation(dst[:, k, :], bank_of((kind, k))[:, 0:width], ACT.Identity,
                                         bias=SH[:, v, k:k + 1], scale=SC[:, v, k:k + 1]).then_inc(s_act, 1)
            for h in range(4):
                item_full(act, ("q", h))
                nc.scalar.activation(qT[:, h, :], bank_of(("q", h))[:, :], ACT.Silu).then_inc(s_act, 1)

            def gates(d):
                if d == 1:
                    act.wait_ge(s["k_ready"], 4 * NS)
                for h in range(4):
                    for key, lo, width in ((("f", d, h), CTX, TOK), (("fc", d, h), 0, CTX)):
                        item_full(act, key)
                        b = bank_of(key)[:, 0:width]
                        nc.scalar.activation(LF[:, h, lo:lo + width], b, ACT.Sigmoid)
                        nc.scalar.activation(KK[:, h, lo:lo + width], b, ACT.Sigmoid, scale=-1.0).then_inc(s_act, 1)
                act.wait_ge(s["f_ready"], d + 1)
                for h in range(4):
                    nc.scalar.activation(LF[:, h, :], LF[:, h, :], ACT.Ln).then_inc(s["logf_ready"], 1)

            def fill(key):
                item_full(act, key)
                b = bank_of(key)
                if key[0] == "u":
                    nc.scalar.activation(UT[:, key[1], :], b[:, :], ACT.Gelu_apprx_tanh).then_inc(s_act, 1)
                else:
                    dst, f = (G, ACT.Silu) if key[0] == "g" else (CV, ACT.Gelu_apprx_tanh)
                    c, tp = key[1:]
                    nc.scalar.activation(dst[:, 2 * tp:2 * tp + 2, 256 * c:256 * (c + 1)], grid(b[:, :], 2),
                                         f).then_inc(s_act, 1)

            def recur(n):
                d, i, t = STEPS[n]
                end = P - 1 if d == 0 else 0
                act.wait_ge(s["b_ready"], n + 1)
                if n:
                    act.wait_ge(s["kt_done"], n)
                    act.wait_ge(s["state_ready"], n)
                for h in range(4):
                    nc.scalar.activation(EK[:, h, :], BB[:, h, :], ACT.Exp, bias=BB[:, h, end:end + 1], scale=-1.0)
                nc.scalar.activation(DEC[:, :], BB[:, :, end], ACT.Exp).then_inc(s["e_end"], 1)
                if t >= NC_:
                    step = 4 * d + i - 2
                    if step:
                        act.wait_ge(s["o_done"], step)
                    nc.scalar.activation(QE, BB, ACT.Exp)
                    act.wait_ge(s["qmid_ready"], step + 1)
                    nc.scalar.activation(QD, QD, ACT.Exp).then_inc(s["e_q"], 1)
                    for j in range(NS):
                        lo, hi = (0, SUB * (j + 1)) if d == 0 else (SUB * j, P)
                        act.wait_ge(s["kmid_ready"], NS * step + j + 1)
                        km = KM[j % 2][:, :, lo:hi]
                        nc.scalar.activation(km, km, ACT.Exp).then_inc(s["e_k"], 1)
                act.wait_ge(s["kt_done"], n + 1)
                if n:
                    act.wait_ge(s["su_done"], n)
                nc.scalar.activation(KTs, grid(banks[6][:, :], 4), ACT.Copy).then_inc(s["kt_copied"], 1)
                if t >= NC_ and d == 0:
                    act.wait_ge(s["o_done"], i - 1)
                    nc.scalar.activation(O[:, t - NC_, :], banks[5][:, :], ACT.Copy).then_inc(s["o_copied"], 1)

            gates(0)
            for n in range(6):
                recur(n)
                fill(FILL0[2 * n])
                fill(FILL0[2 * n + 1])
            act.wait_ge(s["ln_var"], 1)
            nc.scalar.activation(RS[:, :], RS[:, :], ACT.Sqrt).then_inc(s["ln_root"], 1)
            gates(1)
            for n in range(6, 12):
                recur(n)
            act.wait_ge(s["o_sq"], 1)
            nc.scalar.activation(SS2[:, :], SS[:, :], ACT.Sqrt).then_inc(s["o_root"], 1)
            for h in range(4):
                item_full(act, ("aT", h))
                nc.scalar.activation(aT[:, h, :], bank_of(("aT", h))[:, :], ACT.Copy).then_inc(s_act, 1)
            for j in range(2):
                for w, kind in enumerate(("ga", "gb")):
                    for mm in range(4):
                        if w == 1:
                            sk, ck = item_read(("A", 4 * j + mm))
                            act.wait_ge(sk, ck)
                        elif j == 1:
                            act.wait_ge(s["summed"], mm + 1)
                        item_full(act, (kind, 4 * j + mm))
                        nc.scalar.activation(SG[:, mm, :], bank_of((kind, 4 * j + mm))[:, :],
                                             ACT.Sigmoid).then_inc(s_act, 1)
            for c in range(4):
                for tp in range(2):
                    item_full(act, ("y", c, tp))
                    nc.scalar.activation(Y[:, 2 * tp:2 * tp + 2, 256 * c:256 * (c + 1)],
                                         grid(bank_of(("y", c, tp))[:, :], 2), ACT.Copy).then_inc(s_act, 1)
            sy, cy = item_read(("y", 3, 1))
            act.wait_ge(sy, cy)
            for t in range(NT):
                nc.scalar.activation(part(0, D), Y[:, t, :], ACT.Square, accum_out=SS[:, t:t + 1]).then_inc(s["y_sums"], 1)
                act.wait_ge(s["y_sums"], t + 1)
            act.wait_ge(s["y_ss"], 1)
            nc.scalar.activation(SS2[:, 0:4], SS[:, 0:4], ACT.Sqrt).then_inc(s["y_root"], 1)

        @block.vector
        def _(dve):
            order = [0]

            def link(ins):
                order[0] += 1
                ins.then_inc(s["dve_order"], 1)
                dve.wait_ge(s["dve_order"], order[0])

            def mark(ins, name, count):
                ins.then_inc(s[name], 1)
                dve.wait_ge(s[name], count)

            v = nc.vector
            link(v.memset(ONES, 1.0))
            dve.wait_ge(s["cols_in"], 16)
            lbc = col("lb").rearrange("p (d i h) -> p d i h", d=2, i=2)
            LE = LBE.rearrange("p (d i h) -> p d i h", d=2, i=2)
            LBMv = LBM.rearrange("p (d h) -> p d h", d=2)
            LBs = LB1.rearrange("p (d i h) -> p d i h", d=2, i=2)
            link(v.tensor_tensor(LBMv, lbc[:, :, 0, :], lbc[:, :, 1, :], ALU.max))
            for i in range(2):
                ins = v.tensor_tensor(LE[:, :, i, :], lbc[:, :, i, :], LBMv, ALU.subtract)
                link(ins) if i == 0 else mark(ins, "lb_diff", 1)
            dve.wait_ge(s["lb_exp"], 1)
            link(v.tensor_tensor(LBMv, LE[:, :, 0, :], LE[:, :, 1, :], ALU.add))
            link(v.reciprocal(LBM[:, :], LBM[:, :]))
            for i in range(2):
                link(v.tensor_tensor(LBs[:, :, i, :], LE[:, :, i, :], LBMv, ALU.mult))
            dve.wait_ge(s["sums_ready"], NT + NC_)
            mark(v.tensor_scalar(SS[:, 0:6], SS[:, 0:6], 1.0 / D, EPS, ALU.mult, ALU.add), "mean_ready", 1)
            dve.wait_ge(s["root_ready"], 1)
            link(v.reciprocal(SS2[:, 0:6], SS2[:, 0:6]))
            for t in range(NT):
                mark(v.tensor_scalar(XN[:, t, :], X[:, t, :], SS2[:, t:t + 1], None, ALU.mult), "xn_ready", t + 1)
            for t in range(NC_):
                mark(v.tensor_scalar(XCN[:, t, :], XC[:, t, :], SS2[:, NT + t:NT + t + 1], None, ALU.mult),
                     "xn_ready", NT + t + 1)
            for n in range(U_ADAC):
                item_full(dve, ("ada", n))
                sk, ck = item_read(("ada", n))
                v.tensor_copy(ADA[:, 4 * n:4 * n + 4], bank_of(("ada", n))[:, 0:4]).then_inc(s_dve, 1)
                dve.wait_ge(sk, ck)
            b = ADA.rearrange("p (m v) -> p m v", v=2)
            for w in range(2):
                link(v.tensor_tensor(SH[:, w, :], b[:, 0:KD, w], col("bsh1"), ALU.add))
                link(v.tensor_tensor(SC[:, w, :], b[:, KD:2 * KD, w], col("bsc1"), ALU.add))
                ins = v.scalar_tensor_tensor(out=SC[:, w, :], in0=SC[:, w, :], scalar=1.0, in1=col("gpre"),
                                             op0=ALU.add, op1=ALU.mult)
                mark(ins, "ada_ready", w + 1)
            for w, kind, dst, width in ((0, "xT", HT, TOK), (1, "cT", HC, CTX)):
                for k in range(1, KD, 2):
                    item_full(dve, (kind, k))
                    v.tensor_scalar(dst[:, k, :], bank_of((kind, k))[:, 0:width], SC[:, w, k:k + 1],
                                    SH[:, w, k:k + 1], ALU.mult, ALU.add).then_inc(s_dve, 1)

            def forget(d):
                sa, ca = item_read(("fc", d, 3))
                dve.wait_ge(sa, ca)
                for h in range(4):
                    link(v.tensor_scalar(LF[:, h, :], LF[:, h, :], LBs[:, d, 1, h:h + 1], LBs[:, d, 0, h:h + 1],
                                         ALU.mult, ALU.add))
                for h in range(4):
                    ins = v.tensor_scalar(KK[:, h, :], KK[:, h, :], LBs[:, d, 1, h:h + 1], None, ALU.mult)
                    link(ins) if h < 3 else mark(ins, "f_ready", d + 1)

            def recur(n):
                d, i, t = STEPS[n]
                lat = t >= NC_
                step = 4 * d + i - 2
                if i == 0:
                    dve.wait_ge(s["logf_ready"], 4 * (d + 1))
                for h in range(4):
                    o_, i_ = BB[:, h, :], LF[:, h, t * P:(t + 1) * P]
                    if d:
                        o_, i_ = o_[:, ::-1], i_[:, ::-1]
                    ins = v.tensor_tensor_scan(o_, ONES, i_, 0.0, ALU.mult, ALU.add)
                    link(ins) if h < 3 else mark(ins, "b_ready", n + 1)
                if lat:
                    b32 = BB.rearrange("p h (j u) -> p (h j) u", u=SUB)
                    q32 = QD.rearrange("p h (j u) -> p (h j) u", u=SUB)
                    mid = SUB // 2 - 1 if d == 0 else SUB // 2
                    mark(v.tensor_tensor(q32, b32, b32[:, :, mid:mid + 1].to_broadcast([P, 4 * NS, SUB]), ALU.subtract),
                         "qmid_ready", step + 1)

                    def kmid(j):
                        lo, hi = (0, SUB * (j + 1)) if d == 0 else (SUB * j, P)
                        at = SUB * j + mid
                        if NS * step + j >= 2:
                            dve.wait_ge(s["a_done"], NS * step + j - 1)
                        mark(v.tensor_tensor(KM[j % 2][:, :, lo:hi], BB[:, :, at:at + 1].to_broadcast([P, 4, hi - lo]),
                                             BB[:, :, lo:hi], ALU.subtract), "kmid_ready", NS * step + j + 1)

                    kmid(0)
                    kmid(1)
                    qs = qT[:, :, (t - NC_) * P:(t - NC_ + 1) * P]
                    dve.wait_ge(s["e_q"], step + 1)
                    link(v.tensor_tensor(QD, QD, qs, ALU.mult))
                    mark(v.tensor_tensor(QE, QE, qs, ALU.mult), "q_ready", step + 1)
                dve.wait_ge(s["e_end"], n + 1)
                mark(v.tensor_tensor(EK, EK, KK[:, :, t * P:(t + 1) * P], ALU.mult), "kend_ready", n + 1)
                if lat:
                    for j in range(2, NS):
                        kmid(j)
                    dve.wait_ge(s["a_done"], NS * (step + 1))
                    if step:
                        dve.wait_ge(s["o_done"], step)
                    if i == 2:
                        link(v.memset(AT, 0.0))
                    mask = grid(con("maskf" if d == 0 else "maskb").bitcast(U32), 4)
                    mark(v.copy_predicated(AT, mask, grid(banks[4][:, :], 4)), "at_ready", step + 1)
                    dve.wait_ge(s["o_done"], step + 1)
                    if d == 1:
                        mark(v.tensor_tensor(O[:, t - NC_, :], O[:, t - NC_, :], banks[5][:, :], ALU.add),
                             "o_added", i - 1)
                dve.wait_ge(s["su_done"], n + 1)
                su = grid(banks[7][:, :], 4)
                if i == 0:
                    mark(v.tensor_copy(S, su), "state_ready", n + 1)
                else:
                    for h in range(4):
                        ins = v.scalar_tensor_tensor(out=S[:, h, :], in0=S[:, h, :], scalar=DEC[:, h:h + 1],
                                                     in1=su[:, h, :], op0=ALU.mult, op1=ALU.add)
                        link(ins) if h < 3 else mark(ins, "state_ready", n + 1)

            forget(0)
            for c in range(2):
                for tp in range(3):
                    item_full(dve, ("v", c, tp))
                    at = 2 + 2 * tp if tp < 2 else 0
                    v.tensor_copy(V[:, at:at + 2, 256 * c:256 * (c + 1)],
                                  grid(bank_of(("v", c, tp))[:, :], 2)).then_inc(s_dve, 1)
            dve.wait_ge(s["const_in"], 16)
            link(v.memset(KM[0], 0.0))
            link(v.memset(KM[1], 0.0))
            for n in range(6):
                recur(n)
            sa, ca = item_read(("cv", 1, 1))
            dve.wait_ge(sa, ca)
            for t in range(NT):
                link(v.bn_stats(ST[:, 6 * t:6 * t + 6], CV[:, t, :]))
                link(v.bn_aggr(MV[:, 2 * t:2 * t + 2], ST[:, 6 * t:6 * t + 6]))
            mark(v.tensor_scalar(RS[:, :], grid(MV[:, :], 4)[:, :, 1], EPS, None, ALU.add), "ln_var", 1)
            dve.wait_ge(s["ln_root"], 1)
            link(v.reciprocal(RS[:, :], RS[:, :]))
            dve.wait_ge(s["lnrow_in"], 32)
            for t in range(NT):
                link(v.tensor_scalar(CV[:, t, :], CV[:, t, :], MV[:, 2 * t:2 * t + 1], RS[:, t:t + 1],
                                     ALU.subtract, ALU.mult))
                link(v.tensor_tensor(CV[:, t, :], CV[:, t, :], LNG, ALU.mult))
                mark(v.tensor_tensor(CV[:, t, :], CV[:, t, :], LNB, ALU.add), "ln_ready", t + 1)
            forget(1)
            item_full(dve, ("fc", 1, 3))
            mark(v.tensor_copy(CSB, CSC[:, :, 0:1].to_broadcast([P, KD, P])), "csb_ready", 1)
            dve.wait_ge(s["adarow_in"], 16)

            def fill(key):
                item_full(dve, key)
                b = bank_of(key)
                sk, ck = item_read(key)
                if key[0] == "row":
                    r, j = key[1:]
                    dst = ROW[:, r, 512 * j:512 * (j + 1)]
                    v.tensor_tensor(dst, dst, b[:, :], ALU.add).then_inc(s_dve, 1)
                else:
                    g = key[1]
                    v.tensor_tensor(TMP, grid(b[:, :], 4),
                                    BS[:, g:g + 1, :].to_broadcast([P, 4, P]), ALU.add).then_inc(s_dve, 1)
                    dve.wait_ge(sk, ck)
                    mark(v.tensor_tensor(UT[:, g, :], UT[:, g, :], TMP.rearrange("p a b -> p (a b)"), ALU.mult),
                         "bm_ready", g + 1)
                dve.wait_ge(sk, ck)

            TMP = grid(mem["X"][:, 2560:3072], 4)
            for n in range(6, 12):
                recur(n)
                fill(FILL1[2 * (n - 6)])
                fill(FILL1[2 * (n - 6) + 1])
            for t in range(NT):
                link(v.tensor_tensor(BB.rearrange("p a b -> p (a b)"), O[:, t, :], O[:, t, :], ALU.mult))
                link(v.tensor_reduce(SS[:, 4 * t:4 * t + 4], BB, AX, ALU.add))
            mark(v.tensor_scalar(SS[:, :], SS[:, :], 1.0 / P, EPS, ALU.mult, ALU.add), "o_sq", 1)
            dve.wait_ge(s["o_root"], 1)
            link(v.reciprocal(SS2[:, :], SS2[:, :]))
            for t in range(NT):
                o = grid(O[:, t, :], 4)
                r4 = SS2[:, 4 * t:4 * t + 4].rearrange("p (h a) -> p h a", a=1)
                link(v.tensor_tensor(o, o, r4.to_broadcast([P, 4, P]), ALU.mult))
                link(v.tensor_tensor(o, o, GH.rearrange("p (a b) -> p a b", a=1).to_broadcast([P, 4, P]), ALU.mult))
                mark(v.tensor_tensor(O[:, t, :], O[:, t, :], G[:, t, :], ALU.mult), "a_ready", t + 1)
            for j in range(2):
                for w, (kind, gate) in enumerate((("A", "ga"), ("B", "gb"))):
                    for mm in range(4):
                        key = (kind, 4 * j + mm)
                        sk, ck = item_read((gate, 4 * j + mm))
                        dve.wait_ge(sk, ck)
                        item_full(dve, key)
                        sk, ck = item_read(key)
                        dst = yT[:, 4 * j + mm, :] if w == 0 else SG[:, mm, :]
                        v.tensor_tensor(dst, SG[:, mm, :], bank_of(key)[:, :], ALU.mult).then_inc(s_dve, 1)
                        dve.wait_ge(sk, ck)
                        if w == 1:
                            mark(v.tensor_tensor(yT[:, 4 * j + mm, :], yT[:, 4 * j + mm, :], SG[:, mm, :], ALU.add),
                                 "summed", 4 * j + mm + 1)
            dve.wait_ge(s["gain_in"], 16)
            link(v.tensor_tensor(ROW[:, 0, :], ROW[:, 0, :], GAIN[:, 0:D], ALU.mult))
            link(v.scalar_tensor_tensor(out=ROW[:, 2, :], in0=ROW[:, 2, :], scalar=1.0, in1=GAIN[:, D:2 * D],
                                        op0=ALU.add, op1=ALU.mult))
            link(v.tensor_tensor(ROW[:, 3, :], ROW[:, 3, :], GAIN[:, 2 * D:3 * D], ALU.mult))
            sy, cy = item_read(("y", 3, 1))
            dve.wait_ge(sy, cy)
            dve.wait_ge(s["y_sums"], NT)
            mark(v.tensor_scalar(SS[:, 0:4], SS[:, 0:4], 1.0 / D, EPS, ALU.mult, ALU.add), "y_ss", 1)
            dve.wait_ge(s["y_root"], 1)
            link(v.reciprocal(SS2[:, 0:4], SS2[:, 0:4]))
            dve.wait_ge(s["x_again"], 16 * NT)
            for t in range(NT):
                link(v.scalar_tensor_tensor(out=Y[:, t, :], in0=Y[:, t, :], scalar=SS2[:, t:t + 1], in1=ROW[:, 0, :],
                                            op0=ALU.mult, op1=ALU.mult))
                mark(v.tensor_tensor(X[:, t, :], X[:, t, :], Y[:, t, :], ALU.add), "mixed", t + 1)

        @block.tensor
        def _(pe):
            mm = nc.tensor.matmul
            ring = mem["ring"]

            def unit(n):
                return ring[:, (n % RING) * UNIT:(n % RING + 1) * UNIT]

            def features(n, key, half, src, lo, width):
                bank_free(pe, key)
                w = unit(n).rearrange("p (k c) -> p k c", k=KD)
                for k in range(KD):
                    last = mm(bank_of(key)[:, 0:width], w[:, k, half * P:(half + 1) * P], src[:, k, lo:lo + width],
                              start=(k == 0), stop=(k == KD - 1))
                last.then_inc(s_full, 1)

            def tokens(n, key, tp, src):
                bank_free(pe, key)
                w = unit(n).rearrange("p (k c) -> p k c", k=KD)
                for a in range(2):
                    for k in range(KD):
                        last = mm(bank_of(key)[:, 256 * a:256 * (a + 1)], src[:, k, (2 * tp + a) * P:(2 * tp + a + 1) * P],
                                  w[:, k, :], start=(k == 0), stop=(k == KD - 1))
                last.then_inc(s_full, 1)

            def full(key):
                return bank_of(key)

            pe.wait_ge(s["silu_c"], 1)
            for n in range(U_ADAC):
                unit_ready(pe, s_unit, n)
                bank_free(pe, ("ada", n))
                w = unit(n).rearrange("p (k c) -> p k c", k=KD)
                for a in range(2):
                    for k in range(KD):
                        last = mm(full(("ada", n))[:, 2 * a:2 * a + 2], w[:, k, a * P:(a + 1) * P], CSC[:, k, :],
                                  start=(k == 0), stop=(k == KD - 1))
                last.then_inc(s_full, 1)
            pe.wait_ge(s["const_in"], 16)
            for kind, src, tiles, first in (("xT", XN, NT, 0), ("cT", XCN, NC_, NT)):
                pe.wait_ge(s["xn_ready"], first + tiles)
                for k in range(KD):
                    bank_free(pe, (kind, k))
                    for t in range(tiles):
                        last = nc.tensor.transpose(full((kind, k))[:, t * P:(t + 1) * P], src[:, t, k * P:(k + 1) * P],
                                                   ident)
                    last.then_inc(s_full, 1)
            for key in (("xT", 6), ("xT", 7), ("cT", 6), ("cT", 7)):
                pe.wait_ge(*item_read(key))
            for h in range(4):
                n = unit0["q"] + h // 2
                unit_ready(pe, s_unit, n)
                features(n, ("q", h), h % 2, HT, 0, TOK)

            def forget_logits(d):
                for h in range(4):
                    n = unit0[f"f{d}"] + h // 2
                    unit_ready(pe, s_unit, n)
                    features(n, ("f", d, h), h % 2, HT, 0, TOK)
                    features(n, ("fc", d, h), h % 2, HC, 0, CTX)

            def fill(key):
                kind = key[0]
                if kind == "u":
                    n = unit0["u"] + key[1] // 2
                    unit_ready(pe, s_unit, n)
                    features(n, key, key[1] % 2, HT, 0, TOK)
                elif kind in ("g", "cv"):
                    n = unit0[kind] + key[1]
                    unit_ready(pe, s_unit, n)
                    tokens(n, key, key[2], HT)
                elif kind == "row":
                    pe.wait_ge(s["csb_ready"], 1)
                    bank_free(pe, key)
                    for a in range(2):
                        n = unit0["row"] + 4 * key[1] + 2 * key[2] + a
                        unit_ready(pe, s_unit, n)
                        w = unit(n).rearrange("p (k c) -> p k c", k=KD)
                        for k in range(KD):
                            last = mm(full(key)[:, 256 * a:256 * (a + 1)], CSB[:, k, :], w[:, k, :],
                                      start=(k == 0), stop=(k == KD - 1))
                    last.then_inc(s_full, 1)
                else:
                    g = key[1]
                    pe.wait_ge(s["ln_ready"], NT)
                    pe.wait_ge(s["ws_in"], 16)
                    bank_free(pe, key)
                    for t in range(NT):
                        last = mm(full(key)[:, t * P:(t + 1) * P], CV[:, t, g * P:(g + 1) * P], WS[:, g, :],
                                  start=True, stop=True)
                    last.then_inc(s_full, 1)

            def recur(n, filler):
                d, i, t = STEPS[n]
                lat = t >= NC_
                step = 4 * d + i - 2
                if lat:
                    pe.wait_ge(s["q_ready"], step + 1)
                    for j in range(NS):
                        pe.wait_ge(s["k_ready"], NS * step + j + 1)
                        if j == 0 and step:
                            pe.wait_ge(s["at_ready"], step)
                        for h in range(4):
                            last = mm(grid(banks[4][:, :], 4)[:, h, SUB * j:SUB * (j + 1)], KM[j % 2][:, h, :],
                                      QD[:, h, SUB * j:SUB * (j + 1)], start=True, stop=True)
                        last.then_inc(s["a_done"], 1)
                pe.wait_ge(s["kend_ready"], n + 1)
                if n:
                    pe.wait_ge(s["kt_copied"], n)
                for h in range(4):
                    last = nc.tensor.transpose(grid(banks[6][:, :], 4)[:, h, :], EK[:, h, :], ident)
                last.then_inc(s["kt_done"], 1)
                fill(filler[0])
                pe.wait_ge(s["kt_copied"], n + 1)
                if n:
                    pe.wait_ge(s["state_ready"], n)
                for h in range(4):
                    last = mm(grid(banks[7][:, :], 4)[:, h, :], KTs[:, h, :], V[:, t, h * P:(h + 1) * P],
                              start=True, stop=True)
                last.then_inc(s["su_done"], 1)
                if lat:
                    pe.wait_ge(s["at_ready"], step + 1)
                    if 0 < step <= 4:
                        pe.wait_ge(s["o_copied"], step)
                    elif step:
                        pe.wait_ge(s["o_added"], step - 4)
                    for h in range(4):
                        o = grid(banks[5][:, :], 4)[:, h, :]
                        mm(o, AT[:, h, :], V[:, t, h * P:(h + 1) * P], start=True, stop=False)
                        last = mm(o, QE[:, h, :], S[:, h, :], start=False, stop=True)
                    last.then_inc(s["o_done"], 1)
                fill(filler[1])

            forget_logits(0)
            for c in range(2):
                unit_ready(pe, s_unit, unit0["v"] + c)
                for tp in range(3):
                    tokens(unit0["v"] + c, ("v", c, tp), tp if tp < 2 else 0, HT if tp < 2 else HC)
            pe.wait_ge(*item_read(("v", 1, 2)))
            for n in range(6):
                recur(n, FILL0[2 * n:2 * n + 2])
            forget_logits(1)
            for n in range(6, 12):
                recur(n, FILL1[2 * (n - 6):2 * (n - 6) + 2])
            pe.wait_ge(s["a_ready"], NT)
            for h in range(4):
                bank_free(pe, ("aT", h))
                for t in range(NT):
                    last = nc.tensor.transpose(full(("aT", h))[:, t * P:(t + 1) * P], O[:, t, h * P:(h + 1) * P], ident)
                last.then_inc(s_full, 1)
            for j in range(2):
                for kind, src in (("ga", HT), ("A", aT), ("gb", HT), ("B", UT)):
                    for q in range(4):
                        key = (kind, 4 * j + q)
                        if kind in ("ga", "gb"):
                            n = unit0[f"{kind}{j}"] + q // 2
                            unit_ready(pe, s_unit, n)
                            features(n, key, q % 2, HT, 0, TOK)
                            continue
                        n = unit0[f"{kind}{j}"]
                        unit_ready(pe, s_unit, n)
                        if kind == "A":
                            pe.wait_ge(*item_read(("aT", 3)))
                        else:
                            pe.wait_ge(s["bm_ready"], 4)
                        bank_free(pe, key)
                        w = unit(n).rearrange("p (k c) -> p k c", k=4)
                        for k in range(4):
                            last = mm(full(key)[:, :], w[:, k, q * P:(q + 1) * P], src[:, k, :],
                                      start=(k == 0), stop=(k == 3))
                        last.then_inc(s_full, 1)
            pe.wait_ge(s["summed"], KD)
            for c in range(4):
                unit_ready(pe, s_unit, unit0["y"] + c)
                for tp in range(2):
                    tokens(unit0["y"] + c, ("y", c, tp), tp, yT)


def moe(nc, sem, banks, mem, dram, s_unit, stream, experts, rows, w_router):
    W = mem["work"]

    def part(first, width):
        assert first + width <= WORK
        return W[:, first:first + width]

    def grid(a, outer):
        return a.rearrange("p (a b) -> p a b", a=outer)

    X = grid(mem["X"][:, :], NT)
    HT = grid(mem["HT"][:, :], KD)
    ROW = grid(mem["adarow"][:, :], 4)
    ident, before, slots = (mem["const1"][:, C1[n][0]:C1[n][0] + P] for n in ("ident", "before", "slots"))
    tok = mem["const1"][:, C1["tok"][0]:C1["tok"][0] + 4]
    SLOT = 6144
    wslot = [part(0, SLOT), part(SLOT, SLOT), mem["ring"][:, 0:SLOT], mem["ring"][:, SLOT:2 * SLOT]]
    at = [2 * SLOT]

    def take(width):
        at[0] += width
        return part(at[0] - width, width)

    F = grid(take(4096), NT)
    H2 = grid(take(4096), NT)
    base = at[0] - 4096
    JUNK = take(1024)
    SHT = grid(JUNK, 2)
    WR = grid(take(512), KD)
    ONES = take(P)
    XG = [part(base, D), part(base + 1024, D)] + [mem["adarow"][:, D * j:D * (j + 1)] for j in (1, 2)]
    XGT = [grid(part(base + 2048, D), KD), grid(part(base + 3072, D), KD)]
    OVER = take(2 * D)
    OUT = [JUNK, OVER[:, 0:D]]
    PM = take(4 * 68).rearrange("p (t e) -> p t e", t=4)
    R = take(4 * 68 * 3).rearrange("p (t e c) -> p t e c", t=4, c=3)
    CNT = take(NE).bitcast(I32)
    ONEHOT = [grid(OVER[:, D + 512 * i:D + 512 * (i + 1)], 4) for i in range(2)]
    SG, HID, HDT = take(256), take(256), [grid(take(256), 2) for _ in range(2)]
    TOKI, ROWI = take(4).bitcast(I32), take(4).bitcast(I32)
    ROWA, WCA = take(68).bitcast(I32), take(68)
    WC, OFF, SS, SS2, RSW, T8 = take(4), take(2), take(4), take(4), take(4), take(4)
    over = [0]

    def take_over(width):
        over[0] += width
        return OVER[:, over[0] - width:over[0]]

    SCO, SEL, SELM, REP2, MSK, CUM = (grid(take_over(256), 4) for _ in range(6))
    BR = take_over(NE)
    MX = take_over(256).rearrange("p (t g k) -> p t g k", t=4, g=NGRP)
    GSC, VG, REP, GM, V8 = (grid(take_over(w), 4) for w in (48, 32, 48, 32, 32))
    assert over[0] <= 2 * D
    EX = mem["HT"]
    XGX, XGTX, OUTX = EX[:, 0:1024], grid(EX[:, 1024:2048], KD), EX[:, 2048:3072]
    ONEHOTX, HIDX = grid(EX[:, 3072:3584], 4), EX[:, 3584:3840]
    EXR = mem["adarow"]
    SGX, HDTX = EXR[:, 0:256], grid(EXR[:, 256:512], 2)
    IDXX, WCX = EXR[:, 512:514].bitcast(I32), EXR[:, 514:515]
    JUNK2 = EX[:, 0:1024]
    names = ("row_in", "wr_in", "h2_sums", "h2_mean", "h2_root", "h2_ready", "h2_stored", "ht_full", "ht_act", "ht_dve",
             "logits_done", "scores_ready", "mask_ready", "ranks_done", "tables_ready", "cnt_ready",
             "sh_full", "sh_act", "sh_dve", "f_full", "f_copied", "dve_order",
             "onehot", "idx_done", "idx_ready", "placed", "t_done", "xgt_act", "xgt_dve", "gu_done", "sg_ready", "hid_ready",
             "ht2_done", "hdt_ready", "dn_done", "out_act", "out_dve",
             "x_p", "x_idx", "x_idxr", "x_gath", "x_t", "x_e", "x_gu", "x_sg", "x_hid", "x_ht", "x_he", "x_dn", "x_o",
             "x_sc", "acc_ready", "f_sums", "f_mean", "f_root", "done", "zeroed", "copies")
    s = {n: sem("moe_" + n) for n in names}
    s_exp = [sem(f"expert_arrived{k}") for k in range(4)]
    s_gath = [sem(f"gathered{k}") for k in range(4)]
    s_scat = [sem(f"scattered{k}") for k in range(2)]
    s_back = [sem(f"slots_back{k}") for k in range(2)]
    LOADU = [n for n in range(U_MIX, U_MIX + U_SHARED)]
    OUTB = [grid(part(0, 8192), 8), grid(part(2 * SLOT + 4096, 8192), 8)]

    def after(eng, name, i, o, c, k=1):
        value = k * o + c + (4 * k) * i
        if not isinstance(value, int) or value > 0:
            eng.wait_ge(s[name], value)

    def passed(eng, pair, i, o):
        value = 16 * (o // 2 + 1) + 32 * i
        if not isinstance(value, int) or value > 0:
            eng.wait_ge(pair[o % 2], value)

    def index(i, o):
        return bass.ds(4 * i + o, 1)

    def over_experts(eng, body):
        for u in range(4):
            body(0, u)
        with eng.Fori(1, NE // 4) as i:
            for u in range(4):
                body(i, u)

    def more_blocks(eng, i, u, done, body):
        count = eng.value_load(CNT[0:1, index(i, u)])

        def block_of(b):
            with eng.If(count > P * b):
                n = eng.snap(done)
                body(b, n)
                eng.reg_add(done, done, 1)
                if b < 3:
                    block_of(b + 1)

        block_of(1)

    with nc.Block() as block:

        @block.sync
        def _(sp):
            a = ROWS["b_router"][0]
            sp.dma_start(BR, rows[0:1, a:a + NE].to_broadcast([P, NE])).then_inc(s["row_in"], 16)
            sp.dma_start(WR.rearrange("p k c -> p (k c)"), w_router).then_inc(s["wr_in"], 16)
            for n in LOADU:
                sp.dma_start(mem["ring"][:, (n % RING) * UNIT:(n % RING + 1) * UNIT], stream[n]).then_inc(
                    s_unit[n % RING], 16)
            for e in range(2):
                sp.dma_start(wslot[e], experts[e]).then_inc(s_exp[e], 16)
            for t in range(NT):
                sp.wait_ge(s["h2_ready"], t + 1)
                sp.dma_start(dram["xn"][t * P:(t + 1) * P, :], H2[:, t, :]).then_inc(s["h2_stored"], 16)
            sp.wait_ge(s["f_full"], 8)
            for e in (2, 3):
                sp.dma_start(wslot[e], experts[e]).then_inc(s_exp[e], 16)
            with sp.Fori(1, NE // 4) as i:
                for u in range(4):
                    sp.wait_ge(s["dn_done"], 4 * i + (u - 3))
                    sp.dma_start(wslot[u], experts[index(i, u)].rearrange("a p c -> (a p) c")).then_inc(s_exp[u], 16)
            sp.wait_ge(s["dn_done"], NE)
            for n in range(FIRST2, FIRST2 + RING):
                sp.dma_start(mem["ring"][:, (n % RING) * UNIT:(n % RING + 1) * UNIT], stream[n]).then_inc(
                    s_unit[n % RING], 16)
            sp.wait_ge(s_scat[0], 16 * NE // 2)
            sp.wait_ge(s_scat[1], 16 * NE // 2)
            for k in range(4):
                sp.wait_ge(s_gath[k], 16 * (NE // 4 + (k < 3)))
            sp.wait_ge(s["xgt_act"], NE + 1)
            sp.wait_ge(s["xgt_dve"], NE + 1)
            sp.wait_ge(s["idx_done"], NE + 3)
            sp.wait_ge(s["out_act"], NE)
            for t in range(NT):
                if t >= 2:
                    sp.wait_ge(s["acc_ready"], t - 1)
                sp.dma_start(OUTB[t % 2].rearrange("p j d -> p (j d)"),
                             dram["slots"][t * P * TOPK:(t + 1) * P * TOPK, :].rearrange("(p j) d -> p (j d)", j=TOPK)
                             ).then_inc(s_back[t % 2], 16)

        @block.gpsimd
        def _(pool):
            done = pool.alloc_register("further_blocks_pool")
            pool.reg_mov(done, 0)

            def count_copy():
                pool.sem_inc(s["copies"], 1)

            pool.wait_ge(s["h2_stored"], 16 * NT)
            pool.wait_ge(s["cnt_ready"], 1)

            def gather(i, o):
                after(pool, "idx_ready", i, o, 1)
                after(pool, "t_done", i, o - 4, 1)
                count_copy()
                nc.gpsimd.indirect_dma_start(
                    out=XG[o % 4], out_offset=None, in_=dram["xn"][:, :],
                    in_offset=bass.IndirectOffsetOnAxis(ap=TOKI[:, o % 4:o % 4 + 1].bitcast(U32), axis=0),
                    bounds_check=TOK - 1, oob_is_err=False).then_inc(s_gath[o % 4], 16)

            def scatter(i, o):
                after(pool, "out_act", i, o, 1)
                after(pool, "out_dve", i, o, 1)
                count_copy()
                nc.gpsimd.indirect_dma_start(
                    out=dram["slots"][:, :],
                    out_offset=bass.IndirectOffsetOnAxis(ap=ROWI[:, o % 4:o % 4 + 1].bitcast(U32), axis=0),
                    in_=OUT[o % 2], in_offset=None, bounds_check=TOK * TOPK - 1, oob_is_err=False
                    ).then_inc(s_scat[o % 2], 16)

            def further(b, n):
                pool.wait_ge(s["x_idxr"], n + 1)
                count_copy()
                nc.gpsimd.indirect_dma_start(
                    out=XGX, out_offset=None, in_=dram["xn"][:, :],
                    in_offset=bass.IndirectOffsetOnAxis(ap=IDXX[:, 0:1].bitcast(U32), axis=0),
                    bounds_check=TOK - 1, oob_is_err=False).then_inc(s["x_gath"], 16)
                pool.wait_ge(s["x_o"], 2 * n + 2)
                count_copy()
                nc.gpsimd.indirect_dma_start(
                    out=dram["slots"][:, :],
                    out_offset=bass.IndirectOffsetOnAxis(ap=IDXX[:, 1:2].bitcast(U32), axis=0),
                    in_=OUTX, in_offset=None, bounds_check=TOK * TOPK - 1, oob_is_err=False
                    ).then_inc(s["x_sc"], 16)
                pool.wait_ge(s["x_sc"], 16 * n + 16)

            def body(i, u):
                gather(i, u + 3)
                if u or not isinstance(i, int):
                    scatter(i, u - 1)
                more_blocks(pool, i, u, done, further)

            pool.wait_ge(s["zeroed"], 1)
            gather(0, 0)
            gather(0, 1)
            gather(0, 2)
            over_experts(pool, body)
            scatter(NE // 4, -1)
            pool.wait_ge(s_scat[0], 16 * NE // 2)
            pool.wait_ge(s_scat[1], 16 * NE // 2)
            for k in range(4):
                pool.wait_ge(s_gath[k], 16 * (NE // 4 + (k < 3)))

        @block.scalar
        def _(act):
            done = act.alloc_register("further_blocks_act")
            act.reg_mov(done, 0)
            for t in range(NT):
                nc.scalar.activation(JUNK, X[:, t, :], ACT.Square, accum_out=SS[:, t:t + 1]).then_inc(s["h2_sums"], 1)
                act.wait_ge(s["h2_sums"], t + 1)
            act.wait_ge(s["h2_mean"], 1)
            nc.scalar.activation(SS2[:, :], SS[:, :], ACT.Sqrt).then_inc(s["h2_root"], 1)
            for k in range(0, KD, 2):
                act.wait_ge(s["ht_full"], k + 1)
                nc.scalar.activation(HT[:, k, :], banks[k % 4][:, :], ACT.Copy).then_inc(s["ht_act"], 1)
            act.wait_ge(s["logits_done"], 1)
            nc.scalar.activation(SCO.rearrange("p t e -> p (t e)"), banks[4][:, 0:256], ACT.Sigmoid).then_inc(
                s["scores_ready"], 1)
            for m in range(2):
                act.wait_ge(s["sh_full"], m + 1)
                nc.scalar.activation(SHT[:, m, :], banks[m][:, :], ACT.Silu).then_inc(s["sh_act"], 1)

            def copy_xgt(i, o):
                after(act, "t_done", i, o, 1)
                after(act, "gu_done", i, o - 2, 1)
                nc.scalar.activation(XGT[o % 2][:, 0:4, :], grid(banks[0][:, :], 4), ACT.Copy).then_inc(s["xgt_act"], 1)

            def silu(i, o):
                after(act, "gu_done", i, o, 1)
                after(act, "hid_ready", i, o - 1, 1)
                nc.scalar.activation(SG, banks[2][:, 0:256], ACT.Silu).then_inc(s["sg_ready"], 1)

            def scaled_out(i, o):
                after(act, "dn_done", i, o, 1)
                after(act, "placed", i, o, 1)
                passed(act, s_scat, i, o - 2)
                nc.scalar.activation(OUT[o % 2][:, 0:512], banks[4][:, :], ACT.Copy,
                                     scale=WC[:, o % 4:o % 4 + 1]).then_inc(s["out_act"], 1)

            def copy_hdt(i, o):
                after(act, "ht2_done", i, o, 1)
                after(act, "dn_done", i, o - 2, 1)
                nc.scalar.activation(HDT[o % 2], grid(banks[3][:, 0:256], 2), ACT.Copy).then_inc(s["hdt_ready"], 1)

            def further(b, n):
                for h in range(2):
                    act.wait_ge(s["x_t"], 2 * n + h + 1)
                    nc.scalar.activation(XGTX[:, 4 * h:4 * h + 4, :], grid(banks[7][:, :], 4), ACT.Copy).then_inc(
                        s["x_e"], 1)
                act.wait_ge(s["x_gu"], n + 1)
                nc.scalar.activation(SGX, banks[7][:, 0:256], ACT.Silu).then_inc(s["x_sg"], 1)
                act.wait_ge(s["x_ht"], n + 1)
                nc.scalar.activation(HDTX, grid(banks[7][:, 0:256], 2), ACT.Copy).then_inc(s["x_he"], 1)
                for j in range(2):
                    act.wait_ge(s["x_dn"], 2 * n + j + 1)
                    nc.scalar.activation(OUTX[:, 512 * j:512 * (j + 1)], banks[7][:, :], ACT.Copy,
                                         scale=WCX[:, 0:1]).then_inc(s["x_o"], 1)

            def body(i, u):
                silu(i, u)
                copy_xgt(i, u + 1)
                if u or not isinstance(i, int):
                    scaled_out(i, u - 1)
                copy_hdt(i, u)
                more_blocks(act, i, u, done, further)

            act.wait_ge(s["cnt_ready"], 1)
            copy_xgt(0, 0)
            over_experts(act, body)
            scaled_out(NE // 4, -1)
            for t in range(NT):
                act.wait_ge(s["acc_ready"], t + 1)
                nc.scalar.activation(JUNK2, F[:, t, :], ACT.Square, accum_out=SS[:, t:t + 1]).then_inc(s["f_sums"], 1)
                act.wait_ge(s["f_sums"], t + 1)
            act.wait_ge(s["f_mean"], 1)
            nc.scalar.activation(SS2[:, :], SS[:, :], ACT.Sqrt).then_inc(s["f_root"], 1)

        @block.vector
        def _(dve):
            v = nc.vector
            order = [0]
            done = dve.alloc_register("further_blocks_dve")
            dve.reg_mov(done, 0)

            def link(ins):
                order[0] += 1
                ins.then_inc(s["dve_order"], 1)
                dve.wait_ge(s["dve_order"], order[0])

            def mark(ins, name, count):
                ins.then_inc(s[name], 1)
                dve.wait_ge(s[name], count)

            link(v.memset(ONES, 1.0))
            dve.wait_ge(s["h2_sums"], NT)
            mark(v.tensor_scalar(SS[:, :], SS[:, :], 1.0 / D, EPS, ALU.mult, ALU.add), "h2_mean", 1)
            dve.wait_ge(s["h2_root"], 1)
            link(v.reciprocal(SS2[:, :], SS2[:, :]))
            for t in range(NT):
                link(v.scalar_tensor_tensor(out=H2[:, t, :], in0=X[:, t, :], scalar=SS2[:, t:t + 1], in1=ROW[:, 2, :],
                                            op0=ALU.mult, op1=ALU.mult))
                mark(v.tensor_tensor(H2[:, t, :], H2[:, t, :], ROW[:, 1, :], ALU.add), "h2_ready", t + 1)
            for k in range(1, KD, 2):
                dve.wait_ge(s["ht_full"], k + 1)
                v.tensor_copy(HT[:, k, :], banks[k % 4][:, :]).then_inc(s["ht_dve"], 1)
            dve.wait_ge(s["row_in"], 16)
            dve.wait_ge(s["scores_ready"], 1)
            link(v.tensor_tensor(SEL, SCO, BR.rearrange("p (a e) -> p a e", a=1).to_broadcast([P, 4, NE]), ALU.add))
            for t in range(NT):
                for g in range(NGRP):
                    last = v.max(MX[:, t, g, :], SEL[:, t, 8 * g:8 * g + 8])
            link(last)
            for j in range(4):
                last = v.memset(GSC[:, :, 8 + j:9 + j], NEG * (j + 1))
            link(last)
            link(v.tensor_tensor(GSC[:, :, 0:8], MX[:, :, :, 0], MX[:, :, :, 1], ALU.add))
            for t in range(NT):
                last = v.max(VG[:, t, :], GSC[:, t, 0:8])
            link(last)
            link(v.tensor_copy(VG[:, :, 4:8], GSC[:, :, 8:12]))
            for t in range(NT):
                last = v.match_replace(out=REP[:, t, :], in_to_replace=VG[:, t, :], in_values=GSC[:, t, :],
                                       imm_value=200 * NEG)
            link(last)
            link(v.tensor_tensor(GM, REP[:, :, 0:8], GSC[:, :, 0:8], ALU.not_equal))
            link(v.memset(SELM, NEG))
            link(v.copy_predicated(
                SELM.rearrange("p t (g k) -> p (t g) k", k=8),
                GM.bitcast(U32).rearrange("p t (g a) -> p (t g) a", a=1).to_broadcast([P, 32, 8]),
                SEL.rearrange("p t (g k) -> p (t g) k", k=8)))
            for t in range(NT):
                last = v.max(V8[:, t, :], SELM[:, t, :])
            link(last)
            for t in range(NT):
                last = v.match_replace(out=REP2[:, t, :], in_to_replace=V8[:, t, :], in_values=SELM[:, t, :],
                                       imm_value=200 * NEG)
            link(last)
            mark(v.tensor_tensor(MSK, REP2, SELM, ALU.not_equal), "mask_ready", 1)
            link(v.tensor_tensor(SEL, SCO, MSK, ALU.mult))
            link(v.tensor_reduce(RSW[:, :], SEL, AX, ALU.add))
            link(v.reciprocal(RSW[:, :], RSW[:, :]))
            link(v.memset(R.rearrange("p t e c -> p (t e c)"), 0.0))
            link(v.memset(PM.rearrange("p t e -> p (t e)"), -1.0))
            for t in range(NT):
                last = v.tensor_scalar(R[:, t, 0:NE, 2], SEL[:, t, :], RSW[:, t:t + 1], 2.5, ALU.mult, ALU.mult)
            link(last)
            link(v.tensor_scalar(T8[:, :], tok, float(TOPK), float(-1 - TOK * TOPK), ALU.mult, ALU.add))
            for t in range(NT):
                last = v.tensor_tensor_scan(CUM[:, t, :], ONES[:, 0:NE], MSK[:, t, :], 0.0, ALU.mult, ALU.add)
            link(last)
            for t in range(NT):
                v.tensor_scalar(R[:, t, 0:NE, 1], CUM[:, t, :], T8[:, t:t + 1], None, ALU.add)
                last = v.tensor_scalar(R[:, t, 0:NE, 0], tok[:, t:t + 1].to_broadcast([P, NE]), float(-TOK), None,
                                       ALU.add)
            link(last)
            link(v.memset(OFF[:, 0:1], float(TOK)))
            link(v.memset(OFF[:, 1:2], float(TOK * TOPK)))
            dve.wait_ge(s["ranks_done"], 1)
            link(v.scalar_tensor_tensor(out=PM[:, :, 0:NE], in0=grid(banks[5][:, 0:256], 4), scalar=1.0, in1=MSK,
                                        op0=ALU.add, op1=ALU.mult))
            mark(v.tensor_scalar(PM[:, :, 0:NE], PM[:, :, 0:NE], -1.0, None, ALU.add), "tables_ready", 1)
            mark(v.tensor_copy(CNT, banks[6][:, 0:NE]), "cnt_ready", 1)
            for m in range(2):
                dve.wait_ge(s["sh_act"], m + 1)
                dve.wait_ge(s["sh_full"], m + 3)
                mark(v.tensor_tensor(SHT[:, m, :], SHT[:, m, :], banks[2 + m][:, :], ALU.mult), "sh_dve", m + 1)
            for t in range(NT):
                for j in range(2):
                    n = 2 * t + j
                    dve.wait_ge(s["f_full"], n + 1)
                    mark(v.tensor_copy(F[:, t, 512 * j:512 * (j + 1)], banks[n % 4][:, :]), "f_copied", n + 1)
            dve.wait_ge(s["h2_stored"], 16 * NT)
            link(v.memset(XG[0], 0.0))
            for k in range(1, 4):
                link(v.memset(XG[k], 0.0))
            mark(v.memset(XGX, 0.0), "zeroed", 1)

            def onehot(i, o):
                after(dve, "idx_done", i, o - 2, 1)
                for t in range(NT):
                    last = v.tensor_scalar(ONEHOT[o % 2][:, t, :], slots, PM[:, t, index(i, o)], None, ALU.is_equal)
                last.then_inc(s["onehot"], 1)

            def indices(i, o):
                after(dve, "idx_done", i, o, 1)
                if o >= 4 or not isinstance(i, int):
                    dve.wait_ge(s_gath[o % 4], 16 * (o // 4) + 16 * i)
                v.tensor_copy(WCA[:, index(i, o)], banks[6][:, 2:3])
                v.tensor_tensor(ROWA[:, index(i, o)], banks[6][:, 1:2], OFF[:, 1:2], ALU.add)
                v.tensor_tensor(TOKI[:, o % 4:o % 4 + 1], banks[6][:, 0:1], OFF[:, 0:1], ALU.add).then_inc(
                    s["idx_ready"], 1)

            def place(i, o):
                after(dve, "idx_ready", i, o, 1)
                after(dve, "out_act", i, o - 4, 1)
                passed(dve, s_scat, i, o - 4)
                v.tensor_copy(WC[:, o % 4:o % 4 + 1], WCA[:, index(i, o)])
                v.tensor_copy(ROWI[:, o % 4:o % 4 + 1], ROWA[:, index(i, o)]).then_inc(s["placed"], 1)

            def copy_xgt(i, o):
                after(dve, "t_done", i, o, 1)
                after(dve, "gu_done", i, o - 2, 1)
                v.tensor_copy(XGT[o % 2][:, 4:8, :], grid(banks[1][:, :], 4)).then_inc(s["xgt_dve"], 1)

            def hidden(i, o):
                after(dve, "sg_ready", i, o, 1)
                after(dve, "ht2_done", i, o - 1, 1)
                v.tensor_tensor(HID, SG, banks[2][:, 256:512], ALU.mult).then_inc(s["hid_ready"], 1)

            def scaled_out(i, o):
                place(i, o)
                after(dve, "placed", i, o, 1)
                after(dve, "dn_done", i, o, 1)
                passed(dve, s_scat, i, o - 2)
                v.tensor_scalar(OUT[o % 2][:, 512:1024], banks[5][:, :], WC[:, o % 4:o % 4 + 1], None,
                                ALU.mult).then_inc(s["out_dve"], 1)

            def further(b, n):
                e = further_of[0]
                for t in range(NT):
                    last = v.tensor_scalar(ONEHOTX[:, t, :], slots, float(P * b), PM[:, t, e], ALU.add, ALU.is_equal)
                last.then_inc(s["x_p"], 1)
                dve.wait_ge(s["x_idx"], n + 1)
                v.tensor_copy(WCX, banks[7][:, 2:3])
                v.tensor_tensor(IDXX, banks[7][:, 0:2], OFF[:, :], ALU.add).then_inc(s["x_idxr"], 1)
                dve.wait_ge(s["x_sg"], n + 1)
                v.tensor_tensor(HIDX, SGX, banks[7][:, 256:512], ALU.mult).then_inc(s["x_hid"], 1)
                dve.wait_ge(s["x_sc"], 16 * n + 16)

            further_of = [None]

            def body(i, u):
                hidden(i, u)
                copy_xgt(i, u + 1)
                indices(i, u + 3)
                onehot(i, u + 4)
                if u or not isinstance(i, int):
                    scaled_out(i, u - 1)
                further_of[0] = index(i, u)
                more_blocks(dve, i, u, done, further)

            onehot(0, 0)
            onehot(0, 1)
            indices(0, 0)
            onehot(0, 2)
            indices(0, 1)
            onehot(0, 3)
            indices(0, 2)
            copy_xgt(0, 0)
            over_experts(dve, body)
            scaled_out(NE // 4, -1)
            for t in range(NT):
                dve.wait_ge(s_back[t % 2], 16 * (t // 2 + 1))
                b = OUTB[t % 2]
                for j in range(TOPK):
                    ins = v.tensor_tensor(F[:, t, :], F[:, t, :], b[:, j, :], ALU.add)
                    link(ins) if j < TOPK - 1 else mark(ins, "acc_ready", t + 1)
            dve.wait_ge(s["f_sums"], NT)
            mark(v.tensor_scalar(SS[:, :], SS[:, :], 1.0 / D, EPS, ALU.mult, ALU.add), "f_mean", 1)
            dve.wait_ge(s["f_root"], 1)
            link(v.reciprocal(SS2[:, :], SS2[:, :]))
            for t in range(NT):
                link(v.scalar_tensor_tensor(out=F[:, t, :], in0=F[:, t, :], scalar=SS2[:, t:t + 1], in1=ROW[:, 3, :],
                                            op0=ALU.mult, op1=ALU.mult))
                mark(v.tensor_tensor(X[:, t, :], X[:, t, :], F[:, t, :], ALU.add), "done", t + 1)

        @block.tensor
        def _(pe):
            mm = nc.tensor.matmul
            done = pe.alloc_register("further_blocks_pe")
            pe.reg_mov(done, 0)
            ring = mem["ring"]

            def unit(n):
                return ring[:, (n % RING) * UNIT:(n % RING + 1) * UNIT]

            pe.wait_ge(s["h2_ready"], NT)
            for k in range(KD):
                if k >= 4:
                    pe.wait_ge(s["ht_dve" if k % 2 else "ht_act"], (k - 4) // 2 + 1)
                for t in range(NT):
                    last = nc.tensor.transpose(banks[k % 4][:, t * P:(t + 1) * P], H2[:, t, k * P:(k + 1) * P], ident)
                last.then_inc(s["ht_full"], 1)
            pe.wait_ge(s["ht_act"], 4)
            pe.wait_ge(s["ht_dve"], 4)
            pe.wait_ge(s["wr_in"], 16)
            for t in range(NT):
                for k in range(KD):
                    last = mm(banks[4][:, NE * t:NE * (t + 1)], HT[:, k, t * P:(t + 1) * P], WR[:, k, :],
                              start=(k == 0), stop=(k == KD - 1))
            last.then_inc(s["logits_done"], 1)
            for m in range(4):
                n = LOADU[m // 2]
                unit_ready(pe, s_unit, n)
                w = unit(n).rearrange("p (k c) -> p k c", k=KD)
                for k in range(KD):
                    last = mm(banks[m][:, :], w[:, k, (m % 2) * P:(m % 2 + 1) * P], HT[:, k, :],
                              start=(k == 0), stop=(k == KD - 1))
                last.then_inc(s["sh_full"], 1)
            pe.wait_ge(s["mask_ready"], 1)
            for t in range(NT):
                o = banks[5][:, NE * t:NE * (t + 1)]
                mm(o, before, MSK[:, t, :], start=True, stop=(t == 0))
                for q in range(t):
                    mm(o, ONES, MSK[:, q, :], start=False, stop=(q == t - 1))
            for q in range(NT):
                last = mm(banks[6][:, 0:NE], ONES, MSK[:, q, :], start=(q == 0), stop=(q == NT - 1))
            last.then_inc(s["ranks_done"], 1)
            unit_ready(pe, s_unit, LOADU[2])
            pe.wait_ge(s["sh_dve"], 2)
            w = unit(LOADU[2]).rearrange("p (k c) -> p k c", k=2)
            for t in range(NT):
                for j in range(2):
                    n = 2 * t + j
                    if n >= 4:
                        pe.wait_ge(s["f_copied"], n - 3)
                    for k in range(2):
                        last = mm(banks[n % 4][:, :], SHT[:, k, t * P:(t + 1) * P], w[:, k, 512 * j:512 * (j + 1)],
                                  start=(k == 0), stop=(k == 1))
                    last.then_inc(s["f_full"], 1)

            def find(i, o):
                after(pe, "onehot", i, o, 1)
                after(pe, "idx_ready", i, o - 1, 1)
                for t in range(NT):
                    last = mm(banks[6][:, 0:3], ONEHOT[o % 2][:, t, :],
                              R[:, t, index(i, o), :].rearrange("p a c -> p (a c)"),
                              start=(t == 0), stop=(t == NT - 1))
                last.then_inc(s["idx_done"], 1)

            def turn(i, o):
                pe.wait_ge(s_gath[o % 4], 16 * (o // 4 + 1) + 16 * i)
                after(pe, "xgt_act", i, o - 1, 1)
                after(pe, "xgt_dve", i, o - 1, 1)
                for k in range(KD):
                    last = nc.tensor.transpose(banks[k // 4][:, (k % 4) * P:(k % 4 + 1) * P],
                                               XG[o % 4][:, k * P:(k + 1) * P], ident)
                last.then_inc(s["t_done"], 1)

            def gate_up(i, o):
                after(pe, "xgt_act", i, o, 1)
                after(pe, "xgt_dve", i, o, 1)
                after(pe, "hid_ready", i, o - 1, 1)
                pe.wait_ge(s_exp[o % 4], 16 * (o // 4 + 1) + 16 * i)
                w = wslot[o % 4][:, 0:4096].rearrange("p (k c) -> p k c", k=KD)
                for k in range(KD):
                    last = mm(banks[2][:, :], XGT[o % 2][:, k, :], w[:, k, :], start=(k == 0), stop=(k == KD - 1))
                last.then_inc(s["gu_done"], 1)

            def turn_hidden(i, o):
                after(pe, "hid_ready", i, o, 1)
                after(pe, "hdt_ready", i, o - 1, 1)
                for k in range(2):
                    last = nc.tensor.transpose(banks[3][:, k * P:(k + 1) * P], HID[:, k * P:(k + 1) * P], ident)
                last.then_inc(s["ht2_done"], 1)

            def down(i, o):
                after(pe, "hdt_ready", i, o, 1)
                after(pe, "out_act", i, o - 1, 1)
                after(pe, "out_dve", i, o - 1, 1)
                w = wslot[o % 4][:, 4096:6144].rearrange("p (k c) -> p k c", k=2)
                for j in range(2):
                    for k in range(2):
                        last = mm(banks[4 + j][:, :], HDT[o % 2][:, k, :], w[:, k, 512 * j:512 * (j + 1)],
                                  start=(k == 0), stop=(k == 1))
                last.then_inc(s["dn_done"], 1)

            def further(b, n):
                i, u = further_of[0]
                pe.wait_ge(s["x_p"], n + 1)
                for t in range(NT):
                    last = mm(banks[7][:, 0:3], ONEHOTX[:, t, :], R[:, t, index(i, u), :].rearrange("p a c -> p (a c)"),
                              start=(t == 0), stop=(t == NT - 1))
                last.then_inc(s["x_idx"], 1)
                pe.wait_ge(s["x_idxr"], n + 1)
                pe.wait_ge(s["x_gath"], 16 * n + 16)
                for h in range(2):
                    if h:
                        pe.wait_ge(s["x_e"], 2 * n + 1)
                    for k in range(4):
                        last = nc.tensor.transpose(banks[7][:, k * P:(k + 1) * P],
                                                   XGX[:, (4 * h + k) * P:(4 * h + k + 1) * P], ident)
                    last.then_inc(s["x_t"], 1)
                pe.wait_ge(s["x_e"], 2 * n + 2)
                w = wslot[u % 4][:, 0:4096].rearrange("p (k c) -> p k c", k=KD)
                for k in range(KD):
                    last = mm(banks[7][:, :], XGTX[:, k, :], w[:, k, :], start=(k == 0), stop=(k == KD - 1))
                last.then_inc(s["x_gu"], 1)
                pe.wait_ge(s["x_hid"], n + 1)
                for k in range(2):
                    last = nc.tensor.transpose(banks[7][:, k * P:(k + 1) * P], HIDX[:, k * P:(k + 1) * P], ident)
                last.then_inc(s["x_ht"], 1)
                pe.wait_ge(s["x_he"], n + 1)
                w = wslot[u % 4][:, 4096:6144].rearrange("p (k c) -> p k c", k=2)
                for j in range(2):
                    if j:
                        pe.wait_ge(s["x_o"], 2 * n + 1)
                    for k in range(2):
                        last = mm(banks[7][:, :], HDTX[:, k, :], w[:, k, 512 * j:512 * (j + 1)],
                                  start=(k == 0), stop=(k == 1))
                    last.then_inc(s["x_dn"], 1)
                pe.wait_ge(s["x_o"], 2 * n + 2)

            further_of = [None]

            def body(i, u):
                gate_up(i, u)
                turn(i, u + 1)
                find(i, u + 3)
                if u or not isinstance(i, int):
                    down(i, u - 1)
                turn_hidden(i, u)
                further_of[0] = (i, u)
                more_blocks(pe, i, u, done, further)

            pe.wait_ge(s["tables_ready"], 1)
            pe.wait_ge(s["cnt_ready"], 1)
            pe.wait_ge(s["f_copied"], 8)
            find(0, 0)
            find(0, 1)
            find(0, 2)
            turn(0, 0)
            over_experts(pe, body)
            down(NE // 4, -1)


UNITS2 = [("qa", 2), ("kv", 1), ("qr", 2), ("kr", 2), ("vr", 4), ("gr", 4),
          ("ga0", 2), ("YA0", 1), ("gb0", 2), ("YR0", 2), ("ga1", 2), ("YA1", 1), ("gb1", 2), ("YR1", 2),
          ("z", 4), ("ff1", 16), ("ff2", 16)]
FIRST2 = U_MIX + U_SHARED
HEADS, HDIM = 8, 64
RDK, RDV = 128, 256
FILL_ATT = [[("qr", c, tp) for c in range(2) for tp in range(2)], [("kr", c, tp) for c in range(2) for tp in range(2)],
            [("vr", c, tp) for c in range(2) for tp in range(2)], [("vr", c, tp) for c in range(2, 4) for tp in range(2)]]
FILL_RET = [[("gr", c, tp) for tp in range(2)] for c in range(4)]


def block2_items():
    it = Items()
    for k in range(KD):
        it.add(("xT", k), "dve" if k % 2 else "act")
    for c in range(2):
        for tp in range(2):
            it.add(("qa", c, tp), "act")
    for tp in range(2):
        it.add(("kv", 0, tp), "act")
    for p in range(4):
        it.add(("qaT", p), "dve")
    it.add(("kaT", 0), "dve")
    for n in range(NT):
        for key in FILL_ATT[n]:
            it.add(key, "act")
    for h in range(4):
        it.add(("qrT", h), "act")
    for h in range(4):
        it.add(("krT", h), "act")
    for n in range(NT):
        for key in FILL_RET[n]:
            it.add(key, "act")
    for k in range(KD):
        it.add(("rT", k), "dve" if k % 2 else "act")
    for j in range(2):
        for kind, by in (("ga", "act"), ("YA", "dve"), ("gb", "act"), ("YR", "dve")):
            for m in range(4):
                it.add((kind, 4 * j + m), by)
    for c in range(4):
        for tp in range(2):
            it.add(("z", c, tp), "dve")
    for k in range(KD):
        it.add(("mT", k), "dve" if k % 2 else "act")
    for m in range(32):
        it.add(("f1", m), "act")
    return it


def block2(nc, sem, banks, mem, s_unit, stream, rows, const2, out):
    W = mem["work"]

    def part(first, width):
        assert first + width <= WORK
        return W[:, first:first + width]

    def grid(a, outer):
        return a.rearrange("p (a b) -> p a b", a=outer)

    X = grid(mem["X"][:, :], NT)
    HT = grid(mem["HT"][:, :], KD)
    ident = mem["const1"][:, 0:P]
    QA, QR, KV, KR = (grid(part(a, w), NT) for a, w in ((0, 2048), (2048, 2048), (4096, 1024), (5120, 2048)))
    VR, GR = grid(part(7168, 4096), NT), grid(part(11264, 4096), NT)
    XN = grid(part(11264, 4096), NT)
    qaT, kaT = grid(part(15360, 2048), 4), part(17408, 512)
    qrT, krT, attT = (grid(part(a, 2048), 4) for a in (17920, 19968, 22016))
    T0 = 24064
    SCR = grid(part(T0, 2048), 8)
    PT = part(T0 + 2048, 512).rearrange("p (a b q) -> p a b q", a=2, b=2)
    STATE, AR, QD, RO = grid(part(T0, 1024), 4), grid(part(T0 + 1024, 512), 4), grid(part(T0 + 1536, 512), 4), grid(
        part(T0 + 2048, 512), 2)
    small = [T0 + 2560]

    def tiny(width):
        small[0] += width
        return part(small[0] - width, width)

    MX, NM, ES, DEN, SINK = (tiny(8) for _ in range(5))
    SS, SS2, RS = tiny(4), tiny(4), tiny(4)
    BST, MV = tiny(24), tiny(8)
    JUNK = part(0, D)
    yT, retT = grid(part(0, 4096), KD), grid(part(7168, 4096), KD)
    SG = grid(part(T0, 2048), 4)
    HDN = grid(part(0, 16384), 32)
    OUTT = [part(16384, D), part(16384 + D, D)]
    CONST, GAIN = mem["adarow"][:, 0:C2W], mem["adarow"][:, C2W:C2W + D]
    FINAL = part(18432, D)
    NORM = grid(part(0, 4096), NT)
    R1, R2 = mem["const1"][:, 256:768], mem["const1"][:, 768:1280]

    def col(name):
        a, w = PC[name]
        return mem["cols"][:, a:a + w]

    def con(name):
        a, w = C2[name]
        return CONST[:, a:a + w]

    it = block2_items()
    s_full, s_act, s_dve = sem("b2_full"), sem("b2_read_by_act"), sem("b2_read_by_dve")
    freed_by = {"act": s_act, "dve": s_dve}

    def bank_of(key):
        return banks[it.number[key] % NBANK]

    def bank_free(pe, key):
        n = it.number[key]
        if n >= NBANK:
            _, by, count = it.order[n - NBANK]
            pe.wait_ge(freed_by[by], count)

    def item_full(eng, key):
        eng.wait_ge(s_full, it.number[key] + 1)

    def item_read(key):
        _, by, count = it.order[it.number[key]]
        return freed_by[by], count

    names = ("const_in", "gain_in", "sink_in", "final_in", "sums", "mean", "root", "xn_ready", "rot_a", "rot_q", "rot_k",
             "sc_done", "sc_read", "nm_ready", "exp_done", "p_ready", "pt_done", "pt_read", "av_done", "av_read",
             "ar_done", "ar_ready", "qd_ready", "kd_ready", "ro_done", "ro_read", "su_done", "state_ready", "gn_var",
             "gn_root", "gated", "summed", "sq_ready", "f2_full", "added", "out_ready", "dve_order", "es_ready",
             "mlp_sums", "mlp_mean", "mlp_root", "mlp_ready", "fin_sums", "fin_mean", "fin_root", "z_done")
    s = {n: sem("b2_" + n) for n in names}
    s_out = [sem(f"out_rows_stored{k}") for k in range(2)]
    unit0, n0 = {}, FIRST2
    for name, width in UNITS2:
        unit0[name] = n0
        n0 += width
    LAST = n0
    uses = {}

    def use(name, keys):
        for i, key in enumerate(keys):
            uses[unit0[name] + i] = it.number[key] + 1

    for name, width in UNITS2[:6]:
        use(name, [(name, c, 1) for c in range(width)])
    for j in range(2):
        use(f"ga{j}", [("ga", 4 * j + 1), ("ga", 4 * j + 3)])
        use(f"YA{j}", [("YA", 4 * j + 3)])
        use(f"gb{j}", [("gb", 4 * j + 1), ("gb", 4 * j + 3)])
        use(f"YR{j}", [("YR", 4 * j + 1), ("YR", 4 * j + 3)])
    use("z", [("z", c, 1) for c in range(4)])
    use("ff1", [("f1", 2 * n + 1) for n in range(16)])

    with nc.Block() as block:

        @block.sync
        def _(sp):
            sp.dma_start(CONST, const2).then_inc(s["const_in"], 16)
            for name, dst in (("ret_gain", GAIN), ("sinks", SINK)):
                a, w = ROWS[name]
                sp.dma_start(dst, rows[0:1, a:a + w].to_broadcast([P, w])).then_inc(s["gain_in"], 16)
            for n in range(FIRST2 + RING, LAST):
                prev = n - RING
                if prev in uses:
                    sp.wait_ge(s_full, uses[prev])
                else:
                    q = prev - unit0["ff2"]
                    sp.wait_ge(s["f2_full"], q + 1)
                sp.dma_start(mem["ring"][:, (n % RING) * UNIT:(n % RING + 1) * UNIT], stream[n]).then_inc(
                    s_unit[n % RING], 16)
                if n == unit0["ff1"] + 6:
                    a, w = ROWS["norm_final"]
                    sp.dma_start(FINAL, rows[0:1, a:a + w].to_broadcast([P, w])).then_inc(s["final_in"], 16)
            for t in range(NT):
                sp.wait_ge(s["out_ready"], t + 1)
                sp.dma_start(out[t * P:(t + 1) * P, :], OUTT[t % 2]).then_inc(s_out[t % 2], 16)
            for k in range(2):
                sp.wait_ge(s_out[k], 16 * NT // 2)

        @block.scalar
        def _(act):
            for t in range(NT):
                nc.scalar.activation(JUNK, X[:, t, :], ACT.Square, accum_out=SS[:, t:t + 1]).then_inc(s["sums"], 1)
                act.wait_ge(s["sums"], t + 1)
            act.wait_ge(s["mean"], 1)
            nc.scalar.activation(SS2[:, :], SS[:, :], ACT.Sqrt).then_inc(s["root"], 1)

            def turned(kind, gain):
                for k in range(0, KD, 2):
                    item_full(act, (kind, k))
                    nc.scalar.activation(HT[:, k, :], bank_of((kind, k))[:, :], ACT.Copy,
                                         scale=gain[:, k:k + 1]).then_inc(s_act, 1)

            turned("xT", col("nmix"))

            def copy_out(key):
                kind, c, tp = key
                item_full(act, key)
                b = grid(bank_of(key)[:, :], 2)
                if kind == "qa":
                    for a in range(2):
                        dst = QA[:, 2 * tp + a, :].rearrange("p (a v d) -> p a v d", a=4, v=2)[:, :, c, :]
                        last = nc.scalar.activation(dst, b[:, a, :].rearrange("p (a d) -> p a d", a=4), ACT.Copy)
                else:
                    dst = {"kv": KV, "qr": QR, "kr": KR, "vr": VR, "gr": GR}[kind]
                    last = nc.scalar.activation(dst[:, 2 * tp:2 * tp + 2, 256 * c:256 * (c + 1)], b,
                                                ACT.Silu if kind == "gr" else ACT.Copy)
                last.then_inc(s_act, 1)

            for c in range(2):
                for tp in range(2):
                    copy_out(("qa", c, tp))
            for tp in range(2):
                copy_out(("kv", 0, tp))
            for n in range(NT):
                lo = P if n == 0 else 0
                act.wait_ge(s["nm_ready"], n + 1)
                for h in range(HEADS):
                    last = nc.scalar.activation(SCR[:, h, lo:256], SCR[:, h, lo:256], ACT.Exp, bias=NM[:, h:h + 1],
                                                accum_out=DEN[:, h:h + 1])
                last.then_inc(s["exp_done"], 1)
                nc.scalar.activation(ES[:, :], ES[:, :], ACT.Exp).then_inc(s["es_ready"], 1)
                for q in range(4):
                    act.wait_ge(s["pt_done"], 4 * n + q + 1)
                    if 4 * n + q:
                        act.wait_ge(s["av_done"], 4 * n + q)
                    b = banks[6][:, :].rearrange("p (a b q) -> p a b q", a=2, b=2)
                    b0 = 1 if n == 0 else 0
                    nc.scalar.activation(PT[:, :, b0:2, :], b[:, :, b0:2, :], ACT.Copy).then_inc(s["pt_read"], 1)
                act.wait_ge(s["av_done"], 4 * n + 4)
                nc.scalar.activation(attT[:, :, n * P:(n + 1) * P], grid(banks[7][:, :], 4), ACT.Copy).then_inc(
                    s["av_read"], 1)
                for key in FILL_ATT[n]:
                    copy_out(key)
            for kind, dst in (("qrT", qrT), ("krT", krT)):
                for h in range(4):
                    item_full(act, (kind, h))
                    nc.scalar.activation(dst[:, h, :], bank_of((kind, h))[:, :], ACT.Copy).then_inc(s_act, 1)
            for n in range(NT):
                for key in FILL_RET[n]:
                    copy_out(key)
                act.wait_ge(s["gn_var"], n + 1)
                nc.scalar.activation(RS[:, :], RS[:, :], ACT.Sqrt).then_inc(s["gn_root"], 1)
            for k in range(0, KD, 2):
                item_full(act, ("rT", k))
                nc.scalar.activation(retT[:, k, :], bank_of(("rT", k))[:, :], ACT.Copy).then_inc(s_act, 1)
            for j in range(2):
                for w, kind in enumerate(("ga", "gb")):
                    for q in range(4):
                        m = 4 * j + q
                        if w == 1:
                            act.wait_ge(*item_read(("YA", m)))
                        elif j == 1:
                            act.wait_ge(s["summed"], q + 1)
                        item_full(act, (kind, m))
                        nc.scalar.activation(SG[:, q, :], bank_of((kind, m))[:, :], ACT.Sigmoid,
                                             bias=col("bg")[:, 8 * w + m:8 * w + m + 1]).then_inc(s_act, 1)
            act.wait_ge(s["z_done"], 1)
            for t in range(NT):
                nc.scalar.activation(JUNK, X[:, t, :], ACT.Square, accum_out=SS[:, t:t + 1]).then_inc(s["mlp_sums"], 1)
                act.wait_ge(s["mlp_sums"], t + 1)
            act.wait_ge(s["mlp_mean"], 1)
            nc.scalar.activation(SS2[:, :], SS[:, :], ACT.Sqrt).then_inc(s["mlp_root"], 1)
            turned("mT", col("nmlp"))
            for m in range(32):
                item_full(act, ("f1", m))
                nc.scalar.activation(HDN[:, m, :], bank_of(("f1", m))[:, :], ACT.Relu).then_inc(s_act, 1)
            act.wait_ge(s["added"], 16)
            for t in range(NT):
                nc.scalar.activation(JUNK, X[:, t, :], ACT.Square, accum_out=SS[:, t:t + 1]).then_inc(s["fin_sums"], 1)
                act.wait_ge(s["fin_sums"], t + 1)
            act.wait_ge(s["fin_mean"], 1)
            nc.scalar.activation(SS2[:, :], SS[:, :], ACT.Sqrt).then_inc(s["fin_root"], 1)

        @block.vector
        def _(dve):
            v = nc.vector
            order = [0]

            def link(ins):
                order[0] += 1
                ins.then_inc(s["dve_order"], 1)
                dve.wait_ge(s["dve_order"], order[0])

            def mark(ins, name, count):
                ins.then_inc(s[name], 1)
                dve.wait_ge(s[name], count)

            def rstd(sums, mean, root):
                dve.wait_ge(s[sums], NT)
                mark(v.tensor_scalar(SS[:, :], SS[:, :], 1.0 / D, EPS, ALU.mult, ALU.add), mean, 1)
                dve.wait_ge(s[root], 1)
                link(v.reciprocal(SS2[:, :], SS2[:, :]))

            def turned(kind, gain):
                for k in range(1, KD, 2):
                    item_full(dve, (kind, k))
                    v.tensor_scalar(HT[:, k, :], bank_of((kind, k))[:, :], gain[:, k:k + 1], None, ALU.mult).then_inc(
                        s_dve, 1)

            rstd("sums", "mean", "root")
            for t in range(NT):
                mark(v.tensor_scalar(XN[:, t, :], X[:, t, :], SS2[:, t:t + 1], None, ALU.mult), "xn_ready", t + 1)
            turned("xT", col("nmix"))

            def rotate(x, cos, sin, name, count):
                nh, w = x.shape[1], x.shape[2] // 2
                x = x.rearrange("p n (s d) -> p n s d", s=2)
                a = R1[:, 0:nh * 2 * w].rearrange("p (n s d) -> p n s d", n=nh, s=2)
                b = R2[:, 0:nh * 2 * w].rearrange("p (n s d) -> p n s d", n=nh, s=2)
                for q in range(2):
                    c = cos.rearrange("p (a d) -> p a d", a=1).to_broadcast([P, nh, w])
                    n_ = sin.rearrange("p (a d) -> p a d", a=1).to_broadcast([P, nh, w])
                    v.tensor_tensor(a[:, :, q, :], x[:, :, q, :], c, ALU.mult)
                    last = v.tensor_tensor(b[:, :, q, :], x[:, :, 1 - q, :], n_, ALU.mult)
                link(last)
                link(v.tensor_tensor(x[:, :, 0, :], a[:, :, 0, :], b[:, :, 0, :], ALU.subtract))
                mark(v.tensor_tensor(x[:, :, 1, :], a[:, :, 1, :], b[:, :, 1, :], ALU.add), name, count)

            dve.wait_ge(s["const_in"], 16)
            dve.wait_ge(s["gain_in"], 32)
            dve.wait_ge(*item_read(("kv", 0, 1)))
            for t in range(NT):
                c8, s8 = grid(con("acos"), 4)[:, t, :], grid(con("asin"), 4)[:, t, :]
                rotate(grid(QA[:, t, :], HEADS)[:, :, 0:16], c8, s8, "rot_a", 2 * t + 1)
                rotate(grid(KV[:, t, 0:P], 2)[:, :, 0:16], c8, s8, "rot_a", 2 * t + 2)
            for p in range(4):
                item_full(dve, ("qaT", p))
                v.tensor_copy(qaT[:, p, :], bank_of(("qaT", p))[:, :]).then_inc(s_dve, 1)
            item_full(dve, ("kaT", 0))
            v.tensor_copy(kaT, bank_of(("kaT", 0))[:, :]).then_inc(s_dve, 1)
            win = con("win")
            for n in range(NT):
                lo = P if n == 0 else 0
                for q in range(4):
                    dve.wait_ge(s["sc_done"], 4 * n + q + 1)
                    if q == 0 and n:
                        dve.wait_ge(s["pt_done"], 4 * n)
                    b = grid(banks[4 + q % 2][:, :], 2)
                    mark(v.scalar_tensor_tensor(
                        out=SCR[:, 2 * q:2 * q + 2, lo:256], in0=b[:, :, lo:256], scalar=float(HDIM) ** -0.5,
                        in1=win[:, lo:256].rearrange("p (a k) -> p a k", a=1).to_broadcast([P, 2, 256 - lo]),
                        op0=ALU.mult, op1=ALU.add), "sc_read", 4 * n + q + 1)
                link(v.tensor_reduce(MX[:, :], SCR[:, :, lo:256], AX, ALU.max))
                link(v.tensor_tensor(MX[:, :], MX[:, :], SINK, ALU.max))
                link(v.tensor_scalar(NM[:, :], MX[:, :], -1.0, None, ALU.mult))
                mark(v.tensor_tensor(ES[:, :], SINK, NM[:, :], ALU.add), "nm_ready", n + 1)
                dve.wait_ge(s["es_ready"], n + 1)
                link(v.tensor_tensor(DEN[:, :], DEN[:, :], ES[:, :], ALU.add))
                link(v.reciprocal(DEN[:, :], DEN[:, :]))
                for h in range(HEADS):
                    ins = v.tensor_scalar(SCR[:, h, lo:256], SCR[:, h, lo:256], DEN[:, h:h + 1], None, ALU.mult)
                mark(ins, "p_ready", n + 1)
                if n >= 1:
                    dst, name = ((QR, "rot_q"), (KR, "rot_k"))[n - 1] if n < 3 else (None, None)
                    if dst is not None:
                        kind = "qr" if n == 1 else "kr"
                        dve.wait_ge(*item_read((kind, 1, 1)))
                        for t in range(NT):
                            c_, s_ = ("qcos", "qsin") if n == 1 else ("kcos", "ksin")
                            rotate(grid(dst[:, t, :], 4), grid(con(c_), 4)[:, t, :], grid(con(s_), 4)[:, t, :],
                                   name, t + 1)
            for t in range(NT):
                for h in range(HG):
                    if t == 0 and h == 0:
                        item_full(dve, ("krT", 3))
                    last = v.tensor_scalar(KR[:, t, h * P:(h + 1) * P], KR[:, t, h * P:(h + 1) * P],
                                           con("kdec")[:, h:h + 1], None, ALU.mult)
                mark(last, "kd_ready", t + 1)
            dve.wait_ge(*item_read(("qrT", 3)))
            for n in range(NT):
                if n:
                    dve.wait_ge(s["ro_done"], 2 * n)
                    mark(v.tensor_tensor(QD, qrT[:, :, n * P:(n + 1) * P], grid(con("qdec"), 4), ALU.mult), "qd_ready", n)
                else:
                    dve.wait_ge(s["av_done"], 16)
                dve.wait_ge(s["ar_done"], n + 1)
                mark(v.tensor_tensor(AR, grid(banks[4][:, :], 4), grid(con("intra"), 4), ALU.mult), "ar_ready", n + 1)
                if n < NT - 1:
                    for q in range(2):
                        dve.wait_ge(s["su_done"], 2 * n + q + 1)
                        b = grid(banks[7][:, :], 2)
                        if n == 0:
                            mark(v.tensor_copy(STATE[:, 2 * q:2 * q + 2, :], b), "state_ready", 2 * n + q + 1)
                        else:
                            if q == 0:
                                dve.wait_ge(s["ro_done"], 2 * n + 2)
                            for a in range(2):
                                h = 2 * q + a
                                last = v.scalar_tensor_tensor(
                                    out=STATE[:, h, :], in0=STATE[:, h, :], scalar=CHUNK_DECAY[h], in1=b[:, a, :],
                                    op0=ALU.mult, op1=ALU.add)
                            mark(last, "state_ready", 2 * n + q + 1)
                dve.wait_ge(s["ro_done"], 2 * n + 2)
                for h in range(HG):
                    src = banks[5 + h // 2][:, 256 * (h % 2):256 * (h % 2 + 1)]
                    link(v.bn_stats(BST[:, 6 * h:6 * h + 6], src))
                    link(v.bn_aggr(MV[:, 2 * h:2 * h + 2], BST[:, 6 * h:6 * h + 6]))
                mark(v.tensor_scalar(RS[:, :], grid(MV[:, :], 4)[:, :, 1], EPS, None, ALU.add), "gn_var", n + 1)
                dve.wait_ge(s["gn_root"], n + 1)
                link(v.reciprocal(RS[:, :], RS[:, :]))
                dve.wait_ge(*item_read(("gr", 3, 1)) if n == NT - 1 else item_read(("gr", n, 1)))
                for q in range(2):
                    for a in range(2):
                        h = 2 * q + a
                        ins = v.tensor_scalar(RO[:, a, :], banks[5 + q][:, 256 * a:256 * (a + 1)],
                                              MV[:, 2 * h:2 * h + 1], RS[:, h:h + 1], ALU.subtract, ALU.mult)
                        link(ins) if a == 0 else mark(ins, "ro_read", 2 * n + q + 1)
                    ro = RO.rearrange("p a b -> p (a b)")
                    mark(v.tensor_tensor(NORM[:, n, 512 * q:512 * (q + 1)], ro, GAIN[:, 512 * q:512 * (q + 1)], ALU.mult),
                         "gated", 2 * n + q + 1)
            dve.wait_ge(*item_read(("gr", 3, 1)))
            for t in range(NT):
                mark(v.tensor_tensor(GR[:, t, :], GR[:, t, :], NORM[:, t, :], ALU.mult), "gated", 2 * NT + t + 1)
            for k in range(1, KD, 2):
                item_full(dve, ("rT", k))
                v.tensor_copy(retT[:, k, :], bank_of(("rT", k))[:, :]).then_inc(s_dve, 1)
            for j in range(2):
                for w, (kind, gate) in enumerate((("YA", "ga"), ("YR", "gb"))):
                    for q in range(4):
                        m = 4 * j + q
                        dve.wait_ge(*item_read((gate, m)))
                        item_full(dve, (kind, m))
                        dst = yT[:, m, :] if w == 0 else SG[:, q, :]
                        v.tensor_tensor(dst, SG[:, q, :], bank_of((kind, m))[:, :], ALU.mult).then_inc(s_dve, 1)
                        dve.wait_ge(*item_read((kind, m)))
                        if w == 1:
                            mark(v.tensor_tensor(yT[:, m, :], yT[:, m, :], SG[:, q, :], ALU.add), "summed", m + 1)
            for c in range(4):
                for tp in range(2):
                    key = ("z", c, tp)
                    item_full(dve, key)
                    dst = X[:, 2 * tp:2 * tp + 2, 256 * c:256 * (c + 1)]
                    v.tensor_tensor(dst, dst, grid(bank_of(key)[:, :], 2), ALU.add).then_inc(s_dve, 1)
            dve.wait_ge(*item_read(("z", 3, 1)))
            mark(v.memset(SS2[:, :], 0.0), "z_done", 1)
            rstd("mlp_sums", "mlp_mean", "mlp_root")
            for t in range(NT):
                mark(v.tensor_scalar(XN[:, t, :], X[:, t, :], SS2[:, t:t + 1], None, ALU.mult), "mlp_ready", t + 1)
            turned("mT", col("nmlp"))
            for m in range(32):
                dve.wait_ge(*item_read(("f1", m)))
                v.tensor_tensor(HDN[:, m, :], HDN[:, m, :], HDN[:, m, :], ALU.mult).then_inc(s["sq_ready"], 1)
            for c in range(4):
                for t in range(NT):
                    if t == 0:
                        dve.wait_ge(s["f2_full"], 4 * (c + 1))
                    dst = X[:, t, 256 * c:256 * (c + 1)]
                    mark(v.tensor_tensor(dst, dst, banks[4 * (c % 2) + t][:, 0:256], ALU.add), "added", 4 * c + t + 1)
            rstd("fin_sums", "fin_mean", "fin_root")
            dve.wait_ge(s["final_in"], 16)
            for t in range(NT):
                if t >= 2:
                    dve.wait_ge(s_out[t % 2], 16 * (t // 2))
                mark(v.scalar_tensor_tensor(out=OUTT[t % 2], in0=X[:, t, :], scalar=SS2[:, t:t + 1], in1=FINAL,
                                            op0=ALU.mult, op1=ALU.mult), "out_ready", t + 1)

        @block.tensor
        def _(pe):
            mm = nc.tensor.matmul
            ring = mem["ring"]

            def unit(n, chunks):
                unit_ready(pe, s_unit, n)
                return ring[:, (n % RING) * UNIT:(n % RING + 1) * UNIT].rearrange("p (k c) -> p k c", k=chunks)

            def features(n, key, half, src):
                w = unit(n, KD)
                bank_free(pe, key)
                for k in range(KD):
                    last = mm(bank_of(key)[:, :], w[:, k, half * P:(half + 1) * P], src[:, k, :],
                              start=(k == 0), stop=(k == KD - 1))
                last.then_inc(s_full, 1)

            def tokens(n, key, tp, src):
                w = unit(n, KD)
                bank_free(pe, key)
                for a in range(2):
                    for k in range(KD):
                        last = mm(bank_of(key)[:, 256 * a:256 * (a + 1)], src[:, k, (2 * tp + a) * P:(2 * tp + a + 1) * P],
                                  w[:, k, :], start=(k == 0), stop=(k == KD - 1))
                last.then_inc(s_full, 1)

            def turn(key, blocks_):
                bank_free(pe, key)
                for t in range(NT):
                    last = nc.tensor.transpose(bank_of(key)[:, t * P:(t + 1) * P], blocks_(t), ident)
                last.then_inc(s_full, 1)

            def turned_in(kind):
                pe.wait_ge(*item_read((kind, 6)))
                pe.wait_ge(*item_read((kind, 7)))

            pe.wait_ge(s["xn_ready"], NT)
            for k in range(KD):
                turn(("xT", k), lambda t: XN[:, t, k * P:(k + 1) * P])
            turned_in("xT")
            for c in range(2):
                for tp in range(2):
                    tokens(unit0["qa"] + c, ("qa", c, tp), tp, HT)
            for tp in range(2):
                tokens(unit0["kv"], ("kv", 0, tp), tp, HT)
            pe.wait_ge(s["rot_a"], 2 * NT)
            for p in range(4):
                turn(("qaT", p), lambda t: QA[:, t, p * P:(p + 1) * P])
            turn(("kaT", 0), lambda t: KV[:, t, 0:P])
            pe.wait_ge(*item_read(("kaT", 0)))
            for n in range(NT):
                lo = P if n == 0 else 0
                for q in range(4):
                    if 4 * n + q >= 2:
                        pe.wait_ge(s["sc_read"], 4 * n + q - 1)
                    for a in range(2):
                        h = 2 * q + a
                        g, r0 = h % 4, HDIM * (h // 4)
                        last = mm(banks[4 + q % 2][:, 256 * a + lo:256 * (a + 1)],
                                  qaT[r0:r0 + HDIM, g, n * P:(n + 1) * P],
                                  kaT[r0:r0 + HDIM, (n - 1) * P + lo:(n + 1) * P], start=True, stop=True)
                    last.then_inc(s["sc_done"], 1)
                fill = FILL_ATT[n]
                tokens(unit0[fill[0][0]] + fill[0][1], fill[0], fill[0][2], HT)
                tokens(unit0[fill[1][0]] + fill[1][1], fill[1], fill[1][2], HT)
                pe.wait_ge(s["p_ready"], n + 1)
                for q in range(4):
                    if 4 * n + q:
                        pe.wait_ge(s["pt_read"], 4 * n + q)
                    for a in range(2):
                        for b in range(1 if n == 0 else 0, 2):
                            last = nc.tensor.transpose(banks[6][:, (2 * a + b) * P:(2 * a + b + 1) * P],
                                                       SCR[:, 2 * q + a, b * P:(b + 1) * P], ident)
                    last.then_inc(s["pt_done"], 1)
                    if q == 0 and n:
                        pe.wait_ge(s["av_read"], n)
                    pe.wait_ge(s["pt_read"], 4 * n + q + 1)
                    for a in range(2):
                        h = 2 * q + a
                        vcol = P + HDIM * (h // 4)
                        for b in range(1 if n == 0 else 0, 2):
                            last = mm(banks[7][HDIM * a:HDIM * (a + 1), q * P:(q + 1) * P],
                                      KV[:, n - 1 + b, vcol:vcol + HDIM], PT[:, a, b, :],
                                      start=(b == (1 if n == 0 else 0)), stop=(b == 1))
                    last.then_inc(s["av_done"], 1)
                for key in fill[2:]:
                    tokens(unit0[key[0]] + key[1], key, key[2], HT)
            pe.wait_ge(s["rot_q"], NT)
            for h in range(4):
                turn(("qrT", h), lambda t: QR[:, t, h * P:(h + 1) * P])
            pe.wait_ge(s["rot_k"], NT)
            for h in range(4):
                turn(("krT", h), lambda t: KR[:, t, h * P:(h + 1) * P])
            pe.wait_ge(*item_read(("krT", 3)))
            for n in range(NT):
                if n:
                    pe.wait_ge(s["ar_ready"], n)
                for h in range(HG):
                    last = mm(banks[4][:, h * P:(h + 1) * P], krT[:, h, n * P:(n + 1) * P], qrT[:, h, n * P:(n + 1) * P],
                              start=True, stop=True)
                last.then_inc(s["ar_done"], 1)
                tokens(unit0["gr"] + FILL_RET[n][0][1], FILL_RET[n][0], 0, HT)
                pe.wait_ge(s["ar_ready"], n + 1)
                if n:
                    pe.wait_ge(s["qd_ready"], n)
                    pe.wait_ge(s["state_ready"], 2 * n)
                for q in range(2):
                    if n:
                        pe.wait_ge(s["ro_read"], 2 * n - 1 + q)
                    for a in range(2):
                        h = 2 * q + a
                        o = banks[5 + q][:, 256 * a:256 * (a + 1)]
                        last = mm(o, AR[:, h, :], VR[:, n, RDV * h:RDV * (h + 1)], start=True, stop=(n == 0))
                        if n:
                            last = mm(o, QD[:, h, :], STATE[:, h, :], start=False, stop=True)
                    last.then_inc(s["ro_done"], 1)
                if n < NT - 1:
                    pe.wait_ge(s["kd_ready"], n + 1)
                    for q in range(2):
                        if 2 * n + q:
                            pe.wait_ge(s["state_ready"], 2 * n + q)
                        for a in range(2):
                            h = 2 * q + a
                            last = mm(banks[7][:, 256 * a:256 * (a + 1)], KR[:, n, h * P:(h + 1) * P],
                                      VR[:, n, RDV * h:RDV * (h + 1)], start=True, stop=True)
                        last.then_inc(s["su_done"], 1)
                tokens(unit0["gr"] + FILL_RET[n][1][1], FILL_RET[n][1], 1, HT)
            pe.wait_ge(s["gated"], 3 * NT)
            for k in range(KD):
                turn(("rT", k), lambda t: GR[:, t, k * P:(k + 1) * P])
            for j in range(2):
                for kind in ("ga", "YA", "gb", "YR"):
                    for q in range(4):
                        key = (kind, 4 * j + q)
                        if kind == "YA":
                            w = unit(unit0[f"YA{j}"], 4)
                            bank_free(pe, key)
                            for k in range(4):
                                last = mm(bank_of(key)[:, :], w[:, k, q * P:(q + 1) * P], attT[:, k, :],
                                          start=(k == 0), stop=(k == 3))
                            last.then_inc(s_full, 1)
                        else:
                            if key == ("YR", 0):
                                turned_in("rT")
                            features(unit0[f"{kind}{j}"] + q // 2, key, q % 2, retT if kind == "YR" else HT)
            pe.wait_ge(s["summed"], KD)
            for c in range(4):
                for tp in range(2):
                    tokens(unit0["z"] + c, ("z", c, tp), tp, yT)
            pe.wait_ge(s["mlp_ready"], NT)
            for k in range(KD):
                turn(("mT", k), lambda t: XN[:, t, k * P:(k + 1) * P])
            turned_in("mT")
            for m in range(32):
                features(unit0["ff1"] + m // 2, ("f1", m), m % 2, HT)
            pe.wait_ge(s["sq_ready"], 32)
            for c in range(4):
                for kk in range(4):
                    w = unit(unit0["ff2"] + 4 * c + kk, KD)
                    if kk == 0 and c >= 2:
                        pe.wait_ge(s["added"], 4 * (c - 1))
                    for t in range(NT):
                        for k in range(KD):
                            last = mm(banks[4 * (c % 2) + t][:, 0:256], HDN[:, KD * kk + k, t * P:(t + 1) * P], w[:, k, :],
                                      start=(kk == 0 and k == 0), stop=(kk == 3 and k == KD - 1))
                    last.then_inc(s["f2_full"], 1)


def _units(w):
    k, n = w.shape
    return w.reshape(k // P, P, n // 256, 256).transpose(2, 1, 0, 3).reshape(-1, P, UNIT)


def _half_units(w):
    k, n = w.shape
    return w.reshape(4, P, n // 512, 512).transpose(2, 1, 0, 3).reshape(-1, P, UNIT)


def _mixer_stream(i):
    w_in, w_ada = i["w_in"][0], i["w_ada"][0]
    cut = lambda a, b: _units(w_in[:, a:b])
    parts = [_units(w_ada[:, 0:2048]), cut(0, 512), cut(512, 1024), cut(1536, 2048), cut(2048, 2560),
             cut(2560, 3072), cut(3072, 3584), cut(1024, 1536), _units(w_ada[:, 2048:])]
    a, b = _half_units(i["w_branch_a"][0]), _half_units(i["w_branch_b"][0])
    for j in range(2):
        parts += [cut(3584 + 512 * j, 4096 + 512 * j), a[j:j + 1], cut(4608 + 512 * j, 5120 + 512 * j), b[j:j + 1]]
    parts.append(_units(i["w_out"][0]))
    parts.append(_units(i["w_shared_gu"][0]))
    parts.append(i["w_shared_down"][0].reshape(2, P, D).transpose(1, 0, 2).reshape(1, P, 2 * D))
    return parts


def _block2_stream(i):
    w = i["w_in_2"][0]
    edges = [0, 512, 768, 1280, 1792, 2816, 3840, 4352, 4864, 5376, 5888]
    qa, kv, qr, kr, vr, gr, ga0, ga1, gb0, gb1 = (_units(w[:, a:b]) for a, b in zip(edges, edges[1:]))
    ya, yr = _half_units(i["w_att_up_2"][0]), _units(i["w_ret_up_2"][0])
    parts = [qa, kv, qr, kr, vr, gr, ga0, ya[0:1], gb0, yr[0:2], ga1, ya[1:2], gb1, yr[2:4],
             _units(i["w_out_2"][0]), _units(i["w_ff1_2"][0])]
    ff2 = i["w_ff2_2"][0].reshape(4, KD, P, 4, 256)
    return parts + [ff2.transpose(3, 0, 2, 1, 4).reshape(16, P, UNIT)]


def _const2():
    f = np.float32
    pos = np.arange(TOK, dtype=f)

    def table(dim, theta):
        inv = np.power(f(theta), -np.arange(0, dim, 2, dtype=f) / f(dim)).astype(f)
        ang = pos[:, None] * inv[None, :]
        lay = lambda a: a.astype(f).reshape(NT, P, -1).transpose(1, 0, 2).reshape(P, -1)
        return lay(np.cos(ang)), lay(np.sin(ang))

    ac, as_ = table(16, 500000.0)
    rc, rs = table(RDK, 10000.0)
    lg = np.log1p(-np.exp2(f(-5.0) - np.arange(4, dtype=f))).astype(f)
    idx = np.arange(P, dtype=f)
    delta = idx[:, None] + P - np.arange(2 * P, dtype=f)[None, :]
    diff = idx[None, :] - idx[:, None]
    intra = np.where(diff[:, None, :] >= 0, np.exp(np.maximum(diff, 0)[:, None, :] * lg[None, :, None]), 0)
    parts = {
        "acos": ac, "asin": as_, "qcos": rc, "qsin": rs, "kcos": rc * f(RDK ** -0.5), "ksin": rs * f(RDK ** -0.5),
        "win": np.where((delta >= 0) & (delta < P), 0, NEG),
        "intra": intra.reshape(P, 4 * P),
        "qdec": np.tile(np.exp((idx + 1)[None, :] * lg[:, None]).reshape(1, 4 * P), (P, 1)),
        "kdec": np.exp((P - 1 - idx)[:, None] * lg[None, :]), "pad": np.zeros((P, 4)),
    }
    return np.concatenate([np.asarray(parts[k], np.float32) for k in C2], axis=1)


def _columns(v, n):
    return v.reshape(n, P).T


def _const1():
    p, q = np.arange(P)[:, None], np.arange(P)[None, :]
    maskf, maskb = (p <= q), (p >= q)
    parts = {
        "ident": p == q, "before": p < q, "maskf": np.tile(maskf, (1, 4)), "maskb": np.tile(maskb, (1, 4)),
        "slots": np.tile(q, (P, 1)), "part": p, "tok": p + P * np.arange(4)[None, :], "pad": np.zeros((P, 3)),
    }
    return np.concatenate([np.asarray(parts[k], np.float32) for k in C1], axis=1)


def _layout(i):
    f = lambda a: np.ascontiguousarray(a, dtype=np.float32)
    i = {k: np.asarray(v) for k, v in i.items()}
    lb = i["lb_logits"].reshape(2, 2, 4, P).transpose(3, 0, 1, 2).reshape(P, 16)
    b = i["b_ada"][0]
    cols = {"c": _columns(i["c"][0], KD), "cc": _columns(i["c_ctx"], KD), "gpre": _columns(i["g_pre_mix"][0], KD),
            "bsh1": _columns(b[0:D], KD), "bsc1": _columns(b[D:2 * D], KD), "lb": lb,
            "bg": _columns(i["b_gates_2"][0], 16), "nmix": _columns(i["norm_mix_gain_2"][0], KD),
            "nmlp": _columns(i["norm_mlp_gain_2"][0], KD)}
    rows = {"b_ada": b[2 * D:], "g_post_mix": i["g_post_mix"], "g_pre_ffn": i["g_pre_ffn"], "g_post_ffn": i["g_post_ffn"],
            "g_hgrn": i["g_hgrn_out"], "ln_g": i["cm_ln_g"], "ln_b": i["cm_ln_b"], "b_s": i["b_spatial"][0].T,
            "b_router": i["b_router"], "sinks": i["attn_sinks_2"], "ret_gain": i["ret_gn_gain_2"],
            "norm_final": i["norm_final_gain_2"]}
    return {
        "x": f(i["x"][0]), "ctx": f(i["ctx"][0]),
        "stream": f(np.concatenate(_mixer_stream(i) + _block2_stream(i))),
        "rows": f(np.concatenate([rows[k].reshape(-1) for k in ROWS])[None, :]),
        "cols": f(np.concatenate([cols[k] for k in PC], axis=1)),
        "const1": _const1(),
        "w_spatial": f(i["w_spatial"][0].transpose(2, 0, 1).reshape(P, 512)),
        "experts": f(np.concatenate([
            i["w_expert_gu"][0].reshape(NE, KD, P, 512).transpose(0, 2, 1, 3).reshape(NE, P, 4096),
            i["w_expert_down"][0].reshape(NE, 2, P, D).transpose(0, 2, 1, 3).reshape(NE, P, 2 * D)], axis=2)),
        "w_router": f(i["w_router"][0].reshape(KD, P, NE).transpose(1, 0, 2).reshape(P, KD * NE)),
        "const2": _const2(),
    }


def kernel(**inputs):
    import numpy as _np
    import concourse.bacc as _bacc
    from concourse import mybir as _mybir
    from concourse.bass_utils import run_bass_kernel_spmd as _run

    nc = _bacc.Bacc("TRN2", target_bir_lowering=False, num_devices=1)
    arrays, args = {}, []
    for name, a in _layout(inputs).items():
        arrays[f"in_{name}_dram"] = a
        args.append(nc.dram_tensor(f"in_{name}_dram", a.shape, _mybir.dt.from_np(a.dtype), kind="ExternalInput").ap())
    args.append(nc.dram_tensor("out_0_dram", (TOK, D), F32, kind="ExternalOutput").ap())
    program(nc, *args)
    r = _run(nc, [arrays], core_ids=[0])
    return r.results[0]["out_0_dram"].reshape(1, TOK, D)
```

```python
from contextlib import ExitStack

import numpy as np

import concourse.bass as bass
from concourse import mybir

ALU = mybir.AluOpType
ACT = mybir.ActivationFunctionType
F32 = mybir.dt.float32
F32R = mybir.dt.float32r
I32 = mybir.dt.int32
U32 = mybir.dt.uint32
AX = mybir.AxisListType.X

P = 128
TOK, CTX, D = 512, 256, 1024
KD = D // P
NT, NC_ = TOK // P, CTX // P
HG = 4
SUB = 16
NS = P // SUB
NE, TOPK, NGRP = 64, 8, 8
EPS = 1e-6
UNIT = 2048
RING = 6
NBANK = 4
NEG = -1.0e30
CHUNK_DECAY = [float(np.exp(np.float32(P) * np.log1p(-np.exp2(np.float32(-5.0 - h)))).astype(np.float32))
               for h in range(4)]
WORK, WORK_MOE = 26800, 23680

U_ADAC, U_Q, U_F0, U_V, U_G, U_U, U_CV, U_F1, U_ROW = 8, 2, 2, 2, 2, 2, 2, 2, 16
U_MIX = U_ADAC + U_Q + U_F0 + U_V + U_G + U_U + U_CV + U_F1 + U_ROW + 2 * 6 + 4
U_SHARED = 3

PC = {}
for _name, _w in (("c", KD), ("cc", KD), ("gpre", KD), ("bsh1", KD), ("bsc1", KD), ("lb", 16),
                  ("bg", 16), ("nmix", KD), ("nmlp", KD)):
    PC[_name] = (sum(w for _, w in PC.values()), _w)
PCW = sum(w for _, w in PC.values())

C1 = {}
for _name, _w in (("ident", P), ("before", P), ("maskf", 4 * P), ("maskb", 4 * P), ("slots", P), ("part", 1),
                  ("tok", 4), ("pad", 3)):
    C1[_name] = (sum(w for _, w in C1.values()), _w)
C1W = sum(w for _, w in C1.values())

C2 = {}
for _name, _w in (("acos", 4 * 8), ("asin", 4 * 8), ("qcos", 4 * 64), ("qsin", 4 * 64), ("kcos", 4 * 64),
                  ("ksin", 4 * 64), ("win", 256), ("intra", 4 * P), ("qdec", 4 * P), ("kdec", 4), ("pad", 4)):
    C2[_name] = (sum(w for _, w in C2.values()), _w)
C2W = sum(w for _, w in C2.values())

ROWS = {}
for _name, _w in (("b_ada", 4096), ("g_post_mix", D), ("g_pre_ffn", D), ("g_post_ffn", D), ("g_hgrn", P),
                  ("ln_g", 512), ("ln_b", 512), ("b_s", 512), ("b_router", NE), ("sinks", 8),
                  ("ret_gain", D), ("norm_final", D)):
    ROWS[_name] = (sum(w for _, w in ROWS.values()), _w)
ROWSW = sum(w for _, w in ROWS.values())


class Items:

    def __init__(self):
        self.order, self.number, self.freed = [], {}, {"act": 0, "dve": 0}

    def add(self, key, by):
        self.number[key] = len(self.order)
        self.freed[by] += 1
        self.order.append((key, by, self.freed[by]))


def mixer_items():
    it = Items()
    for n in range(U_ADAC):
        it.add(("ada", n), "dve")
    it.add(("adaT",), "dve")
    for k in range(KD):
        it.add(("xT", k), "dve" if k % 2 else "act")
    for k in range(KD):
        it.add(("cT", k), "dve" if k % 2 else "act")
    for m in range(4):
        it.add(("q", m), "act")
    for h in range(4):
        it.add(("f", 0, h), "act")
        it.add(("fc", 0, h), "act")
    for c in range(2):
        for tp in range(3):
            it.add(("v", c, tp), "dve")
    for c in range(2):
        for tp in range(2):
            it.add(("g", c, tp), "act")
    for m in range(4):
        it.add(("u", m), "act")
    for c in range(2):
        for tp in range(2):
            it.add(("cv", c, tp), "act")
    for h in range(4):
        it.add(("f", 1, h), "act")
        it.add(("fc", 1, h), "act")
    for r in range(4):
        for j in range(2):
            it.add(("row", r, j), "dve")
    for g in range(4):
        it.add(("sp", g), "dve")
    for m in range(4):
        it.add(("ga", m), "act")
    for h in range(4):
        it.add(("aT", h), "act")
    for j in range(2):
        for kind, by in (("ga", "act"), ("A", "dve"), ("gb", "act"), ("B", "dve")):
            for m in range(4):
                if (j, kind) != (0, "ga"):
                    it.add((kind, 4 * j + m), by)
    for tp in range(2):
        for c in range(4):
            it.add(("y", c, tp), "act")
    return it


FILL0 = [("g", c, tp) for c in range(2) for tp in range(2)] + [("u", m) for m in range(4)] + \
        [("cv", c, tp) for c in range(2) for tp in range(2)]
FILL1 = [("row", r, j) for r in range(4) for j in range(2)] + [("sp", g) for g in range(4)]
ORDER = ((0, 1, 2, 3, 4, 5), (1, 0, 5, 4, 3, 2))


def program(nc, x, ctx_in, stream, rows, cols, const1, w_spatial, experts, w_router, const2, out):
    with ExitStack() as es:
        def sb(name, width, dt=F32):
            return es.enter_context(nc.sbuf_tensor(name, [P, width], dt))

        banks = [es.enter_context(nc.psum_tensor(f"bank{i}", [P, 512], F32)) for i in range(8)]
        m = {
            "ring": sb("ring", RING * UNIT), "X": sb("X", NT * D), "cols": sb("cols", PCW), "const1": sb("const1", C1W),
            "sums": sb("sums", NT),
        }
        dram = {
            "xn": nc.dram_tensor("h2_rows", [TOK, D], F32),
            "acc": nc.dram_tensor("ffn_sums", [TOK, D], F32),
        }
        s_unit = [es.enter_context(nc.semaphore(f"unit_arrived{i}")) for i in range(RING)]
        taken = []

        def sem(name):
            taken.append(nc.alloc_semaphore(name=name))
            return taken[-1]

        def next_phase():
            nc.all_engine_barrier()
            nc.clear_and_free_semaphores(list(taken))
            taken.clear()
            nc.all_engine_barrier()

        with ExitStack() as early:
            for name, width in (("HT", KD * TOK), ("adarow", 4 * D)):
                m[name] = early.enter_context(nc.sbuf_tensor(name, [P, width], F32))

            def phase(name, width, build, *args):
                with ExitStack() as own:
                    m["work"] = own.enter_context(nc.sbuf_tensor(name, [P, width], F32))
                    m["float32r"] = lambda name, width: own.enter_context(nc.sbuf_tensor(name, [P, width], F32R))
                    build(nc, sem, banks, m, *args)
                    next_phase()

            phase("mixer_work", WORK, mixer, s_unit, x, ctx_in, stream, rows, cols, const1, w_spatial)
            phase("moe_work", WORK_MOE, moe, dram, s_unit, stream, experts, rows, w_router)
            phase("block2_work", WORK, block2, s_unit, stream, rows, const2)
        mlp(nc, sem, banks, m, s_unit, stream, rows, out)


def unit_in(sp, m, stream, s_unit, s_used, last_item, n):
    if n >= RING:
        sp.wait_ge(s_used, last_item(n - RING) + 1)
    s = n % RING
    sp.dma_start(m["ring"][:, s * UNIT:(s + 1) * UNIT], stream[n]).then_inc(s_unit[s], 16)


def unit_ready(eng, s_unit, n):
    eng.wait_ge(s_unit[n % RING], 16 * (n // RING + 1))


def mixer(nc, sem, banks, mem, s_unit, x, ctx_in, stream, rows, cols, const1, w_spatial):
    W = mem["work"]

    def part(first, width):
        assert first + width <= WORK
        return W[:, first:first + width]

    def grid(a, outer):
        return a.rearrange("p (a b) -> p a b", a=outer)

    X = grid(mem["X"][:, :], NT)
    HT = grid(mem["HT"][:, :], KD)
    XN, XC, XCN = grid(part(0, 4096), NT), grid(part(4096, 2048), NC_), grid(part(6144, 2048), NC_)
    JUNK = part(8192, 1024)
    qT, KK, LF = grid(part(0, 2048), 4), grid(part(2048, 3072), 4), grid(part(5120, 3072), 4)
    V, G = grid(part(8192, 3072), 6), grid(part(11264, 2048), 4)
    UT, CV, O = grid(part(13312, 2048), 4), grid(part(15360, 2048), 4), grid(part(17408, 2048), 4)
    HC = grid(part(19456, 2048), KD)
    ADAR = part(21504, 2048)
    CSB = grid(part(20480, 1024), KD)
    BB, EK, QE, QD, KTs, AT, S = (grid(part(21504 + 512 * i, 512), 4) for i in range(7))
    KM = [grid(part(25088 + 512 * i, 512), 4) for i in range(2)]
    ONES, small = part(26112, P), [26112 + P]

    def tiny(width):
        small[0] += width
        return part(small[0] - width, width)

    CSC = grid(tiny(2 * KD), KD)
    SH, SC = grid(tiny(2 * KD), 2), grid(tiny(2 * KD), 2)
    LBE, LB1, LBM = tiny(16), tiny(16), tiny(8)
    ADA = tiny(32)
    DEC, SS, SS2 = tiny(4), tiny(16), tiny(16)
    ST, MV, RS = tiny(24), tiny(8), tiny(4)
    aT, SG, yT = grid(part(0, 2048), 4), grid(part(2048, 2048), 4), grid(part(4096, 4096), KD)
    GAIN, Y = part(8192, 3072), grid(part(11264, 4096), NT)
    XS = mem["X"]
    LNG, LNB, BS, GH = XS[:, 0:512], XS[:, 512:1024], grid(XS[:, 1024:1536], 4), XS[:, 1536:1664]
    WS = grid(XS[:, 2048:2560], 4)
    ROW = grid(mem["adarow"][:, :], 4)

    def col(name):
        a, w = PC[name]
        return mem["cols"][:, a:a + w]

    def con(name):
        a, w = C1[name]
        return mem["const1"][:, a:a + w]

    ident = con("ident")
    it = mixer_items()
    s_full, s_act, s_dve = sem("bank_full"), sem("bank_read_by_act"), sem("bank_read_by_dve")
    freed_by = {"act": s_act, "dve": s_dve}

    def bank_of(key):
        return banks[it.number[key] % NBANK]

    def bank_free(pe, key):
        n = it.number[key]
        if n >= NBANK:
            _, by, count = it.order[n - NBANK]
            pe.wait_ge(freed_by[by], count)

    def item_full(eng, key):
        eng.wait_ge(s_full, it.number[key] + 1)

    def item_read(key):
        _, by, count = it.order[it.number[key]]
        return freed_by[by], count

    names = ("x_in", "ctx_in", "cols_in", "const_in", "lnrow_in", "adarow_in", "gain_in", "x_again", "ws_in",
             "silu_c", "sums_ready", "mean_ready", "root_ready", "xn_ready", "ada_ready", "csb_ready",
             "lb_diff", "lb_exp", "f_ready", "logf_ready",
             "b_ready", "qmid_ready", "kmid_ready", "q_ready", "kend_ready", "at_ready", "state_ready", "o_added",
             "e_end", "e_q", "e_k", "kt_copied", "o_copied", "k_ready", "kt_done", "a_done", "su_done", "o_done",
             "ln_var", "ln_root", "ln_ready", "o_sq", "o_root", "a_ready", "bm_ready", "summed",
             "y_sums", "y_ss", "y_root", "mixed", "next_sums", "dve_order")
    s = {n: sem(n) for n in names}
    unit0 = {}
    n = 0
    for name, width in (("ada", U_ADAC), ("q", 2), ("f0", 2), ("v", 2), ("g", 2), ("u", 2), ("cv", 2), ("f1", 2),
                        ("row", U_ROW), ("ga0", 2), ("A0", 1), ("gb0", 2), ("B0", 1),
                        ("ga1", 2), ("A1", 1), ("gb1", 2), ("B1", 1), ("y", 4)):
        unit0[name] = n
        n += width
    assert n == U_MIX
    uses = {}

    def use(name, keys):
        for i, key in enumerate(keys):
            uses[unit0[name] + i] = it.number[key]

    use("ada", [("ada", n) for n in range(U_ADAC)])
    use("q", [("q", 1), ("q", 3)])
    use("f0", [("fc", 0, 1), ("fc", 0, 3)])
    use("v", [("v", 0, 2), ("v", 1, 2)])
    use("g", [("g", 0, 1), ("g", 1, 1)])
    use("u", [("u", 1), ("u", 3)])
    use("cv", [("cv", 0, 1), ("cv", 1, 1)])
    use("f1", [("fc", 1, 1), ("fc", 1, 3)])
    use("row", [("row", n // 4, n % 4 // 2) for n in range(U_ROW)])
    for j in range(2):
        use(f"ga{j}", [("ga", 4 * j + 1), ("ga", 4 * j + 3)])
        use(f"A{j}", [("A", 4 * j + 3)])
        use(f"gb{j}", [("gb", 4 * j + 1), ("gb", 4 * j + 3)])
        use(f"B{j}", [("B", 4 * j + 3)])
    use("y", [("y", c, 1) for c in range(4)])

    def last_item(n):
        return uses[n]

    STEPS = [(d, i, t) for d in range(2) for i, t in enumerate(ORDER[d])]

    with nc.Block() as block:

        @block.sync
        def _(sp):
            sp.dma_start(mem["cols"][:, :], cols).then_inc(s["cols_in"], 16)
            for n in range(U_ADAC):
                if 1 <= n <= NT:
                    sp.dma_start(X[:, n - 1, :], x[(n - 1) * P:n * P, :]).then_inc(s["x_in"], 16)
                if n == NT + 1:
                    for t in range(NC_):
                        sp.dma_start(XC[:, t, :], ctx_in[t * P:(t + 1) * P, :]).then_inc(s["ctx_in"], 16)
                    sp.dma_start(mem["const1"][:, :], const1).then_inc(s["const_in"], 16)
                unit_in(sp, mem, stream, s_unit, s_full, last_item, n)
            sp.dma_start(mem["adarow"][:, :], rows[0:1, 0:4 * D].to_broadcast([P, 4 * D])).then_inc(s["adarow_in"], 16)
            for n in range(U_ADAC, unit0["g"]):
                unit_in(sp, mem, stream, s_unit, s_full, last_item, n)
            sp.wait_ge(s["xn_ready"], NT)
            a = ROWS["ln_g"][0]
            sp.dma_start(XS[:, 0:1536], rows[0:1, a:a + 1536].to_broadcast([P, 1536])).then_inc(s["lnrow_in"], 16)
            a = ROWS["g_hgrn"][0]
            sp.dma_start(GH, rows[0:1, a:a + P].to_broadcast([P, P])).then_inc(s["lnrow_in"], 16)
            sp.dma_start(XS[:, 2048:2560], w_spatial).then_inc(s["ws_in"], 16)
            for n in range(unit0["g"], unit0["ga0"] + 2):
                unit_in(sp, mem, stream, s_unit, s_full, last_item, n)
            sp.wait_ge(s["o_done"], 8)
            a = ROWS["g_post_mix"][0]
            sp.dma_start(GAIN, rows[0:1, a:a + 3072].to_broadcast([P, 3072])).then_inc(s["gain_in"], 16)
            sp.wait_ge(s["a_ready"], 4)
            sp.wait_ge(s["bm_ready"], 4)
            for t in range(NT):
                sp.dma_start(X[:, t, :], x[t * P:(t + 1) * P, :]).then_inc(s["x_again"], 16)
            for n in range(unit0["ga0"] + 2, U_MIX):
                unit_in(sp, mem, stream, s_unit, s_full, last_item, n)

        @block.gpsimd
        def _(pool):
            step = 0
            for d, i, t in STEPS:
                if t < NC_:
                    continue
                for j in range(NS):
                    lo, hi = (0, SUB * (j + 1)) if d == 0 else (SUB * j, P)
                    pool.wait_ge(s["e_k"], NS * step + j + 1)
                    km = KM[j % 2][:, :, lo:hi]
                    nc.gpsimd.tensor_tensor(km, km, KK[:, :, t * P + lo:t * P + hi], ALU.mult).then_inc(s["k_ready"], 1)
                step += 1

        @block.scalar
        def _(act):
            act.wait_ge(s["cols_in"], 16)
            nc.scalar.activation(CSC[:, :, 0], col("c"), ACT.Silu)
            nc.scalar.activation(CSC[:, :, 1], col("cc"), ACT.Silu).then_inc(s["silu_c"], 1)
            act.wait_ge(s["lb_diff"], 1)
            nc.scalar.activation(LBE[:, :], LBE[:, :], ACT.Exp).then_inc(s["lb_exp"], 1)
            act.wait_ge(s["x_in"], 16 * NT)
            act.wait_ge(s["ctx_in"], 16 * NC_)
            for t in range(NT + NC_):
                src = X[:, t, :] if t < NT else XC[:, t - NT, :]
                nc.scalar.activation(JUNK, src, ACT.Square, accum_out=SS[:, t:t + 1]).then_inc(s["sums_ready"], 1)
                act.wait_ge(s["sums_ready"], t + 1)
            act.wait_ge(s["mean_ready"], 1)
            nc.scalar.activation(SS2[:, 0:6], SS[:, 0:6], ACT.Sqrt).then_inc(s["root_ready"], 1)
            act.wait_ge(s["ada_ready"], 2)
            for v, kind, dst, width in ((0, "xT", HT, TOK), (1, "cT", HC, CTX)):
                for k in range(0, KD, 2):
                    item_full(act, (kind, k))
                    nc.scalar.activation(dst[:, k, :], bank_of((kind, k))[:, 0:width], ACT.Identity,
                                         bias=SH[:, v, k:k + 1], scale=SC[:, v, k:k + 1]).then_inc(s_act, 1)
            for h in range(4):
                item_full(act, ("q", h))
                nc.scalar.activation(qT[:, h, :], bank_of(("q", h))[:, :], ACT.Silu).then_inc(s_act, 1)

            def gates(d):
                if d == 1:
                    act.wait_ge(s["k_ready"], 4 * NS)
                for h in range(4):
                    for key, lo, width in ((("f", d, h), CTX, TOK), (("fc", d, h), 0, CTX)):
                        item_full(act, key)
                        b = bank_of(key)[:, 0:width]
                        nc.scalar.activation(LF[:, h, lo:lo + width], b, ACT.Sigmoid)
                        nc.scalar.activation(KK[:, h, lo:lo + width], b, ACT.Sigmoid, scale=-1.0).then_inc(s_act, 1)
                act.wait_ge(s["f_ready"], d + 1)
                for h in range(4):
                    nc.scalar.activation(LF[:, h, :], LF[:, h, :], ACT.Ln).then_inc(s["logf_ready"], 1)

            def fill(key):
                item_full(act, key)
                b = bank_of(key)
                if key[0] == "u":
                    nc.scalar.activation(UT[:, key[1], :], b[:, :], ACT.Gelu_apprx_tanh).then_inc(s_act, 1)
                else:
                    dst, f = (G, ACT.Silu) if key[0] == "g" else (CV, ACT.Gelu_apprx_tanh)
                    c, tp = key[1:]
                    nc.scalar.activation(dst[:, 2 * tp:2 * tp + 2, 256 * c:256 * (c + 1)], grid(b[:, :], 2),
                                         f).then_inc(s_act, 1)

            def recur(n, filled):
                d, i, t = STEPS[n]
                end = P - 1 if d == 0 else 0
                act.wait_ge(s["b_ready"], n + 1)
                if n:
                    act.wait_ge(s["kt_done"], n)
                    act.wait_ge(s["state_ready"], n)
                for h in range(4):
                    nc.scalar.activation(EK[:, h, :], BB[:, h, :], ACT.Exp, bias=BB[:, h, end:end + 1], scale=-1.0)
                nc.scalar.activation(DEC[:, :], BB[:, :, end], ACT.Exp).then_inc(s["e_end"], 1)
                if t >= NC_:
                    step = 4 * d + i - 2
                    if step:
                        act.wait_ge(s["o_done"], step)
                    nc.scalar.activation(QE, BB, ACT.Exp)
                    act.wait_ge(s["qmid_ready"], step + 1)
                    nc.scalar.activation(QD, QD, ACT.Exp).then_inc(s["e_q"], 1)

                def keys(first, last):
                    for j in range(first, last):
                        lo, hi = (0, SUB * (j + 1)) if d == 0 else (SUB * j, P)
                        act.wait_ge(s["kmid_ready"], NS * step + j + 1)
                        km = KM[j % 2][:, :, lo:hi]
                        nc.scalar.activation(km, km, ACT.Exp).then_inc(s["e_k"], 1)

                if t >= NC_:
                    keys(0, 2)
                act.wait_ge(s["kt_done"], n + 1)
                if n:
                    act.wait_ge(s["su_done"], n)
                nc.scalar.activation(KTs, grid(banks[6][:, :], 4), ACT.Copy).then_inc(s["kt_copied"], 1)
                if t >= NC_:
                    keys(2, NS)
                for key in filled:
                    fill(key)
                if t >= NC_ and d == 0:
                    act.wait_ge(s["o_done"], i - 1)
                    nc.scalar.activation(O[:, t - NC_, :], banks[5][:, :], ACT.Copy).then_inc(s["o_copied"], 1)

            gates(0)
            for n in range(6):
                recur(n, FILL0[2 * n - 2:2 * n] if n else [])
            for key in FILL0[10:12]:
                fill(key)
            act.wait_ge(s["ln_var"], 1)
            nc.scalar.activation(RS[:, :], RS[:, :], ACT.Sqrt).then_inc(s["ln_root"], 1)
            gates(1)
            for n in range(6, 12):
                recur(n, [])
            act.wait_ge(s["o_sq"], 1)
            nc.scalar.activation(SS2[:, :], SS[:, :], ACT.Sqrt).then_inc(s["o_root"], 1)

            def sigmoids(kind, j):
                for q in range(4):
                    if kind == "gb":
                        act.wait_ge(*item_read(("A", 4 * j + q)))
                    elif j == 1:
                        act.wait_ge(s["summed"], q + 1)
                    item_full(act, (kind, 4 * j + q))
                    nc.scalar.activation(SG[:, q, :], bank_of((kind, 4 * j + q))[:, :], ACT.Sigmoid).then_inc(s_act, 1)

            sigmoids("ga", 0)
            for h in range(4):
                item_full(act, ("aT", h))
                nc.scalar.activation(aT[:, h, :], bank_of(("aT", h))[:, :], ACT.Copy).then_inc(s_act, 1)
            sigmoids("gb", 0)
            sigmoids("ga", 1)
            sigmoids("gb", 1)
            for tp in range(2):
                two = slice(2 * tp, 2 * tp + 2)
                for c in range(4):
                    item_full(act, ("y", c, tp))
                    nc.scalar.activation(Y[:, two, 256 * c:256 * (c + 1)], grid(bank_of(("y", c, tp))[:, :], 2),
                                         ACT.Copy).then_inc(s_act, 1)
                act.wait_ge(*item_read(("y", 3, tp)))
                for t in range(2 * tp, 2 * tp + 2):
                    nc.scalar.activation(part(0, D), Y[:, t, :], ACT.Square, accum_out=SS[:, t:t + 1]).then_inc(
                        s["y_sums"], 1)
                    act.wait_ge(s["y_sums"], t + 1)
                act.wait_ge(s["y_ss"], tp + 1)
                nc.scalar.activation(SS2[:, two], SS[:, two], ACT.Sqrt).then_inc(s["y_root"], 1)
            for t in range(NT):
                act.wait_ge(s["mixed"], t + 1)
                nc.scalar.activation(part(0, D), X[:, t, :], ACT.Square, accum_out=mem["sums"][:, t:t + 1]).then_inc(
                    s["next_sums"], 1)
                act.wait_ge(s["next_sums"], t + 1)

        @block.vector
        def _(dve):
            order = [0]

            def link(ins):
                order[0] += 1
                ins.then_inc(s["dve_order"], 1)
                dve.wait_ge(s["dve_order"], order[0])

            def mark(ins, name, count):
                ins.then_inc(s[name], 1)
                dve.wait_ge(s[name], count)

            v = nc.vector
            link(v.memset(ONES, 1.0))
            dve.wait_ge(s["cols_in"], 16)
            lbc = col("lb").rearrange("p (d i h) -> p d i h", d=2, i=2)
            LE = LBE.rearrange("p (d i h) -> p d i h", d=2, i=2)
            LBMv = LBM.rearrange("p (d h) -> p d h", d=2)
            LBs = LB1.rearrange("p (d i h) -> p d i h", d=2, i=2)
            link(v.tensor_tensor(LBMv, lbc[:, :, 0, :], lbc[:, :, 1, :], ALU.max))
            for i in range(2):
                ins = v.tensor_tensor(LE[:, :, i, :], lbc[:, :, i, :], LBMv, ALU.subtract)
                link(ins) if i == 0 else mark(ins, "lb_diff", 1)
            dve.wait_ge(s["lb_exp"], 1)
            link(v.tensor_tensor(LBMv, LE[:, :, 0, :], LE[:, :, 1, :], ALU.add))
            link(v.reciprocal(LBM[:, :], LBM[:, :]))
            for i in range(2):
                link(v.tensor_tensor(LBs[:, :, i, :], LE[:, :, i, :], LBMv, ALU.mult))

            def ada_row(n):
                item_full(dve, ("ada", n))
                v.tensor_copy(ADAR[0:2, 256 * n:256 * (n + 1)], bank_of(("ada", n))[0:2, 0:256]).then_inc(s_dve, 1)
                dve.wait_ge(*item_read(("ada", n)))

            for n in range(U_ADAC - 4):
                ada_row(n)
            dve.wait_ge(s["sums_ready"], NT + NC_)
            mark(v.tensor_scalar(SS[:, 0:6], SS[:, 0:6], 1.0 / D, EPS, ALU.mult, ALU.add), "mean_ready", 1)
            dve.wait_ge(s["root_ready"], 1)
            link(v.reciprocal(SS2[:, 0:6], SS2[:, 0:6]))
            for t in range(NT):
                mark(v.tensor_scalar(XN[:, t, :], X[:, t, :], SS2[:, t:t + 1], None, ALU.mult), "xn_ready", t + 1)
            for t in range(NC_):
                mark(v.tensor_scalar(XCN[:, t, :], XC[:, t, :], SS2[:, NT + t:NT + t + 1], None, ALU.mult),
                     "xn_ready", NT + t + 1)
            for n in range(U_ADAC - 4, U_ADAC):
                ada_row(n)
            item_full(dve, ("adaT",))
            v.tensor_copy(ADA, bank_of(("adaT",))[:, 0:32]).then_inc(s_dve, 1)
            dve.wait_ge(*item_read(("adaT",)))
            b = ADA.rearrange("p (m v) -> p m v", v=2)
            for w in range(2):
                link(v.tensor_tensor(SH[:, w, :], b[:, 0:KD, w], col("bsh1"), ALU.add))
                link(v.tensor_tensor(SC[:, w, :], b[:, KD:2 * KD, w], col("bsc1"), ALU.add))
                ins = v.scalar_tensor_tensor(out=SC[:, w, :], in0=SC[:, w, :], scalar=1.0, in1=col("gpre"),
                                             op0=ALU.add, op1=ALU.mult)
                mark(ins, "ada_ready", w + 1)
            for w, kind, dst, width in ((0, "xT", HT, TOK), (1, "cT", HC, CTX)):
                for k in range(1, KD, 2):
                    item_full(dve, (kind, k))
                    v.tensor_scalar(dst[:, k, :], bank_of((kind, k))[:, 0:width], SC[:, w, k:k + 1],
                                    SH[:, w, k:k + 1], ALU.mult, ALU.add).then_inc(s_dve, 1)

            def forget(d):
                dve.wait_ge(*item_read(("fc", d, 3)))
                for h in range(4):
                    link(v.tensor_scalar(LF[:, h, :], LF[:, h, :], LBs[:, d, 1, h:h + 1], LBs[:, d, 0, h:h + 1],
                                         ALU.mult, ALU.add))
                for h in range(4):
                    ins = v.tensor_scalar(KK[:, h, :], KK[:, h, :], LBs[:, d, 1, h:h + 1], None, ALU.mult)
                    link(ins) if h < 3 else mark(ins, "f_ready", d + 1)

            def recur(n, filled):
                d, i, t = STEPS[n]
                lat = t >= NC_
                step = 4 * d + i - 2
                if i == 0:
                    dve.wait_ge(s["logf_ready"], 4 * (d + 1))
                for h in range(4):
                    o_, i_ = BB[:, h, :], LF[:, h, t * P:(t + 1) * P]
                    if d:
                        o_, i_ = o_[:, ::-1], i_[:, ::-1]
                    ins = v.tensor_tensor_scan(o_, ONES, i_, 0.0, ALU.mult, ALU.add)
                    link(ins) if h < 3 else mark(ins, "b_ready", n + 1)
                if lat:
                    b32 = BB.rearrange("p h (j u) -> p (h j) u", u=SUB)
                    q32 = QD.rearrange("p h (j u) -> p (h j) u", u=SUB)
                    mid = SUB // 2 - 1 if d == 0 else SUB // 2
                    mark(v.tensor_tensor(q32, b32, b32[:, :, mid:mid + 1].to_broadcast([P, 4 * NS, SUB]), ALU.subtract),
                         "qmid_ready", step + 1)

                    def kmid(j):
                        lo, hi = (0, SUB * (j + 1)) if d == 0 else (SUB * j, P)
                        at = SUB * j + mid
                        if NS * step + j >= 2:
                            dve.wait_ge(s["a_done"], NS * step + j - 1)
                        mark(v.tensor_tensor(KM[j % 2][:, :, lo:hi], BB[:, :, at:at + 1].to_broadcast([P, 4, hi - lo]),
                                             BB[:, :, lo:hi], ALU.subtract), "kmid_ready", NS * step + j + 1)

                    kmid(0)
                    kmid(1)
                    qs = qT[:, :, (t - NC_) * P:(t - NC_ + 1) * P]
                    dve.wait_ge(s["e_q"], step + 1)
                    link(v.tensor_tensor(QD, QD, qs, ALU.mult))
                    mark(v.tensor_tensor(QE, QE, qs, ALU.mult), "q_ready", step + 1)
                dve.wait_ge(s["e_end"], n + 1)
                mark(v.tensor_tensor(EK, EK, KK[:, :, t * P:(t + 1) * P], ALU.mult), "kend_ready", n + 1)
                if lat:
                    for j in range(2, NS):
                        kmid(j)
                    dve.wait_ge(s["a_done"], NS * (step + 1))
                    if step:
                        dve.wait_ge(s["o_done"], step)
                    if i == 2:
                        link(v.memset(AT, 0.0))
                    mask = grid(con("maskf" if d == 0 else "maskb").bitcast(U32), 4)
                    mark(v.copy_predicated(AT, mask, grid(banks[4][:, :], 4)), "at_ready", step + 1)
                for key in filled:
                    fill(key)
                if lat:
                    dve.wait_ge(s["o_done"], step + 1)
                    if d == 1:
                        mark(v.tensor_tensor(O[:, t - NC_, :], O[:, t - NC_, :], banks[5][:, :], ALU.add),
                             "o_added", i - 1)
                dve.wait_ge(s["su_done"], n + 1)
                su = grid(banks[7][:, :], 4)
                if i == 0:
                    mark(v.tensor_copy(S, su), "state_ready", n + 1)
                else:
                    for h in range(4):
                        ins = v.scalar_tensor_tensor(out=S[:, h, :], in0=S[:, h, :], scalar=DEC[:, h:h + 1],
                                                     in1=su[:, h, :], op0=ALU.mult, op1=ALU.add)
                        link(ins) if h < 3 else mark(ins, "state_ready", n + 1)

            forget(0)
            for c in range(2):
                for tp in range(3):
                    item_full(dve, ("v", c, tp))
                    at = 2 + 2 * tp if tp < 2 else 0
                    v.tensor_copy(V[:, at:at + 2, 256 * c:256 * (c + 1)],
                                  grid(bank_of(("v", c, tp))[:, :], 2)).then_inc(s_dve, 1)
            dve.wait_ge(s["const_in"], 16)
            link(v.memset(KM[0], 0.0))
            link(v.memset(KM[1], 0.0))
            link(v.memset(banks[4][:, :], 0.0))
            for n in range(6):
                recur(n, [])
            dve.wait_ge(*item_read(("cv", 1, 1)))
            for t in range(NT):
                link(v.bn_stats(ST[:, 6 * t:6 * t + 6], CV[:, t, :]))
                link(v.bn_aggr(MV[:, 2 * t:2 * t + 2], ST[:, 6 * t:6 * t + 6]))
            mark(v.tensor_scalar(RS[:, :], grid(MV[:, :], 4)[:, :, 1], EPS, None, ALU.add), "ln_var", 1)
            dve.wait_ge(s["ln_root"], 1)
            link(v.reciprocal(RS[:, :], RS[:, :]))
            dve.wait_ge(s["lnrow_in"], 32)
            for t in range(NT):
                link(v.tensor_scalar(CV[:, t, :], CV[:, t, :], MV[:, 2 * t:2 * t + 1], RS[:, t:t + 1],
                                     ALU.subtract, ALU.mult))
                link(v.tensor_tensor(CV[:, t, :], CV[:, t, :], LNG, ALU.mult))
                mark(v.tensor_tensor(CV[:, t, :], CV[:, t, :], LNB, ALU.add), "ln_ready", t + 1)
            item_full(dve, ("fc", 1, 3))
            mark(v.tensor_copy(CSB, CSC[:, :, 0:1].to_broadcast([P, KD, P])), "csb_ready", 1)
            forget(1)
            dve.wait_ge(s["adarow_in"], 16)

            def fill(key):
                item_full(dve, key)
                b = bank_of(key)
                sk, ck = item_read(key)
                if key[0] == "row":
                    r, j = key[1:]
                    dst = ROW[:, r, 512 * j:512 * (j + 1)]
                    v.tensor_tensor(dst, dst, b[:, :], ALU.add).then_inc(s_dve, 1)
                else:
                    g = key[1]
                    v.tensor_tensor(TMP, grid(b[:, :], 4),
                                    BS[:, g:g + 1, :].to_broadcast([P, 4, P]), ALU.add).then_inc(s_dve, 1)
                    dve.wait_ge(sk, ck)
                    mark(v.tensor_tensor(UT[:, g, :], UT[:, g, :], TMP.rearrange("p a b -> p (a b)"), ALU.mult),
                         "bm_ready", g + 1)
                dve.wait_ge(sk, ck)

            TMP = grid(mem["X"][:, 2560:3072], 4)
            for n in range(6, 12):
                recur(n, FILL1[2 * (n - 6):2 * (n - 5)])
            for t in range(NT):
                link(v.tensor_tensor(BB.rearrange("p a b -> p (a b)"), O[:, t, :], O[:, t, :], ALU.mult))
                link(v.tensor_reduce(SS[:, 4 * t:4 * t + 4], BB, AX, ALU.add))
            mark(v.tensor_scalar(SS[:, :], SS[:, :], 1.0 / P, EPS, ALU.mult, ALU.add), "o_sq", 1)
            dve.wait_ge(s["o_root"], 1)
            link(v.reciprocal(SS2[:, :], SS2[:, :]))
            for t in range(NT):
                o = grid(O[:, t, :], 4)
                r4 = SS2[:, 4 * t:4 * t + 4].rearrange("p (h a) -> p h a", a=1)
                link(v.tensor_tensor(o, o, r4.to_broadcast([P, 4, P]), ALU.mult))
                link(v.tensor_tensor(o, o, GH.rearrange("p (a b) -> p a b", a=1).to_broadcast([P, 4, P]), ALU.mult))
                mark(v.tensor_tensor(O[:, t, :], O[:, t, :], G[:, t, :], ALU.mult), "a_ready", t + 1)
            for j in range(2):
                for w, (kind, gate) in enumerate((("A", "ga"), ("B", "gb"))):
                    for mm in range(4):
                        key = (kind, 4 * j + mm)
                        sk, ck = item_read((gate, 4 * j + mm))
                        dve.wait_ge(sk, ck)
                        item_full(dve, key)
                        sk, ck = item_read(key)
                        dst = yT[:, 4 * j + mm, :] if w == 0 else SG[:, mm, :]
                        v.tensor_tensor(dst, SG[:, mm, :], bank_of(key)[:, :], ALU.mult).then_inc(s_dve, 1)
                        dve.wait_ge(sk, ck)
                        if w == 1:
                            mark(v.tensor_tensor(yT[:, 4 * j + mm, :], yT[:, 4 * j + mm, :], SG[:, mm, :], ALU.add),
                                 "summed", 4 * j + mm + 1)
            dve.wait_ge(s["gain_in"], 16)
            link(v.tensor_tensor(ROW[:, 0, :], ROW[:, 0, :], GAIN[:, 0:D], ALU.mult))
            link(v.scalar_tensor_tensor(out=ROW[:, 2, :], in0=ROW[:, 2, :], scalar=1.0, in1=GAIN[:, D:2 * D],
                                        op0=ALU.add, op1=ALU.mult))
            link(v.tensor_tensor(ROW[:, 3, :], ROW[:, 3, :], GAIN[:, 2 * D:3 * D], ALU.mult))
            dve.wait_ge(s["x_again"], 16 * NT)
            for tp in range(2):
                two = slice(2 * tp, 2 * tp + 2)
                dve.wait_ge(s["y_sums"], 2 * tp + 2)
                mark(v.tensor_scalar(SS[:, two], SS[:, two], 1.0 / D, EPS, ALU.mult, ALU.add), "y_ss", tp + 1)
                dve.wait_ge(s["y_root"], tp + 1)
                link(v.reciprocal(SS2[:, two], SS2[:, two]))
                for t in range(2 * tp, 2 * tp + 2):
                    link(v.scalar_tensor_tensor(out=Y[:, t, :], in0=Y[:, t, :], scalar=SS2[:, t:t + 1],
                                                in1=ROW[:, 0, :], op0=ALU.mult, op1=ALU.mult))
                    mark(v.tensor_tensor(X[:, t, :], X[:, t, :], Y[:, t, :], ALU.add), "mixed", t + 1)

        @block.tensor
        def _(pe):
            mm = nc.tensor.matmul
            ring = mem["ring"]

            def unit(n):
                return ring[:, (n % RING) * UNIT:(n % RING + 1) * UNIT]

            def features(n, key, half, src, lo, width):
                bank_free(pe, key)
                w = unit(n).rearrange("p (k c) -> p k c", k=KD)
                for k in range(KD):
                    last = mm(bank_of(key)[:, 0:width], w[:, k, half * P:(half + 1) * P], src[:, k, lo:lo + width],
                              start=(k == 0), stop=(k == KD - 1))
                last.then_inc(s_full, 1)

            def tokens(n, key, tp, src):
                bank_free(pe, key)
                w = unit(n).rearrange("p (k c) -> p k c", k=KD)
                for a in range(2):
                    for k in range(KD):
                        last = mm(bank_of(key)[:, 256 * a:256 * (a + 1)], src[:, k, (2 * tp + a) * P:(2 * tp + a + 1) * P],
                                  w[:, k, :], start=(k == 0), stop=(k == KD - 1))
                last.then_inc(s_full, 1)

            def full(key):
                return bank_of(key)

            pe.wait_ge(s["silu_c"], 1)
            for n in range(U_ADAC):
                unit_ready(pe, s_unit, n)
                bank_free(pe, ("ada", n))
                w = unit(n).rearrange("p (k c) -> p k c", k=KD)
                for k in range(KD):
                    last = mm(full(("ada", n))[0:2, 0:256], CSC[:, k, :], w[:, k, :], start=(k == 0), stop=(k == KD - 1))
                last.then_inc(s_full, 1)
            pe.wait_ge(s["const_in"], 16)
            pe.wait_ge(*item_read(("ada", U_ADAC - 1)))
            for c in range(16):
                last = nc.tensor.transpose(full(("adaT",))[:, 2 * c:2 * c + 2], ADAR[0:2, P * c:P * (c + 1)],
                                           ident[0:2, 0:2])
            last.then_inc(s_full, 1)
            for kind, src, tiles, first in (("xT", XN, NT, 0), ("cT", XCN, NC_, NT)):
                pe.wait_ge(s["xn_ready"], first + tiles)
                for k in range(KD):
                    bank_free(pe, (kind, k))
                    for t in range(tiles):
                        last = nc.tensor.transpose(full((kind, k))[:, t * P:(t + 1) * P], src[:, t, k * P:(k + 1) * P],
                                                   ident)
                    last.then_inc(s_full, 1)
            for key in (("xT", 6), ("xT", 7), ("cT", 6), ("cT", 7)):
                pe.wait_ge(*item_read(key))
            for h in range(4):
                n = unit0["q"] + h // 2
                unit_ready(pe, s_unit, n)
                features(n, ("q", h), h % 2, HT, 0, TOK)

            def forget_logits(d):
                for h in range(4):
                    n = unit0[f"f{d}"] + h // 2
                    unit_ready(pe, s_unit, n)
                    features(n, ("f", d, h), h % 2, HT, 0, TOK)
                    features(n, ("fc", d, h), h % 2, HC, 0, CTX)

            def fill(key):
                kind = key[0]
                if kind == "u":
                    n = unit0["u"] + key[1] // 2
                    unit_ready(pe, s_unit, n)
                    features(n, key, key[1] % 2, HT, 0, TOK)
                elif kind in ("g", "cv"):
                    n = unit0[kind] + key[1]
                    unit_ready(pe, s_unit, n)
                    tokens(n, key, key[2], HT)
                elif kind == "row":
                    pe.wait_ge(s["csb_ready"], 1)
                    bank_free(pe, key)
                    for a in range(2):
                        n = unit0["row"] + 4 * key[1] + 2 * key[2] + a
                        unit_ready(pe, s_unit, n)
                        w = unit(n).rearrange("p (k c) -> p k c", k=KD)
                        for k in range(KD):
                            last = mm(full(key)[:, 256 * a:256 * (a + 1)], CSB[:, k, :], w[:, k, :],
                                      start=(k == 0), stop=(k == KD - 1))
                    last.then_inc(s_full, 1)
                else:
                    g = key[1]
                    pe.wait_ge(s["ln_ready"], NT)
                    pe.wait_ge(s["ws_in"], 16)
                    bank_free(pe, key)
                    for t in range(NT):
                        last = mm(full(key)[:, t * P:(t + 1) * P], CV[:, t, g * P:(g + 1) * P], WS[:, g, :],
                                  start=True, stop=True)
                    last.then_inc(s_full, 1)

            def recur(n, filler):
                d, i, t = STEPS[n]
                lat = t >= NC_
                step = 4 * d + i - 2
                pe.wait_ge(s["kend_ready"], n + 1)
                if n:
                    pe.wait_ge(s["kt_copied"], n)
                for h in range(4):
                    last = nc.tensor.transpose(grid(banks[6][:, :], 4)[:, h, :], EK[:, h, :], ident)
                last.then_inc(s["kt_done"], 1)
                if lat:
                    pe.wait_ge(s["q_ready"], step + 1)
                    for j in range(NS):
                        pe.wait_ge(s["k_ready"], NS * step + j + 1)
                        if j == 0 and step:
                            pe.wait_ge(s["at_ready"], step)
                        hi = P if d else -(-SUB * (j + 1) // 32) * 32
                        lo = (0, 0, 64, 96)[SUB * j // 32] if d else 0
                        for h in range(4):
                            last = mm(grid(banks[4][:, :], 4)[lo:hi, h, SUB * j:SUB * (j + 1)], KM[j % 2][:, h, lo:hi],
                                      QD[:, h, SUB * j:SUB * (j + 1)], start=True, stop=True)
                        last.then_inc(s["a_done"], 1)
                pe.wait_ge(s["kt_copied"], n + 1)
                if n:
                    pe.wait_ge(s["state_ready"], n)
                for h in range(4):
                    last = mm(grid(banks[7][:, :], 4)[:, h, :], KTs[:, h, :], V[:, t, h * P:(h + 1) * P],
                              start=True, stop=True)
                last.then_inc(s["su_done"], 1)
                if lat:
                    pe.wait_ge(s["at_ready"], step + 1)
                    if 0 < step <= 4:
                        pe.wait_ge(s["o_copied"], step)
                    elif step:
                        pe.wait_ge(s["o_added"], step - 4)
                    for h in range(4):
                        o = grid(banks[5][:, :], 4)[:, h, :]
                        mm(o, AT[:, h, :], V[:, t, h * P:(h + 1) * P], start=True, stop=False)
                        last = mm(o, QE[:, h, :], S[:, h, :], start=False, stop=True)
                    last.then_inc(s["o_done"], 1)
                for key in filler:
                    fill(key)

            forget_logits(0)
            for c in range(2):
                unit_ready(pe, s_unit, unit0["v"] + c)
                for tp in range(3):
                    tokens(unit0["v"] + c, ("v", c, tp), tp if tp < 2 else 0, HT if tp < 2 else HC)
            pe.wait_ge(*item_read(("v", 1, 2)))
            for n in range(6):
                recur(n, FILL0[2 * n:2 * n + 2])
            forget_logits(1)
            for key in FILL1[0:2]:
                fill(key)
            for n in range(6, 12):
                recur(n, FILL1[2 * (n - 5):2 * (n - 5) + 2])

            def gates(kind, j):
                for q in range(4):
                    n = unit0[f"{kind}{j}"] + q // 2
                    unit_ready(pe, s_unit, n)
                    features(n, (kind, 4 * j + q), q % 2, HT, 0, TOK)

            gates("ga", 0)
            pe.wait_ge(s["a_ready"], NT)
            for h in range(4):
                bank_free(pe, ("aT", h))
                for t in range(NT):
                    last = nc.tensor.transpose(full(("aT", h))[:, t * P:(t + 1) * P], O[:, t, h * P:(h + 1) * P], ident)
                last.then_inc(s_full, 1)
            for j in range(2):
                for kind, src in (("ga", HT), ("A", aT), ("gb", HT), ("B", UT)):
                    if kind in ("ga", "gb"):
                        if (j, kind) != (0, "ga"):
                            gates(kind, j)
                        continue
                    for q in range(4):
                        key = (kind, 4 * j + q)
                        n = unit0[f"{kind}{j}"]
                        unit_ready(pe, s_unit, n)
                        if kind == "A":
                            pe.wait_ge(*item_read(("aT", 3)))
                        else:
                            pe.wait_ge(s["bm_ready"], 4)
                        bank_free(pe, key)
                        w = unit(n).rearrange("p (k c) -> p k c", k=4)
                        for k in range(4):
                            last = mm(full(key)[:, :], w[:, k, q * P:(q + 1) * P], src[:, k, :],
                                      start=(k == 0), stop=(k == 3))
                        last.then_inc(s_full, 1)
            pe.wait_ge(s["summed"], KD)
            for tp in range(2):
                for c in range(4):
                    unit_ready(pe, s_unit, unit0["y"] + c)
                    tokens(unit0["y"] + c, ("y", c, tp), tp, yT)


def moe(nc, sem, banks, mem, dram, s_unit, stream, experts, rows, w_router):
    W = mem["work"]

    def part(first, width):
        assert first + width <= WORK_MOE
        return W[:, first:first + width]

    def grid(a, outer):
        return a.rearrange("p (a b) -> p a b", a=outer)

    X = grid(mem["X"][:, :], NT)
    HT = grid(mem["HT"][:, :], KD)
    ROW = grid(mem["adarow"][:, :], 4)
    ident, before, slots = (mem["const1"][:, C1[n][0]:C1[n][0] + P] for n in ("ident", "before", "slots"))
    tok = mem["const1"][:, C1["tok"][0]:C1["tok"][0] + 4]
    SLOT = 6144
    wslot = [part(0, SLOT), part(SLOT, SLOT), mem["ring"][:, 0:SLOT], mem["ring"][:, SLOT:2 * SLOT]]
    at = [2 * SLOT]

    def take(width):
        at[0] += width
        return part(at[0] - width, width)

    FF = take(4096)
    F = grid(FF, NT)
    H2 = grid(take(4096), NT)
    base = at[0] - 4096
    JUNK = take(1024)
    SHT = grid(JUNK, 2)
    WR = grid(take(512), KD)
    ONES = take(P)
    XG = [part(base, D), part(base + 1024, D)] + [mem["adarow"][:, D * j:D * (j + 1)] for j in (1, 2)]
    XGT = [grid(part(base + 2048, D), KD), grid(part(base + 3072, D), KD)]
    OVER = FF[:, 0:2 * D]
    OUT = [FF[:, D * k:D * (k + 1)] for k in range(4)]
    PM = take(4 * 68).rearrange("p (t e) -> p t e", t=4)
    exact = lambda name, width: mem["float32r"](name, width)[:, :]
    R = exact("selected", 4 * 68 * 4).rearrange("p (t e c) -> p t e c", t=4, c=4)
    ONEHOT = [grid(exact(f"onehot{k}", 512), 4) for k in range(2)]
    ONEHOTX = grid(exact("onehot_further", 512), 4)
    CNT = take(NE).bitcast(I32)
    SG, HID, HDT = take(256), take(256), [grid(take(256), 2) for _ in range(2)]
    TOKI, ROWI = take(4).bitcast(I32), take(4).bitcast(I32)
    ROWA, WCA = take(68).bitcast(I32), take(68)
    WC, OFF, SS, SS2, RSW = take(4), take(1), take(4), take(4), take(4)
    over = [0]

    def take_over(width):
        over[0] += width
        return OVER[:, over[0] - width:over[0]]

    SCO, SEL, SELM, REP2, MSK = (grid(take_over(256), 4) for _ in range(5))
    BR = take_over(NE)
    MX = take_over(256).rearrange("p (t g k) -> p t g k", t=4, g=NGRP)
    GSC, VG, REP, GM, V8 = (grid(take_over(w), 4) for w in (48, 32, 48, 32, 32))
    assert over[0] <= 2 * D
    EX = mem["HT"]
    XGX, XGTX, OUTX = EX[:, 0:1024], grid(EX[:, 1024:2048], KD), EX[:, 2048:3072]
    HIDX = EX[:, 3584:3840]
    EXR = mem["adarow"]
    SGX, HDTX = EXR[:, 0:256], grid(EXR[:, 256:512], 2)
    IDXX, WCX = EXR[:, 512:513].bitcast(I32), EXR[:, 513:514]
    JUNK2 = EX[:, 0:1024]
    names = ("row_in", "wr_in", "h2_mean", "h2_root", "h2_ready", "h2_stored", "ht_full", "ht_act", "ht_dve",
             "logits_done", "scores_ready", "mask_ready", "ranks_done", "tables_ready", "cnt_ready",
             "sh_full", "sh_act", "sh_dve", "f_full", "f_copied", "dve_order",
             "onehot", "idx_done", "idx_ready", "placed", "t_done", "xgt_act", "xgt_dve", "gu_done", "sg_ready", "hid_ready",
             "ht2_done", "hdt_ready", "dn_done", "out_act", "out_dve",
             "x_p", "x_idx", "x_idxr", "x_gath", "x_t", "x_e", "x_gu", "x_sg", "x_hid", "x_ht", "x_he", "x_dn", "x_o",
             "x_sc", "acc_stored", "scattered", "f_sums", "f_mean", "f_root", "normed", "added", "last_added", "next_sums", "zeroed", "copies")
    s = {n: sem("moe_" + n) for n in names}
    s_back = [sem(f"sums_back{t}") for t in range(NT)]
    s_exp = [sem(f"expert_arrived{k}") for k in range(4)]
    s_gath = [sem(f"gathered{k}") for k in range(4)]
    LOADU = [n for n in range(U_MIX, U_MIX + U_SHARED)]

    def after(eng, name, i, o, c, k=1):
        value = k * o + c + (4 * k) * i
        if not isinstance(value, int) or value > 0:
            eng.wait_ge(s[name], value)

    def scattered(eng, i, o):
        after(eng, "scattered", i, o, 16, 16)

    def index(i, o):
        return bass.ds(4 * i + o, 1)

    def over_experts(eng, body):
        for u in range(4):
            body(0, u)
        with eng.Fori(1, NE // 4) as i:
            for u in range(4):
                body(i, u)

    def block_ahead(eng, i, u, done, find):
        count = eng.value_load(CNT[0:1, index(i, u)])
        with eng.If(count > P):
            find(1, eng.snap(done))

    def more_blocks(eng, i, u, done, find, body):
        count = eng.value_load(CNT[0:1, index(i, u)])

        def block_of(b):
            with eng.If(count > P * b):
                n = eng.snap(done)
                if b > 1:
                    find(b, n)
                body(b, n)
                eng.reg_add(done, done, 1)
                if b < 3:
                    block_of(b + 1)

        block_of(1)

    with nc.Block() as block:

        @block.sync
        def _(sp):
            a = ROWS["b_router"][0]
            sp.dma_start(BR, rows[0:1, a:a + NE].to_broadcast([P, NE])).then_inc(s["row_in"], 16)
            sp.dma_start(WR.rearrange("p k c -> p (k c)"), w_router).then_inc(s["wr_in"], 16)
            for n in LOADU:
                sp.dma_start(mem["ring"][:, (n % RING) * UNIT:(n % RING + 1) * UNIT], stream[n]).then_inc(
                    s_unit[n % RING], 16)
            for e in range(2):
                sp.dma_start(wslot[e], experts[e]).then_inc(s_exp[e], 16)
            for t in range(NT):
                sp.wait_ge(s["h2_ready"], t + 1)
                sp.dma_start(dram["xn"][t * P:(t + 1) * P, :], H2[:, t, :]).then_inc(s["h2_stored"], 16)
            for t in range(NT):
                sp.wait_ge(s["f_copied"], 2 * t + 2)
                sp.dma_start(dram["acc"][t * P:(t + 1) * P, :], F[:, t, :]).then_inc(s["acc_stored"], 16)
            for e in (2, 3):
                sp.dma_start(wslot[e], experts[e]).then_inc(s_exp[e], 16)
            with sp.Fori(1, NE // 4) as i:
                for u in range(4):
                    sp.wait_ge(s["dn_done"], 4 * i + (u - 3))
                    sp.dma_start(wslot[u], experts[index(i, u)].rearrange("a p c -> (a p) c")).then_inc(s_exp[u], 16)
            sp.wait_ge(s["scattered"], 16 * NE)
            for k in range(4):
                sp.wait_ge(s_gath[k], 16 * (NE // 4 + (k < 3)))
            sp.wait_ge(s["xgt_act"], NE + 1)
            sp.wait_ge(s["xgt_dve"], NE + 1)
            sp.wait_ge(s["idx_done"], NE + 3)
            sp.wait_ge(s["out_act"], NE)
            for t in range(NT):
                sp.dma_start(F[:, t, :], dram["acc"][t * P:(t + 1) * P, :]).then_inc(s_back[t], 16)
            sp.wait_ge(s["dn_done"], NE)
            for n in range(FIRST2, FIRST2 + RING):
                sp.dma_start(mem["ring"][:, (n % RING) * UNIT:(n % RING + 1) * UNIT], stream[n]).then_inc(
                    s_unit[n % RING], 16)

        @block.gpsimd
        def _(pool):
            done = pool.alloc_register("further_blocks_pool")
            pool.reg_mov(done, 0)

            def count_copy():
                pool.sem_inc(s["copies"], 1)

            pool.wait_ge(s["h2_stored"], 16 * NT)
            pool.wait_ge(s["cnt_ready"], 1)

            def gather(i, o):
                after(pool, "idx_ready", i, o, 1)
                after(pool, "t_done", i, o - 4, 1)
                count_copy()
                nc.gpsimd.indirect_dma_start(
                    out=XG[o % 4], out_offset=None, in_=dram["xn"][:, :],
                    in_offset=bass.IndirectOffsetOnAxis(ap=TOKI[:, o % 4:o % 4 + 1].bitcast(U32), axis=0),
                    bounds_check=TOK - 1, oob_is_err=False).then_inc(s_gath[o % 4], 16)

            def scatter(i, o):
                after(pool, "out_act", i, o, 1)
                after(pool, "out_dve", i, o, 1)
                scattered(pool, i, o - 1)
                count_copy()
                nc.gpsimd.indirect_dma_start(
                    out=dram["acc"][:, :],
                    out_offset=bass.IndirectOffsetOnAxis(ap=ROWI[:, o % 4:o % 4 + 1].bitcast(U32), axis=0),
                    in_=OUT[o % 4], in_offset=None, bounds_check=TOK - 1, oob_is_err=False, compute_op=ALU.add
                    ).then_inc(s["scattered"], 16)

            def find_further(b, n):
                pool.wait_ge(s["x_idxr"], n + 1)
                count_copy()
                nc.gpsimd.indirect_dma_start(
                    out=XGX, out_offset=None, in_=dram["xn"][:, :],
                    in_offset=bass.IndirectOffsetOnAxis(ap=IDXX[:, 0:1].bitcast(U32), axis=0),
                    bounds_check=TOK - 1, oob_is_err=False).then_inc(s["x_gath"], 16)

            def further(b, n):
                pool.wait_ge(s["x_o"], 2 * n + 2)
                scattered(pool, *before_it[0])
                count_copy()
                nc.gpsimd.indirect_dma_start(
                    out=dram["acc"][:, :],
                    out_offset=bass.IndirectOffsetOnAxis(ap=IDXX[:, 0:1].bitcast(U32), axis=0),
                    in_=OUTX, in_offset=None, bounds_check=TOK - 1, oob_is_err=False, compute_op=ALU.add
                    ).then_inc(s["x_sc"], 16)
                pool.wait_ge(s["x_sc"], 16 * n + 16)

            def body(i, u):
                block_ahead(pool, i, u, done, find_further)
                gather(i, u + 3)
                if u or not isinstance(i, int):
                    scatter(i, u - 1)
                before_it[0] = (i, u - 1)
                more_blocks(pool, i, u, done, find_further, further)

            before_it = [None]
            pool.wait_ge(s["zeroed"], 1)
            gather(0, 0)
            gather(0, 1)
            gather(0, 2)
            pool.wait_ge(s["acc_stored"], 16 * NT)
            over_experts(pool, body)
            scatter(NE // 4, -1)
            pool.wait_ge(s["scattered"], 16 * NE)
            for k in range(4):
                pool.wait_ge(s_gath[k], 16 * (NE // 4 + (k < 3)))
            pool.wait_ge(s["normed"], 1)
            nc.gpsimd.tensor_tensor(X[:, NT - 1, :], X[:, NT - 1, :], F[:, NT - 1, :], ALU.add).then_inc(
                s["last_added"], 1)

        @block.scalar
        def _(act):
            done = act.alloc_register("further_blocks_act")
            act.reg_mov(done, 0)
            act.wait_ge(s["h2_mean"], 1)
            nc.scalar.activation(SS2[:, :], SS[:, :], ACT.Sqrt).then_inc(s["h2_root"], 1)
            for k in range(0, KD, 2):
                act.wait_ge(s["ht_full"], k + 1)
                nc.scalar.activation(HT[:, k, :], banks[k % 4][:, :], ACT.Copy).then_inc(s["ht_act"], 1)
            act.wait_ge(s["logits_done"], 1)
            nc.scalar.activation(SCO.rearrange("p t e -> p (t e)"), banks[4][:, 0:256], ACT.Sigmoid).then_inc(
                s["scores_ready"], 1)
            for m in range(2):
                act.wait_ge(s["sh_full"], m + 1)
                nc.scalar.activation(SHT[:, m, :], banks[m][:, :], ACT.Silu).then_inc(s["sh_act"], 1)

            def copy_xgt(i, o):
                after(act, "t_done", i, o, 1)
                after(act, "gu_done", i, o - 2, 1)
                nc.scalar.activation(XGT[o % 2][:, 0:4, :], grid(banks[0][:, :], 4), ACT.Copy).then_inc(s["xgt_act"], 1)

            def silu(i, o):
                after(act, "gu_done", i, o, 1)
                after(act, "hid_ready", i, o - 1, 1)
                nc.scalar.activation(SG, banks[2][:, 0:256], ACT.Silu).then_inc(s["sg_ready"], 1)

            def scaled_out(i, o):
                after(act, "dn_done", i, o, 1)
                after(act, "placed", i, o, 1)
                scattered(act, i, o - 4)
                nc.scalar.activation(OUT[o % 4][:, 0:512], banks[4][:, :], ACT.Copy,
                                     scale=WC[:, o % 4:o % 4 + 1]).then_inc(s["out_act"], 1)

            def copy_hdt(i, o):
                after(act, "ht2_done", i, o, 1)
                after(act, "dn_done", i, o - 2, 1)
                nc.scalar.activation(HDT[o % 2], grid(banks[3][:, 0:256], 2), ACT.Copy).then_inc(s["hdt_ready"], 1)

            def further(b, n):
                for h in range(2):
                    act.wait_ge(s["x_t"], 2 * n + h + 1)
                    nc.scalar.activation(XGTX[:, 4 * h:4 * h + 4, :], grid(banks[7][:, :], 4), ACT.Copy).then_inc(
                        s["x_e"], 1)
                act.wait_ge(s["x_gu"], n + 1)
                nc.scalar.activation(SGX, banks[7][:, 0:256], ACT.Silu).then_inc(s["x_sg"], 1)
                act.wait_ge(s["x_ht"], n + 1)
                nc.scalar.activation(HDTX, grid(banks[7][:, 0:256], 2), ACT.Copy).then_inc(s["x_he"], 1)
                for j in range(2):
                    act.wait_ge(s["x_dn"], 2 * n + j + 1)
                    nc.scalar.activation(OUTX[:, 512 * j:512 * (j + 1)], banks[7][:, :], ACT.Copy,
                                         scale=WCX[:, 0:1]).then_inc(s["x_o"], 1)

            def body(i, u):
                silu(i, u)
                copy_xgt(i, u + 1)
                if u or not isinstance(i, int):
                    scaled_out(i, u - 1)
                copy_hdt(i, u)
                more_blocks(act, i, u, done, lambda b, n: None, further)

            act.wait_ge(s["cnt_ready"], 1)
            copy_xgt(0, 0)
            act.wait_ge(s["acc_stored"], 16 * NT)
            over_experts(act, body)
            scaled_out(NE // 4, -1)
            for t in range(NT):
                act.wait_ge(s_back[t], 16)
                nc.scalar.activation(JUNK2, F[:, t, :], ACT.Square, accum_out=SS[:, t:t + 1]).then_inc(s["f_sums"], 1)
                act.wait_ge(s["f_sums"], t + 1)
            act.wait_ge(s["f_mean"], 1)
            nc.scalar.activation(SS2[:, :], SS[:, :], ACT.Sqrt).then_inc(s["f_root"], 1)
            for t in range(NT - 1, -1, -1):
                act.wait_ge(*((s["last_added"], 1) if t == NT - 1 else (s["added"], NT - 1 - t)))
                nc.scalar.activation(JUNK2, X[:, t, :], ACT.Square, accum_out=mem["sums"][:, t:t + 1]).then_inc(
                    s["next_sums"], 1)
                act.wait_ge(s["next_sums"], NT - t)

        @block.vector
        def _(dve):
            v = nc.vector
            order = [0]
            done = dve.alloc_register("further_blocks_dve")
            dve.reg_mov(done, 0)

            def link(ins):
                order[0] += 1
                ins.then_inc(s["dve_order"], 1)
                dve.wait_ge(s["dve_order"], order[0])

            def mark(ins, name, count):
                ins.then_inc(s[name], 1)
                dve.wait_ge(s[name], count)

            link(v.memset(ONES, 1.0))
            mark(v.tensor_scalar(SS[:, :], mem["sums"][:, :], 1.0 / D, EPS, ALU.mult, ALU.add), "h2_mean", 1)
            dve.wait_ge(s["h2_root"], 1)
            link(v.reciprocal(SS2[:, :], SS2[:, :]))
            for t in range(NT):
                link(v.scalar_tensor_tensor(out=H2[:, t, :], in0=X[:, t, :], scalar=SS2[:, t:t + 1], in1=ROW[:, 2, :],
                                            op0=ALU.mult, op1=ALU.mult))
                mark(v.tensor_tensor(H2[:, t, :], H2[:, t, :], ROW[:, 1, :], ALU.add), "h2_ready", t + 1)
            for k in range(1, KD, 2):
                dve.wait_ge(s["ht_full"], k + 1)
                v.tensor_copy(HT[:, k, :], banks[k % 4][:, :]).then_inc(s["ht_dve"], 1)
            dve.wait_ge(s["h2_stored"], 16 * NT)
            for k in range(4):
                link(v.memset(XG[k], 0.0)) if k < 3 else mark(v.memset(XG[k], 0.0), "zeroed", 1)
            dve.wait_ge(s["row_in"], 16)
            dve.wait_ge(s["scores_ready"], 1)
            link(v.tensor_tensor(SEL, SCO, BR.rearrange("p (a e) -> p a e", a=1).to_broadcast([P, 4, NE]), ALU.add))
            for t in range(NT):
                for g in range(NGRP):
                    last = v.max(MX[:, t, g, :], SEL[:, t, 8 * g:8 * g + 8])
            link(last)
            for j in range(4):
                last = v.memset(GSC[:, :, 8 + j:9 + j], NEG * (j + 1))
            link(last)
            link(v.tensor_tensor(GSC[:, :, 0:8], MX[:, :, :, 0], MX[:, :, :, 1], ALU.add))
            for t in range(NT):
                last = v.max(VG[:, t, :], GSC[:, t, 0:8])
            link(last)
            link(v.tensor_copy(VG[:, :, 4:8], GSC[:, :, 8:12]))
            for t in range(NT):
                last = v.match_replace(out=REP[:, t, :], in_to_replace=VG[:, t, :], in_values=GSC[:, t, :],
                                       imm_value=200 * NEG)
            link(last)
            link(v.tensor_tensor(GM, REP[:, :, 0:8], GSC[:, :, 0:8], ALU.not_equal))
            link(v.memset(SELM, NEG))
            link(v.copy_predicated(
                SELM.rearrange("p t (g k) -> p (t g) k", k=8),
                GM.bitcast(U32).rearrange("p t (g a) -> p (t g) a", a=1).to_broadcast([P, 32, 8]),
                SEL.rearrange("p t (g k) -> p (t g) k", k=8)))
            for t in range(NT):
                last = v.max(V8[:, t, :], SELM[:, t, :])
            link(last)
            for t in range(NT):
                last = v.match_replace(out=REP2[:, t, :], in_to_replace=V8[:, t, :], in_values=SELM[:, t, :],
                                       imm_value=200 * NEG)
            link(last)
            mark(v.tensor_tensor(MSK, REP2, SELM, ALU.not_equal), "mask_ready", 1)
            link(v.tensor_tensor(SEL, SCO, MSK, ALU.mult))
            link(v.tensor_reduce(RSW[:, :], SEL, AX, ALU.add))
            link(v.reciprocal(RSW[:, :], RSW[:, :]))
            link(v.memset(R.rearrange("p t e c -> p (t e c)").bitcast(F32), 0.0))
            link(v.memset(PM.rearrange("p t e -> p (t e)"), -1.0))
            for t in range(NT):
                last = v.tensor_scalar(SELM[:, t, :], SEL[:, t, :], RSW[:, t:t + 1], 2.5, ALU.mult, ALU.mult)
            link(last)
            link(v.tensor_copy(R[:, :, 0:NE, 1], SELM))
            link(v.tensor_tensor(R[:, :, 0:NE, 2], SELM, R[:, :, 0:NE, 1], ALU.subtract))
            for t in range(NT):
                last = v.tensor_scalar(R[:, t, 0:NE, 0], tok[:, t:t + 1].to_broadcast([P, NE]), float(-TOK), None,
                                       ALU.add)
            link(last)
            link(v.memset(OFF, float(TOK)))
            dve.wait_ge(s["ranks_done"], 1)
            link(v.scalar_tensor_tensor(out=PM[:, :, 0:NE], in0=grid(banks[5][:, 0:256], 4), scalar=1.0, in1=MSK,
                                        op0=ALU.add, op1=ALU.mult))
            mark(v.tensor_scalar(PM[:, :, 0:NE], PM[:, :, 0:NE], -1.0, None, ALU.add), "tables_ready", 1)
            mark(v.tensor_copy(CNT, banks[6][:, 0:NE]), "cnt_ready", 1)
            def onehot(i, o):
                after(dve, "idx_done", i, o - 2, 1)
                for t in range(NT):
                    last = v.tensor_scalar(ONEHOT[o % 2][:, t, :], slots, PM[:, t, index(i, o)], None, ALU.is_equal)
                last.then_inc(s["onehot"], 1)

            def indices(i, o):
                after(dve, "idx_done", i, o, 1)
                if o >= 4 or not isinstance(i, int):
                    dve.wait_ge(s_gath[o % 4], 16 * (o // 4) + 16 * i)
                v.tensor_reduce(WCA[:, index(i, o)], banks[6][:, 1:3], AX, ALU.add)
                v.tensor_tensor(ROWA[:, index(i, o)], banks[6][:, 0:1], OFF, ALU.add)
                v.tensor_tensor(TOKI[:, o % 4:o % 4 + 1], banks[6][:, 0:1], OFF, ALU.add).then_inc(
                    s["idx_ready"], 1)

            def place(i, o):
                after(dve, "idx_ready", i, o, 1)
                after(dve, "out_act", i, o - 4, 1)
                scattered(dve, i, o - 4)
                v.tensor_copy(WC[:, o % 4:o % 4 + 1], WCA[:, index(i, o)])
                v.tensor_copy(ROWI[:, o % 4:o % 4 + 1], ROWA[:, index(i, o)]).then_inc(s["placed"], 1)

            def copy_xgt(i, o):
                after(dve, "t_done", i, o, 1)
                after(dve, "gu_done", i, o - 2, 1)
                v.tensor_copy(XGT[o % 2][:, 4:8, :], grid(banks[1][:, :], 4)).then_inc(s["xgt_dve"], 1)

            def hidden(i, o):
                after(dve, "sg_ready", i, o, 1)
                after(dve, "ht2_done", i, o - 1, 1)
                v.tensor_tensor(HID, SG, banks[2][:, 256:512], ALU.mult).then_inc(s["hid_ready"], 1)

            def scaled_out(i, o):
                place(i, o)
                after(dve, "placed", i, o, 1)
                after(dve, "dn_done", i, o, 1)
                scattered(dve, i, o - 4)
                v.tensor_scalar(OUT[o % 4][:, 512:1024], banks[5][:, :], WC[:, o % 4:o % 4 + 1], None,
                                ALU.mult).then_inc(s["out_dve"], 1)

            def find_further(b, n):
                e = further_of[0]
                for t in range(NT):
                    last = v.tensor_scalar(ONEHOTX[:, t, :], slots, float(P * b), PM[:, t, e], ALU.add, ALU.is_equal)
                last.then_inc(s["x_p"], 1)
                dve.wait_ge(s["x_idx"], n + 1)
                v.tensor_reduce(WCX, banks[7][:, 1:3], AX, ALU.add)
                v.tensor_tensor(IDXX, banks[7][:, 0:1], OFF, ALU.add).then_inc(s["x_idxr"], 1)

            def further(b, n):
                dve.wait_ge(s["x_sg"], n + 1)
                v.tensor_tensor(HIDX, SGX, banks[7][:, 256:512], ALU.mult).then_inc(s["x_hid"], 1)
                dve.wait_ge(s["x_sc"], 16 * n + 16)

            further_of = [None]

            def body(i, u):
                further_of[0] = index(i, u)
                block_ahead(dve, i, u, done, find_further)
                hidden(i, u)
                copy_xgt(i, u + 1)
                indices(i, u + 3)
                onehot(i, u + 4)
                if u or not isinstance(i, int):
                    scaled_out(i, u - 1)
                more_blocks(dve, i, u, done, find_further, further)

            onehot(0, 0)
            onehot(0, 1)
            indices(0, 0)
            onehot(0, 2)
            indices(0, 1)
            onehot(0, 3)
            indices(0, 2)
            for m in range(2):
                dve.wait_ge(s["sh_act"], m + 1)
                dve.wait_ge(s["sh_full"], m + 3)
                mark(v.tensor_tensor(SHT[:, m, :], SHT[:, m, :], banks[2 + m][:, :], ALU.mult), "sh_dve", m + 1)
            for t in range(NT):
                for j in range(2):
                    n = 2 * t + j
                    dve.wait_ge(s["f_full"], n + 1)
                    mark(v.tensor_copy(F[:, t, 512 * j:512 * (j + 1)], banks[n % 4][:, :]), "f_copied", n + 1)
            link(v.memset(XGX, 0.0))
            copy_xgt(0, 0)
            dve.wait_ge(s["acc_stored"], 16 * NT)
            over_experts(dve, body)
            scaled_out(NE // 4, -1)
            dve.wait_ge(s["f_sums"], NT)
            mark(v.tensor_scalar(SS[:, :], SS[:, :], 1.0 / D, EPS, ALU.mult, ALU.add), "f_mean", 1)
            dve.wait_ge(s["f_root"], 1)
            link(v.reciprocal(SS2[:, :], SS2[:, :]))
            for t in range(NT):
                t = NT - 1 - t
                v.scalar_tensor_tensor(out=F[:, t, :], in0=F[:, t, :], scalar=SS2[:, t:t + 1], in1=ROW[:, 3, :],
                                       op0=ALU.mult, op1=ALU.mult).then_inc(s["normed"], 1)
            for t in range(NT - 2, -1, -1):
                dve.wait_ge(s["normed"], NT - t)
                v.tensor_tensor(X[:, t, :], X[:, t, :], F[:, t, :], ALU.add).then_inc(s["added"], 1)

        @block.tensor
        def _(pe):
            mm = nc.tensor.matmul
            done = pe.alloc_register("further_blocks_pe")
            pe.reg_mov(done, 0)
            ring = mem["ring"]

            def unit(n):
                return ring[:, (n % RING) * UNIT:(n % RING + 1) * UNIT]

            pe.wait_ge(s["h2_ready"], NT)
            for k in range(KD):
                if k >= 4:
                    pe.wait_ge(s["ht_dve" if k % 2 else "ht_act"], (k - 4) // 2 + 1)
                for t in range(NT):
                    last = nc.tensor.transpose(banks[k % 4][:, t * P:(t + 1) * P], H2[:, t, k * P:(k + 1) * P], ident)
                last.then_inc(s["ht_full"], 1)
            pe.wait_ge(s["ht_act"], 4)
            pe.wait_ge(s["ht_dve"], 4)
            pe.wait_ge(s["wr_in"], 16)
            for t in range(NT):
                for k in range(KD):
                    last = mm(banks[4][:, NE * t:NE * (t + 1)], HT[:, k, t * P:(t + 1) * P], WR[:, k, :],
                              start=(k == 0), stop=(k == KD - 1))
            last.then_inc(s["logits_done"], 1)
            for m in range(4):
                n = LOADU[m // 2]
                unit_ready(pe, s_unit, n)
                w = unit(n).rearrange("p (k c) -> p k c", k=KD)
                for k in range(KD):
                    last = mm(banks[m][:, :], w[:, k, (m % 2) * P:(m % 2 + 1) * P], HT[:, k, :],
                              start=(k == 0), stop=(k == KD - 1))
                last.then_inc(s["sh_full"], 1)
            pe.wait_ge(s["mask_ready"], 1)
            for t in range(NT):
                o = banks[5][:, NE * t:NE * (t + 1)]
                mm(o, before, MSK[:, t, :], start=True, stop=(t == 0))
                for q in range(t):
                    mm(o, ONES, MSK[:, q, :], start=False, stop=(q == t - 1))
            for q in range(NT):
                last = mm(banks[6][:, 0:NE], ONES, MSK[:, q, :], start=(q == 0), stop=(q == NT - 1))
            last.then_inc(s["ranks_done"], 1)
            def find(i, o):
                after(pe, "onehot", i, o, 1)
                after(pe, "idx_ready", i, o - 1, 1)
                for t in range(NT):
                    last = mm(banks[6][:, 0:4], ONEHOT[o % 2][:, t, :],
                              R[:, t, index(i, o), :].rearrange("p a c -> p (a c)"),
                              start=(t == 0), stop=(t == NT - 1))
                last.then_inc(s["idx_done"], 1)

            def turn(i, o):
                pe.wait_ge(s_gath[o % 4], 16 * (o // 4 + 1) + 16 * i)
                after(pe, "xgt_act", i, o - 1, 1)
                after(pe, "xgt_dve", i, o - 1, 1)
                for k in range(KD):
                    last = nc.tensor.transpose(banks[k // 4][:, (k % 4) * P:(k % 4 + 1) * P],
                                               XG[o % 4][:, k * P:(k + 1) * P], ident)
                last.then_inc(s["t_done"], 1)

            def gate_up(i, o):
                after(pe, "xgt_act", i, o, 1)
                after(pe, "xgt_dve", i, o, 1)
                after(pe, "hid_ready", i, o - 1, 1)
                pe.wait_ge(s_exp[o % 4], 16 * (o // 4 + 1) + 16 * i)
                w = wslot[o % 4][:, 0:4096].rearrange("p (k c) -> p k c", k=KD)
                for k in range(KD):
                    last = mm(banks[2][:, :], XGT[o % 2][:, k, :], w[:, k, :], start=(k == 0), stop=(k == KD - 1))
                last.then_inc(s["gu_done"], 1)

            def turn_hidden(i, o):
                after(pe, "hid_ready", i, o, 1)
                after(pe, "hdt_ready", i, o - 1, 1)
                for k in range(2):
                    last = nc.tensor.transpose(banks[3][:, k * P:(k + 1) * P], HID[:, k * P:(k + 1) * P], ident)
                last.then_inc(s["ht2_done"], 1)

            def down(i, o):
                after(pe, "hdt_ready", i, o, 1)
                after(pe, "out_act", i, o - 1, 1)
                after(pe, "out_dve", i, o - 1, 1)
                w = wslot[o % 4][:, 4096:6144].rearrange("p (k c) -> p k c", k=2)
                for j in range(2):
                    for k in range(2):
                        last = mm(banks[4 + j][:, :], HDT[o % 2][:, k, :], w[:, k, 512 * j:512 * (j + 1)],
                                  start=(k == 0), stop=(k == 1))
                last.then_inc(s["dn_done"], 1)

            def find_further(b, n):
                i, u = further_of[0]
                pe.wait_ge(s["x_p"], n + 1)
                for t in range(NT):
                    last = mm(banks[7][:, 0:4], ONEHOTX[:, t, :], R[:, t, index(i, u), :].rearrange("p a c -> p (a c)"),
                              start=(t == 0), stop=(t == NT - 1))
                last.then_inc(s["x_idx"], 1)

            def further(b, n):
                i, u = further_of[0]
                pe.wait_ge(s["x_idxr"], n + 1)
                pe.wait_ge(s["x_gath"], 16 * n + 16)
                for h in range(2):
                    if h:
                        pe.wait_ge(s["x_e"], 2 * n + 1)
                    for k in range(4):
                        last = nc.tensor.transpose(banks[7][:, k * P:(k + 1) * P],
                                                   XGX[:, (4 * h + k) * P:(4 * h + k + 1) * P], ident)
                    last.then_inc(s["x_t"], 1)
                pe.wait_ge(s["x_e"], 2 * n + 2)
                w = wslot[u % 4][:, 0:4096].rearrange("p (k c) -> p k c", k=KD)
                for k in range(KD):
                    last = mm(banks[7][:, :], XGTX[:, k, :], w[:, k, :], start=(k == 0), stop=(k == KD - 1))
                last.then_inc(s["x_gu"], 1)
                pe.wait_ge(s["x_hid"], n + 1)
                for k in range(2):
                    last = nc.tensor.transpose(banks[7][:, k * P:(k + 1) * P], HIDX[:, k * P:(k + 1) * P], ident)
                last.then_inc(s["x_ht"], 1)
                pe.wait_ge(s["x_he"], n + 1)
                w = wslot[u % 4][:, 4096:6144].rearrange("p (k c) -> p k c", k=2)
                for j in range(2):
                    if j:
                        pe.wait_ge(s["x_o"], 2 * n + 1)
                    for k in range(2):
                        last = mm(banks[7][:, :], HDTX[:, k, :], w[:, k, 512 * j:512 * (j + 1)],
                                  start=(k == 0), stop=(k == 1))
                    last.then_inc(s["x_dn"], 1)
                pe.wait_ge(s["x_o"], 2 * n + 2)

            further_of = [None]

            def body(i, u):
                gate_up(i, u)
                further_of[0] = (i, u)
                block_ahead(pe, i, u, done, find_further)
                turn(i, u + 1)
                find(i, u + 3)
                if u or not isinstance(i, int):
                    down(i, u - 1)
                turn_hidden(i, u)
                more_blocks(pe, i, u, done, find_further, further)

            pe.wait_ge(s["tables_ready"], 1)
            pe.wait_ge(s["cnt_ready"], 1)
            find(0, 0)
            find(0, 1)
            find(0, 2)
            unit_ready(pe, s_unit, LOADU[2])
            pe.wait_ge(s["sh_dve"], 2)
            w = unit(LOADU[2]).rearrange("p (k c) -> p k c", k=2)
            for t in range(NT):
                for j in range(2):
                    n = 2 * t + j
                    if n >= 4:
                        pe.wait_ge(s["f_copied"], n - 3)
                    for k in range(2):
                        last = mm(banks[n % 4][:, :], SHT[:, k, t * P:(t + 1) * P], w[:, k, 512 * j:512 * (j + 1)],
                                  start=(k == 0), stop=(k == 1))
                    last.then_inc(s["f_full"], 1)
            pe.wait_ge(s["f_copied"], 8)
            turn(0, 0)
            over_experts(pe, body)
            down(NE // 4, -1)


UNITS2 = [("kv", 1), ("qa", 2), ("qr", 2), ("kr", 2), ("vr", 4), ("gr", 4),
          ("ga0", 2), ("YA0", 1), ("gb0", 2), ("YR0", 2), ("ga1", 2), ("YA1", 1), ("gb1", 2), ("YR1", 2),
          ("z", 4)]
FIRST2 = U_MIX + U_SHARED
FIRST3 = FIRST2 + sum(w for _, w in UNITS2)
HEADS, HDIM = 8, 64
RDK, RDV = 128, 256
FILL_ATT = [[("qr", c, tp) for c in range(2) for tp in range(2)], [("kr", c, tp) for c in range(2) for tp in range(2)],
            [("vr", c, tp) for c in range(2) for tp in range(2)], [("vr", c, tp) for c in range(2, 4) for tp in range(2)]]
FILL_RET = [[("gr", c, tp) for tp in range(2)] for c in range(4)]


def block2_items():
    it = Items()
    for k in range(KD):
        it.add(("xT", k), "dve" if k % 2 else "act")
    for tp in range(2):
        it.add(("kv", 0, tp), "act")
    for tp in range(2):
        for c in range(2):
            it.add(("qa", c, tp), "act")
    for p in range(4):
        it.add(("qaT", p), "dve")
    it.add(("kaT", 0), "dve")
    for n in range(NT):
        for key in FILL_ATT[n]:
            it.add(key, "act")
    for h in range(4):
        it.add(("qrT", h), "act")
    for h in range(4):
        it.add(("krT", h), "act")
    for n in range(NT):
        for key in FILL_RET[n]:
            it.add(key, "act")
    for m in range(4):
        it.add(("ga", m), "act")
    for k in range(KD):
        it.add(("rT", k), "dve" if k % 2 else "act")
    for j in range(2):
        for kind, by in (("ga", "act"), ("YA", "dve"), ("gb", "act"), ("YR", "dve")):
            for m in range(4):
                if (j, kind) != (0, "ga"):
                    it.add((kind, 4 * j + m), by)
    for tp in range(2):
        for c in range(4):
            it.add(("z", c, tp), "dve")
    return it


def block2(nc, sem, banks, mem, s_unit, stream, rows, const2):
    W = mem["work"]

    def part(first, width):
        assert first + width <= WORK
        return W[:, first:first + width]

    def grid(a, outer):
        return a.rearrange("p (a b) -> p a b", a=outer)

    X = grid(mem["X"][:, :], NT)
    HT = grid(mem["HT"][:, :], KD)
    ident = mem["const1"][:, 0:P]
    QA, QR, KV, KR = (grid(part(a, w), NT) for a, w in ((0, 2048), (2048, 2048), (4096, 1024), (5120, 2048)))
    VR, GR = grid(part(7168, 4096), NT), grid(part(11264, 4096), NT)
    XN = grid(part(11264, 4096), NT)
    qaT, kaT = grid(part(15360, 2048), 4), part(17408, 512)
    qrT, krT, attT = (grid(part(a, 2048), 4) for a in (17920, 19968, 22016))
    T0 = 24064
    SCR = grid(part(T0, 2048), 8)
    PT = part(T0 + 2048, 512).rearrange("p (a b q) -> p a b q", a=2, b=2)
    STATE, AR, QD, RO = grid(part(T0, 1024), 4), grid(part(T0 + 1024, 512), 4), grid(part(T0 + 1536, 512), 4), grid(
        part(T0 + 2048, 512), 2)
    small = [T0 + 2560]

    def tiny(width):
        small[0] += width
        return part(small[0] - width, width)

    MX, NM, ES, DEN, SINK = (tiny(8) for _ in range(5))
    SS, SS2, RS = tiny(4), tiny(4), tiny(4)
    BST, MV = tiny(24), tiny(8)
    yT, retT = grid(part(0, 4096), KD), grid(part(7168, 4096), KD)
    SG = grid(part(T0, 2048), 4)
    CONST, GAIN = mem["adarow"][:, 0:C2W], mem["adarow"][:, C2W:C2W + D]
    NORM = grid(part(0, 4096), NT)
    R1, R2 = mem["const1"][:, 256:768], mem["const1"][:, 768:1280]

    def col(name):
        a, w = PC[name]
        return mem["cols"][:, a:a + w]

    def con(name):
        a, w = C2[name]
        return CONST[:, a:a + w]

    it = block2_items()
    s_full, s_act, s_dve = sem("b2_full"), sem("b2_read_by_act"), sem("b2_read_by_dve")
    freed_by = {"act": s_act, "dve": s_dve}

    def bank_of(key):
        return banks[it.number[key] % NBANK]

    def bank_free(pe, key):
        n = it.number[key]
        if n >= NBANK:
            _, by, count = it.order[n - NBANK]
            pe.wait_ge(freed_by[by], count)

    def item_full(eng, key):
        eng.wait_ge(s_full, it.number[key] + 1)

    def item_read(key):
        _, by, count = it.order[it.number[key]]
        return freed_by[by], count

    names = ("const_in", "gain_in", "next_sums", "mean", "root", "xn_ready", "rot_a", "rot_q", "rot_k",
             "sc_done", "sc_read", "nm_ready", "exp_done", "p_ready", "pt_done", "pt_read", "av_done", "av_read",
             "ar_done", "ar_ready", "qd_ready", "kd_ready", "ro_done", "ro_read", "su_done", "state_ready", "gn_var",
             "gn_root", "gated", "summed", "dve_order", "es_ready")
    s = {n: sem("b2_" + n) for n in names}
    unit0, n0 = {}, FIRST2
    for name, width in UNITS2:
        unit0[name] = n0
        n0 += width
    uses = {}

    def use(name, keys):
        for i, key in enumerate(keys):
            uses[unit0[name] + i] = it.number[key] + 1

    for name, width in UNITS2[:6]:
        use(name, [(name, c, 1) for c in range(width)])
    for j in range(2):
        use(f"ga{j}", [("ga", 4 * j + 1), ("ga", 4 * j + 3)])
        use(f"YA{j}", [("YA", 4 * j + 3)])
        use(f"gb{j}", [("gb", 4 * j + 1), ("gb", 4 * j + 3)])
        use(f"YR{j}", [("YR", 4 * j + 1), ("YR", 4 * j + 3)])
    use("z", [("z", c, 1) for c in range(4)])

    with nc.Block() as block:

        @block.sync
        def _(sp):
            sp.dma_start(CONST, const2).then_inc(s["const_in"], 16)
            for name, dst in (("ret_gain", GAIN), ("sinks", SINK)):
                a, w = ROWS[name]
                sp.dma_start(dst, rows[0:1, a:a + w].to_broadcast([P, w])).then_inc(s["gain_in"], 16)
            for n in range(FIRST2 + RING, FIRST3 + RING):
                sp.wait_ge(s_full, uses[n - RING])
                sp.dma_start(mem["ring"][:, (n % RING) * UNIT:(n % RING + 1) * UNIT], stream[n]).then_inc(
                    s_unit[n % RING], 16)

        @block.scalar
        def _(act):
            act.wait_ge(s["mean"], 1)
            nc.scalar.activation(SS2[:, :], SS[:, :], ACT.Sqrt).then_inc(s["root"], 1)

            def turned(kind, gain):
                for k in range(0, KD, 2):
                    item_full(act, (kind, k))
                    nc.scalar.activation(HT[:, k, :], bank_of((kind, k))[:, :], ACT.Copy,
                                         scale=gain[:, k:k + 1]).then_inc(s_act, 1)

            turned("xT", col("nmix"))

            def copy_out(key):
                kind, c, tp = key
                item_full(act, key)
                b = grid(bank_of(key)[:, :], 2)
                if kind == "qa":
                    for a in range(2):
                        dst = QA[:, 2 * tp + a, :].rearrange("p (a v d) -> p a v d", a=4, v=2)[:, :, c, :]
                        last = nc.scalar.activation(dst, b[:, a, :].rearrange("p (a d) -> p a d", a=4), ACT.Copy)
                else:
                    dst = {"kv": KV, "qr": QR, "kr": KR, "vr": VR, "gr": GR}[kind]
                    last = nc.scalar.activation(dst[:, 2 * tp:2 * tp + 2, 256 * c:256 * (c + 1)], b,
                                                ACT.Silu if kind == "gr" else ACT.Copy)
                last.then_inc(s_act, 1)

            for tp in range(2):
                copy_out(("kv", 0, tp))
            for tp in range(2):
                for c in range(2):
                    copy_out(("qa", c, tp))
            for n in range(NT):
                lo = P if n == 0 else 0
                act.wait_ge(s["nm_ready"], n + 1)
                for h in range(HEADS):
                    last = nc.scalar.activation(SCR[:, h, lo:256], SCR[:, h, lo:256], ACT.Exp, bias=NM[:, h:h + 1],
                                                accum_out=DEN[:, h:h + 1])
                last.then_inc(s["exp_done"], 1)
                nc.scalar.activation(ES[:, :], ES[:, :], ACT.Exp).then_inc(s["es_ready"], 1)
                for q in range(4):
                    act.wait_ge(s["pt_done"], 4 * n + q + 1)
                    if 4 * n + q:
                        act.wait_ge(s["av_done"], 4 * n + q)
                    b = banks[6][:, :].rearrange("p (a b q) -> p a b q", a=2, b=2)
                    b0 = 1 if n == 0 else 0
                    nc.scalar.activation(PT[:, :, b0:2, :], b[:, :, b0:2, :], ACT.Copy).then_inc(s["pt_read"], 1)
                act.wait_ge(s["av_done"], 4 * n + 4)
                nc.scalar.activation(attT[:, :, n * P:(n + 1) * P], grid(banks[7][:, :], 4), ACT.Copy).then_inc(
                    s["av_read"], 1)
                for key in FILL_ATT[n]:
                    copy_out(key)
            for kind, dst in (("qrT", qrT), ("krT", krT)):
                for h in range(4):
                    item_full(act, (kind, h))
                    nc.scalar.activation(dst[:, h, :], bank_of((kind, h))[:, :], ACT.Copy).then_inc(s_act, 1)
            for n in range(NT):
                for key in FILL_RET[n]:
                    copy_out(key)
                act.wait_ge(s["gn_var"], n + 1)
                nc.scalar.activation(RS[:, :], RS[:, :], ACT.Sqrt).then_inc(s["gn_root"], 1)

            def sigmoids(w, kind, j):
                for q in range(4):
                    m = 4 * j + q
                    if w == 1:
                        act.wait_ge(*item_read(("YA", m)))
                    elif j == 1:
                        act.wait_ge(s["summed"], q + 1)
                    item_full(act, (kind, m))
                    nc.scalar.activation(SG[:, q, :], bank_of((kind, m))[:, :], ACT.Sigmoid,
                                         bias=col("bg")[:, 8 * w + m:8 * w + m + 1]).then_inc(s_act, 1)

            sigmoids(0, "ga", 0)
            for k in range(0, KD, 2):
                item_full(act, ("rT", k))
                nc.scalar.activation(retT[:, k, :], bank_of(("rT", k))[:, :], ACT.Copy).then_inc(s_act, 1)
            sigmoids(1, "gb", 0)
            sigmoids(0, "ga", 1)
            sigmoids(1, "gb", 1)
            for t in range(NT):
                act.wait_ge(*item_read(("z", 3, t // 2)))
                nc.scalar.activation(SG.rearrange("p a b -> p (a b)")[:, 0:D], X[:, t, :], ACT.Square,
                                     accum_out=mem["sums"][:, t:t + 1]).then_inc(s["next_sums"], 1)
                act.wait_ge(s["next_sums"], t + 1)

        @block.vector
        def _(dve):
            v = nc.vector
            order = [0]

            def link(ins):
                order[0] += 1
                ins.then_inc(s["dve_order"], 1)
                dve.wait_ge(s["dve_order"], order[0])

            def mark(ins, name, count):
                ins.then_inc(s[name], 1)
                dve.wait_ge(s[name], count)

            def turned(kind, gain):
                for k in range(1, KD, 2):
                    item_full(dve, (kind, k))
                    v.tensor_scalar(HT[:, k, :], bank_of((kind, k))[:, :], gain[:, k:k + 1], None, ALU.mult).then_inc(
                        s_dve, 1)

            mark(v.tensor_scalar(SS[:, :], mem["sums"][:, :], 1.0 / D, EPS, ALU.mult, ALU.add), "mean", 1)
            dve.wait_ge(s["root"], 1)
            link(v.reciprocal(SS2[:, :], SS2[:, :]))
            for t in range(NT):
                mark(v.tensor_scalar(XN[:, t, :], X[:, t, :], SS2[:, t:t + 1], None, ALU.mult), "xn_ready", t + 1)
            turned("xT", col("nmix"))

            def rotate(x, cos, sin, name, count):
                nh, w = x.shape[1], x.shape[2] // 2
                x = x.rearrange("p n (s d) -> p n s d", s=2)
                a = R1[:, 0:nh * 2 * w].rearrange("p (n s d) -> p n s d", n=nh, s=2)
                b = R2[:, 0:nh * 2 * w].rearrange("p (n s d) -> p n s d", n=nh, s=2)
                for q in range(2):
                    c = cos.rearrange("p (a d) -> p a d", a=1).to_broadcast([P, nh, w])
                    n_ = sin.rearrange("p (a d) -> p a d", a=1).to_broadcast([P, nh, w])
                    v.tensor_tensor(a[:, :, q, :], x[:, :, q, :], c, ALU.mult)
                    last = v.tensor_tensor(b[:, :, q, :], x[:, :, 1 - q, :], n_, ALU.mult)
                link(last)
                link(v.tensor_tensor(x[:, :, 0, :], a[:, :, 0, :], b[:, :, 0, :], ALU.subtract))
                mark(v.tensor_tensor(x[:, :, 1, :], a[:, :, 1, :], b[:, :, 1, :], ALU.add), name, count)

            dve.wait_ge(s["const_in"], 16)
            dve.wait_ge(s["gain_in"], 32)
            angles = [(grid(con("acos"), 4)[:, t, :], grid(con("asin"), 4)[:, t, :]) for t in range(NT)]
            dve.wait_ge(*item_read(("kv", 0, 1)))
            for t in range(NT):
                rotate(grid(KV[:, t, 0:P], 2)[:, :, 0:16], *angles[t], "rot_a", t + 1)
            for t in range(NT):
                dve.wait_ge(*item_read(("qa", 1, t // 2)))
                rotate(grid(QA[:, t, :], HEADS)[:, :, 0:16], *angles[t], "rot_a", NT + t + 1)
            for p in range(4):
                item_full(dve, ("qaT", p))
                v.tensor_copy(qaT[:, p, :], bank_of(("qaT", p))[:, :]).then_inc(s_dve, 1)
            item_full(dve, ("kaT", 0))
            v.tensor_copy(kaT, bank_of(("kaT", 0))[:, :]).then_inc(s_dve, 1)
            win = con("win")
            for n in range(NT):
                lo = P if n == 0 else 0
                for q in range(4):
                    dve.wait_ge(s["sc_done"], 4 * n + q + 1)
                    if q == 0 and n:
                        dve.wait_ge(s["pt_done"], 4 * n)
                    b = grid(banks[4 + q % 2][:, :], 2)
                    mark(v.scalar_tensor_tensor(
                        out=SCR[:, 2 * q:2 * q + 2, lo:256], in0=b[:, :, lo:256], scalar=float(HDIM) ** -0.5,
                        in1=win[:, lo:256].rearrange("p (a k) -> p a k", a=1).to_broadcast([P, 2, 256 - lo]),
                        op0=ALU.mult, op1=ALU.add), "sc_read", 4 * n + q + 1)
                link(v.tensor_reduce(MX[:, :], SCR[:, :, lo:256], AX, ALU.max))
                link(v.tensor_tensor(MX[:, :], MX[:, :], SINK, ALU.max))
                link(v.tensor_scalar(NM[:, :], MX[:, :], -1.0, None, ALU.mult))
                mark(v.tensor_tensor(ES[:, :], SINK, NM[:, :], ALU.add), "nm_ready", n + 1)
                dve.wait_ge(s["es_ready"], n + 1)
                link(v.tensor_tensor(DEN[:, :], DEN[:, :], ES[:, :], ALU.add))
                link(v.reciprocal(DEN[:, :], DEN[:, :]))
                for h in range(HEADS):
                    ins = v.tensor_scalar(SCR[:, h, lo:256], SCR[:, h, lo:256], DEN[:, h:h + 1], None, ALU.mult)
                mark(ins, "p_ready", n + 1)
                if n >= 1:
                    dst, name = ((QR, "rot_q"), (KR, "rot_k"))[n - 1] if n < 3 else (None, None)
                    if dst is not None:
                        kind = "qr" if n == 1 else "kr"
                        dve.wait_ge(*item_read((kind, 1, 1)))
                        for t in range(NT):
                            c_, s_ = ("qcos", "qsin") if n == 1 else ("kcos", "ksin")
                            rotate(grid(dst[:, t, :], 4), grid(con(c_), 4)[:, t, :], grid(con(s_), 4)[:, t, :],
                                   name, t + 1)
            for t in range(NT):
                for h in range(HG):
                    if t == 0 and h == 0:
                        item_full(dve, ("krT", 3))
                    last = v.tensor_scalar(KR[:, t, h * P:(h + 1) * P], KR[:, t, h * P:(h + 1) * P],
                                           con("kdec")[:, h:h + 1], None, ALU.mult)
                mark(last, "kd_ready", t + 1)
            dve.wait_ge(*item_read(("qrT", 3)))
            for n in range(NT):
                if n:
                    dve.wait_ge(s["ro_done"], 2 * n)
                    mark(v.tensor_tensor(QD, qrT[:, :, n * P:(n + 1) * P], grid(con("qdec"), 4), ALU.mult), "qd_ready", n)
                else:
                    dve.wait_ge(s["av_done"], 16)
                dve.wait_ge(s["ar_done"], n + 1)
                mark(v.tensor_tensor(AR, grid(banks[4][:, :], 4), grid(con("intra"), 4), ALU.mult), "ar_ready", n + 1)
                if n < NT - 1:
                    for q in range(2):
                        dve.wait_ge(s["su_done"], 2 * n + q + 1)
                        b = grid(banks[7][:, :], 2)
                        if n == 0:
                            mark(v.tensor_copy(STATE[:, 2 * q:2 * q + 2, :], b), "state_ready", 2 * n + q + 1)
                        else:
                            if q == 0:
                                dve.wait_ge(s["ro_done"], 2 * n + 2)
                            for a in range(2):
                                h = 2 * q + a
                                last = v.scalar_tensor_tensor(
                                    out=STATE[:, h, :], in0=STATE[:, h, :], scalar=CHUNK_DECAY[h], in1=b[:, a, :],
                                    op0=ALU.mult, op1=ALU.add)
                            mark(last, "state_ready", 2 * n + q + 1)
                dve.wait_ge(s["ro_done"], 2 * n + 2)
                for h in range(HG):
                    src = banks[5 + h // 2][:, 256 * (h % 2):256 * (h % 2 + 1)]
                    link(v.bn_stats(BST[:, 6 * h:6 * h + 6], src))
                    link(v.bn_aggr(MV[:, 2 * h:2 * h + 2], BST[:, 6 * h:6 * h + 6]))
                mark(v.tensor_scalar(RS[:, :], grid(MV[:, :], 4)[:, :, 1], EPS, None, ALU.add), "gn_var", n + 1)
                dve.wait_ge(s["gn_root"], n + 1)
                link(v.reciprocal(RS[:, :], RS[:, :]))
                dve.wait_ge(*item_read(("gr", 3, 1)) if n == NT - 1 else item_read(("gr", n, 1)))
                for q in range(2):
                    for a in range(2):
                        h = 2 * q + a
                        ins = v.tensor_scalar(RO[:, a, :], banks[5 + q][:, 256 * a:256 * (a + 1)],
                                              MV[:, 2 * h:2 * h + 1], RS[:, h:h + 1], ALU.subtract, ALU.mult)
                        link(ins) if a == 0 else mark(ins, "ro_read", 2 * n + q + 1)
                    ro = RO.rearrange("p a b -> p (a b)")
                    mark(v.tensor_tensor(NORM[:, n, 512 * q:512 * (q + 1)], ro, GAIN[:, 512 * q:512 * (q + 1)], ALU.mult),
                         "gated", 2 * n + q + 1)
            dve.wait_ge(*item_read(("gr", 3, 1)))
            for t in range(NT):
                mark(v.tensor_tensor(GR[:, t, :], GR[:, t, :], NORM[:, t, :], ALU.mult), "gated", 2 * NT + t + 1)
            for k in range(1, KD, 2):
                item_full(dve, ("rT", k))
                v.tensor_copy(retT[:, k, :], bank_of(("rT", k))[:, :]).then_inc(s_dve, 1)
            for j in range(2):
                for w, (kind, gate) in enumerate((("YA", "ga"), ("YR", "gb"))):
                    for q in range(4):
                        m = 4 * j + q
                        dve.wait_ge(*item_read((gate, m)))
                        item_full(dve, (kind, m))
                        dst = yT[:, m, :] if w == 0 else SG[:, q, :]
                        v.tensor_tensor(dst, SG[:, q, :], bank_of((kind, m))[:, :], ALU.mult).then_inc(s_dve, 1)
                        dve.wait_ge(*item_read((kind, m)))
                        if w == 1:
                            mark(v.tensor_tensor(yT[:, m, :], yT[:, m, :], SG[:, q, :], ALU.add), "summed", m + 1)
            for tp in range(2):
                for c in range(4):
                    key = ("z", c, tp)
                    item_full(dve, key)
                    dst = X[:, 2 * tp:2 * tp + 2, 256 * c:256 * (c + 1)]
                    v.tensor_tensor(dst, dst, grid(bank_of(key)[:, :], 2), ALU.add).then_inc(s_dve, 1)

        @block.tensor
        def _(pe):
            mm = nc.tensor.matmul
            ring = mem["ring"]

            def unit(n, chunks):
                unit_ready(pe, s_unit, n)
                return ring[:, (n % RING) * UNIT:(n % RING + 1) * UNIT].rearrange("p (k c) -> p k c", k=chunks)

            def features(n, key, half, src):
                w = unit(n, KD)
                bank_free(pe, key)
                for k in range(KD):
                    last = mm(bank_of(key)[:, :], w[:, k, half * P:(half + 1) * P], src[:, k, :],
                              start=(k == 0), stop=(k == KD - 1))
                last.then_inc(s_full, 1)

            def tokens(n, key, tp, src):
                w = unit(n, KD)
                bank_free(pe, key)
                for a in range(2):
                    for k in range(KD):
                        last = mm(bank_of(key)[:, 256 * a:256 * (a + 1)], src[:, k, (2 * tp + a) * P:(2 * tp + a + 1) * P],
                                  w[:, k, :], start=(k == 0), stop=(k == KD - 1))
                last.then_inc(s_full, 1)

            def turn(key, blocks_):
                bank_free(pe, key)
                for t in range(NT):
                    last = nc.tensor.transpose(bank_of(key)[:, t * P:(t + 1) * P], blocks_(t), ident)
                last.then_inc(s_full, 1)

            def turned_in(kind):
                pe.wait_ge(*item_read((kind, 6)))
                pe.wait_ge(*item_read((kind, 7)))

            pe.wait_ge(s["xn_ready"], NT)
            for k in range(KD):
                turn(("xT", k), lambda t: XN[:, t, k * P:(k + 1) * P])
            turned_in("xT")
            for tp in range(2):
                tokens(unit0["kv"], ("kv", 0, tp), tp, HT)
            for tp in range(2):
                for c in range(2):
                    tokens(unit0["qa"] + c, ("qa", c, tp), tp, HT)
            pe.wait_ge(s["rot_a"], 2 * NT)
            for p in range(4):
                turn(("qaT", p), lambda t: QA[:, t, p * P:(p + 1) * P])
            turn(("kaT", 0), lambda t: KV[:, t, 0:P])
            pe.wait_ge(*item_read(("kaT", 0)))
            for n in range(NT):
                lo = P if n == 0 else 0
                for q in range(4):
                    if 4 * n + q >= 2:
                        pe.wait_ge(s["sc_read"], 4 * n + q - 1)
                    for a in range(2):
                        h = 2 * q + a
                        g, r0 = h % 4, HDIM * (h // 4)
                        last = mm(banks[4 + q % 2][:, 256 * a + lo:256 * (a + 1)],
                                  qaT[r0:r0 + HDIM, g, n * P:(n + 1) * P],
                                  kaT[r0:r0 + HDIM, (n - 1) * P + lo:(n + 1) * P], start=True, stop=True)
                    last.then_inc(s["sc_done"], 1)
                fill = FILL_ATT[n]
                tokens(unit0[fill[0][0]] + fill[0][1], fill[0], fill[0][2], HT)
                tokens(unit0[fill[1][0]] + fill[1][1], fill[1], fill[1][2], HT)
                pe.wait_ge(s["p_ready"], n + 1)
                for q in range(4):
                    if 4 * n + q:
                        pe.wait_ge(s["pt_read"], 4 * n + q)
                    for a in range(2):
                        for b in range(1 if n == 0 else 0, 2):
                            last = nc.tensor.transpose(banks[6][:, (2 * a + b) * P:(2 * a + b + 1) * P],
                                                       SCR[:, 2 * q + a, b * P:(b + 1) * P], ident)
                    last.then_inc(s["pt_done"], 1)
                    if q == 0 and n:
                        pe.wait_ge(s["av_read"], n)
                    pe.wait_ge(s["pt_read"], 4 * n + q + 1)
                    for a in range(2):
                        h = 2 * q + a
                        vcol = P + HDIM * (h // 4)
                        for b in range(1 if n == 0 else 0, 2):
                            last = mm(banks[7][HDIM * a:HDIM * (a + 1), q * P:(q + 1) * P],
                                      KV[:, n - 1 + b, vcol:vcol + HDIM], PT[:, a, b, :],
                                      start=(b == (1 if n == 0 else 0)), stop=(b == 1))
                    last.then_inc(s["av_done"], 1)
                for key in fill[2:]:
                    tokens(unit0[key[0]] + key[1], key, key[2], HT)
            pe.wait_ge(s["rot_q"], NT)
            for h in range(4):
                turn(("qrT", h), lambda t: QR[:, t, h * P:(h + 1) * P])
            pe.wait_ge(s["rot_k"], NT)
            for h in range(4):
                turn(("krT", h), lambda t: KR[:, t, h * P:(h + 1) * P])
            pe.wait_ge(*item_read(("krT", 3)))
            for n in range(NT):
                if n:
                    pe.wait_ge(s["ar_ready"], n)
                for h in range(HG):
                    last = mm(banks[4][:, h * P:(h + 1) * P], krT[:, h, n * P:(n + 1) * P], qrT[:, h, n * P:(n + 1) * P],
                              start=True, stop=True)
                last.then_inc(s["ar_done"], 1)
                tokens(unit0["gr"] + FILL_RET[n][0][1], FILL_RET[n][0], 0, HT)
                pe.wait_ge(s["ar_ready"], n + 1)
                if n:
                    pe.wait_ge(s["qd_ready"], n)
                    pe.wait_ge(s["state_ready"], 2 * n)
                for q in range(2):
                    if n:
                        pe.wait_ge(s["ro_read"], 2 * n - 1 + q)
                    for a in range(2):
                        h = 2 * q + a
                        o = banks[5 + q][:, 256 * a:256 * (a + 1)]
                        last = mm(o, AR[:, h, :], VR[:, n, RDV * h:RDV * (h + 1)], start=True, stop=(n == 0))
                        if n:
                            last = mm(o, QD[:, h, :], STATE[:, h, :], start=False, stop=True)
                    last.then_inc(s["ro_done"], 1)
                if n < NT - 1:
                    pe.wait_ge(s["kd_ready"], n + 1)
                    for q in range(2):
                        if 2 * n + q:
                            pe.wait_ge(s["state_ready"], 2 * n + q)
                        for a in range(2):
                            h = 2 * q + a
                            last = mm(banks[7][:, 256 * a:256 * (a + 1)], KR[:, n, h * P:(h + 1) * P],
                                      VR[:, n, RDV * h:RDV * (h + 1)], start=True, stop=True)
                        last.then_inc(s["su_done"], 1)
                tokens(unit0["gr"] + FILL_RET[n][1][1], FILL_RET[n][1], 1, HT)
            for q in range(4):
                features(unit0["ga0"] + q // 2, ("ga", q), q % 2, HT)
            pe.wait_ge(s["gated"], 3 * NT)
            for k in range(KD):
                turn(("rT", k), lambda t: GR[:, t, k * P:(k + 1) * P])
            for j in range(2):
                for kind in ("YA", "gb", "YR") if j == 0 else ("ga", "YA", "gb", "YR"):
                    for q in range(4):
                        key = (kind, 4 * j + q)
                        if kind == "YA":
                            w = unit(unit0[f"YA{j}"], 4)
                            bank_free(pe, key)
                            for k in range(4):
                                last = mm(bank_of(key)[:, :], w[:, k, q * P:(q + 1) * P], attT[:, k, :],
                                          start=(k == 0), stop=(k == 3))
                            last.then_inc(s_full, 1)
                        else:
                            if key == ("YR", 0):
                                turned_in("rT")
                            features(unit0[f"{kind}{j}"] + q // 2, key, q % 2, retT if kind == "YR" else HT)
            pe.wait_ge(s["summed"], KD)
            for tp in range(2):
                for c in range(4):
                    tokens(unit0["z"] + c, ("z", c, tp), tp, yT)


def mlp(nc, sem, banks, mem, s_unit, stream, rows, out):
    with ExitStack() as es:
        def alloc(name, width, dt=F32R):
            return es.enter_context(nc.sbuf_tensor(name, [P, width], dt))

        def grid(a, outer):
            return a.rearrange("p (a b) -> p a b", a=outer)

        X = grid(mem["X"][:, :], NT)
        ident, DIAG = mem["const1"][:, 0:P], grid(mem["const1"][:, 256:768], NT)
        RELU = [mem["const1"][:, 256 + 512 * k:768 + 512 * k] for k in range(2)]
        gain = mem["cols"][:, PC["nmlp"][0]:PC["nmlp"][0] + KD]
        HH, HL = (grid(alloc(f"h_{n}", KD * TOK)[:, :], KD) for n in ("high", "rest"))
        UH, UL = (grid(alloc(f"hidden_{n}", 16 * TOK)[:, :], 16) for n in ("high", "rest"))
        WH, WL = ([alloc(f"w_{n}{k}", UNIT)[:, :].rearrange("p (k c) -> p k c", k=KD) for k in range(2)]
                  for n in ("high", "rest"))
        tmp = alloc("tmp", 1024, F32)
        TMP, JUNK = [tmp[:, 512 * k:512 * (k + 1)] for k in range(2)], tmp[:, :]
        FINAL = alloc("final_gain", D, F32)[:, :]
        small = alloc("small", 16, F32)
        SS, SS2, RS = small[:, 0:4], small[:, 4:8], small[:, 8:12]
        names = ("final_in", "mean", "root", "diag_ready", "t_full", "value", "high", "rest", "relu_ready",
                 "w_high", "w_rest", "f1_full", "f2_full", "added", "fin_sums", "fin_mean", "fin_root",
                 "out_ready", "out_stored", "dve_order")
        s = {n: sem("mlp_" + n) for n in names}
        NU = 32

        def raw(u):
            n = FIRST3 + u
            return mem["ring"][:, (n % RING) * UNIT:(n % RING + 1) * UNIT].rearrange("p (k c) -> p k c", k=KD)

        def unit_used(eng, u):
            h, i = divmod(u, 16)
            if i < 8:
                eng.wait_ge(s["f1_full"], 16 * h + 2 * i + 2)
            else:
                eng.wait_ge(s["f2_full"], 8 * h + i - 7)

        with nc.Block() as block:

            @block.sync
            def _(sp):
                a, w = ROWS["norm_final"]
                sp.dma_start(FINAL, rows[0:1, a:a + w].to_broadcast([P, w])).then_inc(s["final_in"], 16)
                for u in range(RING, NU):
                    sp.wait_ge(s["w_rest"], u - RING + 1)
                    n = FIRST3 + u
                    sp.dma_start(mem["ring"][:, (n % RING) * UNIT:(n % RING + 1) * UNIT], stream[n]).then_inc(
                        s_unit[n % RING], 16)
                for t in range(NT):
                    sp.wait_ge(s["out_ready"], t + 1)
                    sp.dma_start(out[t * P:(t + 1) * P, :], X[:, t, :]).then_inc(s["out_stored"], 16)
                sp.wait_ge(s["out_stored"], 16 * NT)

            @block.scalar
            def _(act):
                def w_high(u):
                    unit_ready(act, s_unit, FIRST3 + u)
                    if u >= 2:
                        unit_used(act, u - 2)
                    nc.scalar.activation(WH[u % 2], raw(u), ACT.Copy).then_inc(s["w_high"], 1)

                def high(n, dst):
                    act.wait_ge(s["value"], n + 1)
                    nc.scalar.activation(dst, TMP[n % 2], ACT.Copy).then_inc(s["high"], 1)

                act.wait_ge(s["mean"], 1)
                nc.scalar.activation(SS2, SS, ACT.Sqrt).then_inc(s["root"], 1)
                w_high(0)
                w_high(1)
                for k in range(KD):
                    high(k, HH[:, k, :])
                for u in range(NU):
                    h, i = divmod(u, 16)
                    if i < 8:
                        for j in (2 * i, 2 * i + 1):
                            act.wait_ge(s["f1_full"], 16 * h + j + 1)
                            if 16 * h + j >= 2:
                                act.wait_ge(s["value"], KD + 16 * h + j - 1)
                            nc.scalar.activation(RELU[j % 2], banks[j % 4][:, :], ACT.Relu).then_inc(s["relu_ready"], 1)
                            high(KD + 16 * h + j, UH[:, j, :])
                    if u + 2 < NU:
                        w_high(u + 2)
                act.wait_ge(s["added"], 32)
                for t in range(NT):
                    nc.scalar.activation(JUNK, X[:, t, :], ACT.Square, accum_out=SS[:, t:t + 1]).then_inc(
                        s["fin_sums"], 1)
                    act.wait_ge(s["fin_sums"], t + 1)
                act.wait_ge(s["fin_mean"], 1)
                nc.scalar.activation(SS2, SS, ACT.Sqrt).then_inc(s["fin_root"], 1)

            @block.vector
            def _(dve):
                v = nc.vector
                order = [0]

                def link(ins):
                    order[0] += 1
                    ins.then_inc(s["dve_order"], 1)
                    dve.wait_ge(s["dve_order"], order[0])

                def mark(ins, name, count):
                    ins.then_inc(s[name], 1)
                    dve.wait_ge(s[name], count)

                def rstd(sums, mean, root):
                    mark(v.tensor_scalar(SS, sums, 1.0 / D, EPS, ALU.mult, ALU.add), mean, 1)
                    dve.wait_ge(s[root], 1)
                    link(v.reciprocal(RS, SS2))

                def rest(n, dst, hi):
                    dve.wait_ge(s["high"], n + 1)
                    v.tensor_tensor(dst, TMP[n % 2], hi, ALU.subtract).then_inc(s["rest"], 1)

                def w_rest(u):
                    dve.wait_ge(s["w_high"], u + 1)
                    v.tensor_tensor(WL[u % 2], raw(u), WH[u % 2], ALU.subtract).then_inc(s["w_rest"], 1)

                def tmp_free(n):
                    if n >= 2:
                        dve.wait_ge(s["rest"], n - 1)

                rstd(mem["sums"][:, :], "mean", "root")
                for t in range(NT):
                    last = v.tensor_scalar(DIAG[:, t, :], ident, RS[:, t:t + 1], None, ALU.mult)
                last.then_inc(s["diag_ready"], 1)
                w_rest(0)
                w_rest(1)
                for k in range(KD):
                    dve.wait_ge(s["t_full"], k + 1)
                    tmp_free(k)
                    v.tensor_scalar(TMP[k % 2], banks[4 + k % 4][:, :], gain[:, k:k + 1], None, ALU.mult).then_inc(
                        s["value"], 1)
                    if k:
                        rest(k - 1, HL[:, k - 1, :], HH[:, k - 1, :])
                rest(KD - 1, HL[:, KD - 1, :], HH[:, KD - 1, :])
                for u in range(NU):
                    h, i = divmod(u, 16)
                    if i < 8:
                        for j in (2 * i, 2 * i + 1):
                            n = KD + 16 * h + j
                            dve.wait_ge(s["relu_ready"], 16 * h + j + 1)
                            tmp_free(n)
                            v.tensor_tensor(TMP[n % 2], RELU[j % 2], RELU[j % 2], ALU.mult).then_inc(s["value"], 1)
                            rest(n, UL[:, j, :], UH[:, j, :])
                    if u + 2 < NU:
                        w_rest(u + 2)
                    if i >= 8 and i % 2:
                        c = (i - 8) // 2
                        dve.wait_ge(s["f2_full"], 8 * h + 2 * c + 2)
                        for t in range(NT):
                            dst = X[:, t, 256 * c:256 * (c + 1)]
                            mark(v.tensor_tensor(dst, dst, banks[4 * ((c + 1) % 2) + t][:, 0:256], ALU.add), "added",
                                 16 * h + 4 * c + t + 1)
                dve.wait_ge(s["fin_sums"], NT)
                rstd(SS, "fin_mean", "fin_root")
                dve.wait_ge(s["final_in"], 16)
                for t in range(NT):
                    v.scalar_tensor_tensor(out=X[:, t, :], in0=X[:, t, :], scalar=RS[:, t:t + 1], in1=FINAL,
                                           op0=ALU.mult, op1=ALU.mult).then_inc(s["out_ready"], 1)

            @block.tensor
            def _(pe):
                mm = nc.tensor.matmul

                def product(bank, w, h, first, final):
                    for i, (a, b) in enumerate(((w[0], h[0]), (w[0], h[1]), (w[1], h[0]))):
                        ins = mm(bank, a, b, start=(first and i == 0), stop=(final and i == 2))
                    return ins

                pe.wait_ge(s["diag_ready"], 1)
                for k in range(KD):
                    if k >= 4:
                        pe.wait_ge(s["value"], k - 3)
                    for t in range(NT):
                        last = mm(banks[4 + k % 4][:, t * P:(t + 1) * P], X[:, t, k * P:(k + 1) * P], DIAG[:, t, :],
                                  start=True, stop=True)
                    last.then_inc(s["t_full"], 1)
                for h in range(2):
                    for j in range(16):
                        u = 16 * h + j // 2
                        if j % 2 == 0:
                            pe.wait_ge(s["w_rest"], u + 1)
                        if j >= 4:
                            pe.wait_ge(s["relu_ready"], 16 * h + j - 3)
                        elif h:
                            pe.wait_ge(s["added"], 12 + j + 1)
                        cols = slice((j % 2) * P, (j % 2 + 1) * P)
                        for k in range(KD):
                            if u == 0 and j == 0:
                                pe.wait_ge(s["rest"], k + 1)
                            last = product(banks[j % 4][:, :], (WH[u % 2][:, k, cols], WL[u % 2][:, k, cols]),
                                           (HH[:, k, :], HL[:, k, :]), k == 0, k == KD - 1)
                        last.then_inc(s["f1_full"], 1)
                    for c in range(4):
                        for kk in range(2):
                            u = 16 * h + 8 + 2 * c + kk
                            pe.wait_ge(s["w_rest"], u + 1)
                            pe.wait_ge(s["rest"], KD + 16 * h + 8 * (kk + 1))
                            if kk == 0 and c == 0 and h == 1:
                                pe.wait_ge(s["added"], 12)
                            if kk == 0 and c == 1:
                                pe.wait_ge(s["relu_ready"], 16 * (h + 1))
                            if kk == 0 and c >= 2:
                                pe.wait_ge(s["added"], 16 * h + 4 * (c - 1))
                            for t in range(NT):
                                tok = slice(t * P, (t + 1) * P)
                                for k in range(KD):
                                    hk = KD * kk + k
                                    last = product(banks[4 * ((c + 1) % 2) + t][:, 0:256],
                                                   (UH[:, hk, tok], UL[:, hk, tok]),
                                                   (WH[u % 2][:, k, :], WL[u % 2][:, k, :]),
                                                   kk == 0 and k == 0, kk == 1 and k == KD - 1)
                            last.then_inc(s["f2_full"], 1)


def _units(w):
    k, n = w.shape
    return w.reshape(k // P, P, n // 256, 256).transpose(2, 1, 0, 3).reshape(-1, P, UNIT)


def _half_units(w):
    k, n = w.shape
    return w.reshape(4, P, n // 512, 512).transpose(2, 1, 0, 3).reshape(-1, P, UNIT)


def _mixer_stream(i):
    w_in, w_ada = i["w_in"][0], i["w_ada"][0]
    cut = lambda a, b: _units(w_in[:, a:b])
    parts = [_units(w_ada[:, 0:2048]), cut(0, 512), cut(512, 1024), cut(1536, 2048), cut(2048, 2560),
             cut(2560, 3072), cut(3072, 3584), cut(1024, 1536), _units(w_ada[:, 2048:])]
    a, b = _half_units(i["w_branch_a"][0]), _half_units(i["w_branch_b"][0])
    for j in range(2):
        parts += [cut(3584 + 512 * j, 4096 + 512 * j), a[j:j + 1], cut(4608 + 512 * j, 5120 + 512 * j), b[j:j + 1]]
    parts.append(_units(i["w_out"][0]))
    parts.append(_units(i["w_shared_gu"][0]))
    parts.append(i["w_shared_down"][0].reshape(2, P, D).transpose(1, 0, 2).reshape(1, P, 2 * D))
    return parts


def _block2_stream(i):
    w = i["w_in_2"][0]
    edges = [0, 512, 768, 1280, 1792, 2816, 3840, 4352, 4864, 5376, 5888]
    qa, kv, qr, kr, vr, gr, ga0, ga1, gb0, gb1 = (_units(w[:, a:b]) for a, b in zip(edges, edges[1:]))
    ya, yr = _half_units(i["w_att_up_2"][0]), _units(i["w_ret_up_2"][0])
    parts = [kv, qa, qr, kr, vr, gr, ga0, ya[0:1], gb0, yr[0:2], ga1, ya[1:2], gb1, yr[2:4],
             _units(i["w_out_2"][0])]
    ff1 = _units(i["w_ff1_2"][0])
    ff2 = i["w_ff2_2"][0].reshape(4, KD, P, 4, 256).transpose(3, 0, 2, 1, 4).reshape(4, 4, P, UNIT)
    for h in range(2):
        parts += [ff1[8 * h:8 * h + 8], ff2[:, 2 * h:2 * h + 2].reshape(8, P, UNIT)]
    return parts


def _const2():
    f = np.float32
    pos = np.arange(TOK, dtype=f)

    def table(dim, theta):
        inv = np.power(f(theta), -np.arange(0, dim, 2, dtype=f) / f(dim)).astype(f)
        ang = pos[:, None] * inv[None, :]
        lay = lambda a: a.astype(f).reshape(NT, P, -1).transpose(1, 0, 2).reshape(P, -1)
        return lay(np.cos(ang)), lay(np.sin(ang))

    ac, as_ = table(16, 500000.0)
    rc, rs = table(RDK, 10000.0)
    lg = np.log1p(-np.exp2(f(-5.0) - np.arange(4, dtype=f))).astype(f)
    idx = np.arange(P, dtype=f)
    delta = idx[:, None] + P - np.arange(2 * P, dtype=f)[None, :]
    diff = idx[None, :] - idx[:, None]
    intra = np.where(diff[:, None, :] >= 0, np.exp(np.maximum(diff, 0)[:, None, :] * lg[None, :, None]), 0)
    parts = {
        "acos": ac, "asin": as_, "qcos": rc, "qsin": rs, "kcos": rc * f(RDK ** -0.5), "ksin": rs * f(RDK ** -0.5),
        "win": np.where((delta >= 0) & (delta < P), 0, NEG),
        "intra": intra.reshape(P, 4 * P),
        "qdec": np.tile(np.exp((idx + 1)[None, :] * lg[:, None]).reshape(1, 4 * P), (P, 1)),
        "kdec": np.exp((P - 1 - idx)[:, None] * lg[None, :]), "pad": np.zeros((P, 4)),
    }
    return np.concatenate([np.asarray(parts[k], np.float32) for k in C2], axis=1)


def _columns(v, n):
    return v.reshape(n, P).T


def _const1():
    p, q = np.arange(P)[:, None], np.arange(P)[None, :]
    maskf, maskb = (p <= q), (p >= q)
    parts = {
        "ident": p == q, "before": p < q, "maskf": np.tile(maskf, (1, 4)), "maskb": np.tile(maskb, (1, 4)),
        "slots": np.tile(q, (P, 1)), "part": p, "tok": p + P * np.arange(4)[None, :], "pad": np.zeros((P, 3)),
    }
    return np.concatenate([np.asarray(parts[k], np.float32) for k in C1], axis=1)


def _layout(i):
    f = lambda a: np.ascontiguousarray(a, dtype=np.float32)
    i = {k: np.asarray(v) for k, v in i.items()}
    lb = i["lb_logits"].reshape(2, 2, 4, P).transpose(3, 0, 1, 2).reshape(P, 16)
    b = i["b_ada"][0]
    cols = {"c": _columns(i["c"][0], KD), "cc": _columns(i["c_ctx"], KD), "gpre": _columns(i["g_pre_mix"][0], KD),
            "bsh1": _columns(b[0:D], KD), "bsc1": _columns(b[D:2 * D], KD), "lb": lb,
            "bg": _columns(i["b_gates_2"][0], 16), "nmix": _columns(i["norm_mix_gain_2"][0], KD),
            "nmlp": _columns(i["norm_mlp_gain_2"][0], KD)}
    rows = {"b_ada": b[2 * D:], "g_post_mix": i["g_post_mix"], "g_pre_ffn": i["g_pre_ffn"], "g_post_ffn": i["g_post_ffn"],
            "g_hgrn": i["g_hgrn_out"], "ln_g": i["cm_ln_g"], "ln_b": i["cm_ln_b"], "b_s": i["b_spatial"][0].T,
            "b_router": i["b_router"], "sinks": i["attn_sinks_2"], "ret_gain": i["ret_gn_gain_2"],
            "norm_final": i["norm_final_gain_2"]}
    return {
        "x": f(i["x"][0]), "ctx": f(i["ctx"][0]),
        "stream": f(np.concatenate(_mixer_stream(i) + _block2_stream(i))),
        "rows": f(np.concatenate([rows[k].reshape(-1) for k in ROWS])[None, :]),
        "cols": f(np.concatenate([cols[k] for k in PC], axis=1)),
        "const1": _const1(),
        "w_spatial": f(i["w_spatial"][0].transpose(2, 0, 1).reshape(P, 512)),
        "experts": f(np.concatenate([
            i["w_expert_gu"][0].reshape(NE, KD, P, 512).transpose(0, 2, 1, 3).reshape(NE, P, 4096),
            i["w_expert_down"][0].reshape(NE, 2, P, D).transpose(0, 2, 1, 3).reshape(NE, P, 2 * D)], axis=2)),
        "w_router": f(i["w_router"][0].reshape(KD, P, NE).transpose(1, 0, 2).reshape(P, KD * NE)),
        "const2": _const2(),
    }


def kernel(**inputs):
    import numpy as _np
    import concourse.bacc as _bacc
    from concourse import mybir as _mybir
    from concourse.bass_utils import run_bass_kernel_spmd as _run

    nc = _bacc.Bacc("TRN2", target_bir_lowering=False, num_devices=1)
    arrays, args = {}, []
    for name, a in _layout(inputs).items():
        arrays[f"in_{name}_dram"] = a
        args.append(nc.dram_tensor(f"in_{name}_dram", a.shape, _mybir.dt.from_np(a.dtype), kind="ExternalInput").ap())
    args.append(nc.dram_tensor("out_0_dram", (TOK, D), F32, kind="ExternalOutput").ap())
    program(nc, *args)
    r = _run(nc, [arrays], core_ids=[0])
    return r.results[0]["out_0_dram"].reshape(1, TOK, D)
```
